# Optimizing a Trainium2 kernel written in Bass

```python
import jax, jax.numpy as jnp
from jax import lax
import numpy as np

D_MODEL = 1024
BATCH = 1
SEQ = 256
DEPTH = 2

N_A_LAYERS = DEPTH // 2
N_B_LAYERS = DEPTH - N_A_LAYERS
HG_HEADS = 8
HG_DK = D_MODEL // HG_HEADS
HG_DV = D_MODEL // HG_HEADS
HG_CHUNK = 32
SW_Q_HEADS = 16
SW_KV_HEADS = 4
SW_HEAD_DIM = D_MODEL // SW_Q_HEADS
SW_GROUP = SW_Q_HEADS // SW_KV_HEADS
SW_WINDOW = 128
ROPE_THETA = 500000.0
ROPE_DIMS = SW_HEAD_DIM // 4
PEER_HEADS = 8
PEER_NKEYS = 128
PEER_EXPERTS = PEER_NKEYS * PEER_NKEYS
PEER_QDIM = 256
PEER_HALF = PEER_QDIM // 2
PEER_TOPK = 16
PEER_TOKEN_BLOCK = 128
DN_ALPHA = (2.0 * DEPTH) ** 0.25
DN_BETA = (8.0 * DEPTH) ** -0.25
LN_EPS = 1e-5
RMS_EPS = 1e-6

kernel_name = "yoco_hgrn2_swa_sink_peer_deepnorm"

F32 = jnp.float32

def _layernorm(x, g, b):
    xf = x.astype(F32)
    mu = jnp.mean(xf, -1, keepdims=True)
    var = jnp.mean(jnp.square(xf - mu), -1, keepdims=True)
    y = (xf - mu) * lax.rsqrt(var + LN_EPS) * g.astype(F32) + b.astype(F32)
    return y.astype(x.dtype)

def _rope_tables(positions):
    inv = ROPE_THETA ** (-jnp.arange(0, ROPE_DIMS, 2, dtype=F32) / ROPE_DIMS)
    ang = positions.astype(F32)[..., None] * inv
    return jnp.cos(ang), jnp.sin(ang)

def _partial_rope(x, cos, sin):
    half = ROPE_DIMS // 2
    xf = x.astype(F32)
    x1 = xf[..., :half]
    x2 = xf[..., half:ROPE_DIMS]
    c = cos[:, :, None, :]
    s = sin[:, :, None, :]
    out = jnp.concatenate([x1 * c - x2 * s, x2 * c + x1 * s, xf[..., ROPE_DIMS:]], axis=-1)
    return out.astype(x.dtype)

def _hgrn2(h, w_in, lb, norm_w, w_o):
    B, S, _ = h.shape
    H, DK, DV, C = HG_HEADS, HG_DK, HG_DV, HG_CHUNK
    nC = S // C
    proj = h @ w_in
    q, f, i, g = jnp.split(proj, [H * DK, 2 * H * DK, 2 * H * DK + H * DV], axis=-1)
    q = jax.nn.silu(q.astype(F32))
    lbf = lb.astype(F32)
    fg = lbf + (1.0 - lbf) * jax.nn.sigmoid(f.astype(F32))
    k = 1.0 - fg
    logf = jnp.log(fg)

    def chunk(t, d):
        return t.reshape(B, nC, C, H, d).transpose(1, 0, 3, 2, 4)

    qc, kc, lc = chunk(q, DK), chunk(k, DK), chunk(logf, DK)
    vc = chunk(i.astype(F32), DV)
    b = jnp.cumsum(lc, axis=3)
    b_last = b[:, :, :, -1:, :]
    qd = qc * jnp.exp(b)
    kd = kc * jnp.exp(-b)
    kl = kc * jnp.exp(b_last - b)
    causal = jnp.tril(jnp.ones((C, C), dtype=bool))
    att = jnp.where(causal, jnp.einsum('nbhid,nbhjd->nbhij', qd, kd), 0.0)
    o_intra = jnp.einsum('nbhij,nbhje->nbhie', att, vc)

    def step(state, xs):
        qd_n, kl_n, v_n, dec_n = xs
        o = jnp.einsum('bhid,bhde->bhie', qd_n, state)
        state = state * dec_n[..., None] + jnp.einsum('bhid,bhie->bhde', kl_n, v_n)
        return state, o

    s0 = jnp.zeros((B, H, DK, DV), F32)
    _, o_inter = lax.scan(step, s0, (qd, kl, vc, jnp.exp(b_last[:, :, :, 0, :])))
    o = (o_intra + o_inter).transpose(1, 0, 3, 2, 4).reshape(B, S, H, DV)
    o = o * lax.rsqrt(jnp.mean(jnp.square(o), -1, keepdims=True) + RMS_EPS)
    o = o.reshape(B, S, H * DV) * norm_w.astype(F32) * jax.nn.silu(g.astype(F32))
    return o.astype(h.dtype) @ w_o

def _shared_kv(h, w_kv, cos, sin):
    B, S, _ = h.shape
    kv = (h @ w_kv).reshape(B, S, 2, SW_KV_HEADS, SW_HEAD_DIM)
    k = _partial_rope(kv[:, :, 0], cos, sin)
    v = kv[:, :, 1]
    return k, v

def _swa_sink(h, k, v, w_q, sinks, w_o, cos, sin):
    B, S, _ = h.shape
    W, NKV, G, HD = SW_WINDOW, SW_KV_HEADS, SW_GROUP, SW_HEAD_DIM
    nb = S // W
    q = _partial_rope((h @ w_q).reshape(B, S, SW_Q_HEADS, HD), cos, sin)
    qb = q.reshape(B, nb, W, NKV, G, HD)

    def band(t):
        tp = jnp.pad(t, ((0, 0), (W, 0), (0, 0), (0, 0)))
        prev = tp[:, :S].reshape(B, nb, W, NKV, HD)
        cur = t.reshape(B, nb, W, NKV, HD)
        return jnp.concatenate([prev, cur], axis=2)

    kb, vb = band(k), band(v)
    logits = jnp.einsum('bnqhgd,bnkhd->bnhgqk', qb.astype(F32), kb.astype(F32)) * (HD ** -0.5)
    qi = jnp.arange(W)[:, None]
    kj = jnp.arange(2 * W)[None, :]
    diff = W + qi - kj
    in_win = (diff >= 0) & (diff < W)
    blk = jnp.arange(nb)[:, None, None]
    valid = in_win[None] & ((blk * W + kj[None] - W) >= 0)
    logits = jnp.where(valid[None, :, None, None], logits, -jnp.inf)
    sink = sinks.astype(F32).reshape(NKV, G)[None, None, :, :, None, None]
    full = jnp.concatenate([logits, jnp.broadcast_to(sink, logits.shape[:-1] + (1,))], axis=-1)
    p = jax.nn.softmax(full, axis=-1)[..., :-1]
    o = jnp.einsum('bnhgqk,bnkhd->bnqhgd', p, vb.astype(F32)).reshape(B, S, SW_Q_HEADS * HD)
    return o.astype(h.dtype) @ w_o

def _peer(h, w_pq, sub_keys, u_tab, v_tab):
    B, S, D = h.shape
    T = B * S
    K, NK, BLK = PEER_TOPK, PEER_NKEYS, PEER_TOKEN_BLOCK
    xf = h.reshape(T, D)
    q = (xf @ w_pq).astype(F32).reshape(T, PEER_HEADS, 2, PEER_HALF)
    s = jnp.einsum('thcd,hckd->thck', q, sub_keys.astype(F32))
    s1, i1 = lax.top_k(s[:, :, 0], K)
    s2, i2 = lax.top_k(s[:, :, 1], K)
    cand = (s1[..., :, None] + s2[..., None, :]).reshape(T, PEER_HEADS, K * K)
    cidx = (i1[..., :, None] * NK + i2[..., None, :]).reshape(T, PEER_HEADS, K * K)
    top_s, j = lax.top_k(cand, K)
    idx = jnp.take_along_axis(cidx, j, axis=-1)
    gate = jax.nn.softmax(top_s, axis=-1)
    nblk = T // BLK

    def block(args):
        xb, ib, gb = args
        a = jnp.einsum('td,thkd->thk', xb.astype(F32), u_tab[ib].astype(F32))
        w = gb * jax.nn.gelu(a, approximate=False)
        return jnp.einsum('thk,thkd->td', w, v_tab[ib].astype(F32))

    out = lax.map(block, (xf.reshape(nblk, BLK, D), idx.reshape(nblk, BLK, PEER_HEADS, K),
                          gate.reshape(nblk, BLK, PEER_HEADS, K)))
    return out.reshape(B, S, D).astype(h.dtype)

def setup_inputs(seed: int = 0) -> dict:
    key = jax.random.key(seed)
    ks = jax.random.split(key, 20)
    D = D_MODEL
    HGW = HG_HEADS * HG_DK
    nrm = jax.random.normal
    x = nrm(ks[0], (BATCH, SEQ, D), F32)
    positions = (jnp.arange(SEQ, dtype=jnp.int32)[None, :]
                 + jax.random.randint(ks[1], (BATCH, 1), 0, SEQ, dtype=jnp.int32))
    col_scale = jnp.concatenate([jnp.ones((2 * HGW,), F32), DN_BETA * jnp.ones((HGW,), F32),
                                 jnp.ones((HGW,), F32)]) * (D ** -0.5)
    hg_w_in = nrm(ks[2], (N_A_LAYERS, D, 4 * HGW), F32) * col_scale
    hg_lb = 0.1 * nrm(ks[3], (N_A_LAYERS + 1, HGW), F32)
    hg_norm_w = 1.0 + 0.02 * nrm(ks[4], (N_A_LAYERS, HG_HEADS * HG_DV), F32)
    hg_w_o = nrm(ks[5], (N_A_LAYERS, HG_HEADS * HG_DV, D), F32) * ((HG_HEADS * HG_DV) ** -0.5) * DN_BETA
    sw_w_q = nrm(ks[6], (N_B_LAYERS, D, SW_Q_HEADS * SW_HEAD_DIM), F32) * (D ** -0.5)
    sw_sinks = 0.5 * nrm(ks[7], (N_B_LAYERS, SW_Q_HEADS), F32)
    sw_w_o = nrm(ks[8], (N_B_LAYERS, SW_Q_HEADS * SW_HEAD_DIM, D), F32) * ((SW_Q_HEADS * SW_HEAD_DIM) ** -0.5) * DN_BETA
    kvw = SW_KV_HEADS * SW_HEAD_DIM
    w_kv = jnp.concatenate([nrm(ks[9], (D, kvw), F32) * (D ** -0.5),
                            nrm(ks[10], (D, kvw), F32) * (D ** -0.5) * DN_BETA], axis=1)
    peer_w_q = nrm(ks[11], (DEPTH, D, PEER_HEADS * PEER_QDIM), F32) * (D ** -0.5)
    peer_sub_keys = nrm(ks[12], (DEPTH, PEER_HEADS, 2, PEER_NKEYS, PEER_HALF), F32) * (PEER_HALF ** -0.5)
    peer_u = nrm(ks[13], (DEPTH, PEER_EXPERTS, D), F32) * (D ** -0.5)
    peer_v = nrm(ks[14], (DEPTH, PEER_EXPERTS, D), F32) * DN_BETA
    ln_mix_g = 1.0 + 0.02 * nrm(ks[15], (DEPTH, D), F32)
    ln_mix_b = 0.02 * nrm(ks[16], (DEPTH, D), F32)
    ln_ffn_g = 1.0 + 0.02 * nrm(ks[17], (DEPTH, D), F32)
    ln_ffn_b = 0.02 * nrm(ks[18], (DEPTH, D), F32)
    return {"x": x, "positions": positions, "hg_w_in": hg_w_in, "hg_lb": hg_lb,
            "hg_norm_w": hg_norm_w, "hg_w_o": hg_w_o, "sw_w_q": sw_w_q, "sw_sinks": sw_sinks,
            "sw_w_o": sw_w_o, "w_kv": w_kv, "peer_w_q": peer_w_q, "peer_sub_keys": peer_sub_keys,
            "peer_u": peer_u, "peer_v": peer_v, "ln_mix_g": ln_mix_g, "ln_mix_b": ln_mix_b,
            "ln_ffn_g": ln_ffn_g, "ln_ffn_b": ln_ffn_b}

def reference(x, positions, hg_w_in, hg_lb, hg_norm_w, hg_w_o, sw_w_q, sw_sinks, sw_w_o, w_kv,
              peer_w_q, peer_sub_keys, peer_u, peer_v, ln_mix_g, ln_mix_b, ln_ffn_g, ln_ffn_b):
    cos, sin = _rope_tables(positions)
    lb_all = jnp.cumsum(jax.nn.softmax(hg_lb.astype(F32), axis=0), axis=0)
    h = x
    k_sh = None
    v_sh = None
    for l in range(DEPTH):
        if l < N_A_LAYERS:
            mix = _hgrn2(h, hg_w_in[l], lb_all[l], hg_norm_w[l], hg_w_o[l])
        else:
            jb = l - N_A_LAYERS
            mix = _swa_sink(h, k_sh, v_sh, sw_w_q[jb], sw_sinks[jb], sw_w_o[jb], cos, sin)
        h = _layernorm(DN_ALPHA * h + mix, ln_mix_g[l], ln_mix_b[l])
        h = _layernorm(DN_ALPHA * h + _peer(h, peer_w_q[l], peer_sub_keys[l], peer_u[l], peer_v[l]),
                       ln_ffn_g[l], ln_ffn_b[l])
        if l == N_A_LAYERS - 1:
            k_sh, v_sh = _shared_kv(h, w_kv, cos, sin)
    return h


_drawn_inputs = setup_inputs


def setup_inputs(seed=0):
    import zlib

    import numpy as np

    out = dict(_drawn_inputs(seed))
    spreads = {}
    factors = {'hg_lb': 2.963, 'sw_sinks': 29.238}
    for name, (base, spread) in spreads.items():
        noise = np.random.default_rng([zlib.crc32(name.encode()), seed]).standard_normal(out[name].shape)
        drawn = base * np.exp(spread * noise) if base else spread * noise
        out[name] = __import__('jax').numpy.asarray(drawn.astype(out[name].dtype))
    for name, factor in factors.items():
        out[name] = (out[name] * factor).astype(out[name].dtype)
    return out
```

```python
from contextlib import ExitStack

import numpy as np

import concourse.bass as bass
from concourse import mybir

F32 = mybir.dt.float32
F32R = mybir.dt.float32r
I32 = mybir.dt.int32
U32 = mybir.dt.uint32
ALU = mybir.AluOpType
ACT = mybir.ActivationFunctionType
AX = mybir.AxisListType.X

P = 128
D = 1024
SEQ = 256
TB = SEQ // P
DC = D // P
HEADS = 8
CHUNK = 32
NCH = SEQ // CHUNK
CPB = P // CHUNK
QH = 16
KVH = 4
GRP = QH // KVH
HD = D // QH
ROPE = HD // 4
HALF = ROPE // 2
THETA = 500000.0
TOPK = 16
NKEYS = 128
NHC = 2 * HEADS
DEPTH = 2
ALPHA = (2.0 * DEPTH) ** 0.25
LN_EPS = 1e-5
RMS_EPS = 1e-6
LOWEST = -3.0e38
TWO_PI = 6.283185307179586
C1 = 6.28125
C2 = 0.0019350051879882812
C3 = TWO_PI - C1 - C2
PI_IN = 3.1415925
ROUND = 12582912.0

UNIT = 1024
RAW = 2
RING = 4
AHEAD = 2
U_F = 0
U_Q = U_F + DC
U_I = U_Q + DC
U_G = U_I + DC
U_O0 = U_G + DC
U_KEYS0 = U_O0 + DC
U_PQ0 = U_KEYS0 + 2
U_D0 = U_PQ0 + NHC
U_KV = U_D0 + 2 * NKEYS
U_WQ = U_KV + DC // 2
U_O1 = U_WQ + DC
U_KEYS1 = U_O1 + DC
U_PQ1 = U_KEYS1 + 2
U_D1 = U_PQ1 + NHC
N_UNITS = U_D1 + 2 * NKEYS
U_KEYS = (U_KEYS0, U_KEYS1)
U_PQ = (U_PQ0, U_PQ1)
U_D = (U_D0, U_D1)
TILES_LOOP = 4
TRIPS = (NKEYS - 4) // TILES_LOOP


def consumed(u):
    return u + 1 - sum(min(max(u + 1 - k, 0), 2) for k in U_KEYS)


STOP_UNITS = {1: U_PQ0 + 2, 2: U_KV + 2, 3: U_PQ1}


def head_at(j):
    return 2 * (j % 2) + j // 2


class Chain:

    def __init__(self, eng, sem):
        self.eng, self.sem, self.n, self.more = eng, sem, 0, 0

    def __call__(self, ins):
        self.n += 1
        ins.then_inc(self.sem, 1)
        self.eng.wait_ge(self.sem, self.n + self.more)

    def enter(self, i, per_trip):
        self.start, self.per_trip, self.more = self.n, per_trip, i * per_trip

    def leave(self, trips):
        assert self.n - self.start == self.per_trip, (self.n - self.start, self.per_trip)
        self.n, self.more = self.start + self.per_trip * trips, 0


def build(nc, x, xT, positions, stream, lb, norm_w, sinks, ln, out, stages=99):
    with ExitStack() as ctx:
        def sb(name, shape, dt=F32):
            return ctx.enter_context(nc.sbuf_tensor(name, shape, dt))

        def sem(name):
            return ctx.enter_context(nc.semaphore(name))

        raw = sb("raw", [P, RAW, UNIT])
        hi = sb("hi", [P, RING, UNIT], F32R)
        lo = sb("lo", [P, RING, UNIT], F32R)
        h_row = sb("h_row", [P, TB, D])
        hT_hi = sb("hT_hi", [P, DC, SEQ], F32R)
        hT_lo = sb("hT_lo", [P, DC, SEQ], F32R)
        gateT = sb("gateT", [P, SEQ])
        key1T = sb("key1T", [P, SEQ])
        key2T = sb("key2T", [P, SEQ])
        ident = sb("ident", [P, P])
        iota = sb("iota", [P, P])
        cos_t = sb("cos_t", [P, TB, HALF])
        sin_t = sb("sin_t", [P, TB, HALF])
        sink_t = sb("sink_t", [P, QH])
        stats = sb("stats", [P, TB, 2, 6])
        mean_var = sb("mean_var", [P, TB, 2])
        rstd = sb("rstd", [P, TB])
        rinv = sb("rinv", [P, TB])

        def overlaid(*groups):
            sizes = []
            keep = {}
            for g in groups:
                inner = ExitStack()
                for name, shape, dt in g:
                    keep[name] = inner.enter_context(nc.sbuf_tensor(name, shape, dt))
                sizes.append(sum(int(np.prod(s[1:])) * 4 for _, s, _ in g))
                inner.close()
            ctx.enter_context(nc.sbuf_tensor(f"room_{groups[0][0][0]}", [P, max(sizes) // 4], F32))
            return keep

        small = overlaid(
            [("onehot1", [P, 2, 4, P], F32), ("onehot2", [P, 2, 4, P], F32)],
            [("gelu_a", [P, 2, SEQ], F32), ("w_full", [P, SEQ], F32), ("w_hi", [P, 2, SEQ], F32R),
             ("w_lo", [P, 2, SEQ], F32R)],
            [("ln_par", [P, 2, D], F32)],
        )
        onehot1, onehot2, gelu_a = small["onehot1"], small["onehot2"], small["gelu_a"]
        w_full, w_hi, w_lo, ln_par = small["w_full"], small["w_hi"], small["w_lo"], small["ln_par"]

        big = overlaid(
            [("gates", [P, SEQ, NKEYS], F32)],
            [("fT", [P, HEADS, SEQ], F32), ("kT", [P, HEADS, SEQ], F32), ("decT", [P, HEADS, SEQ], F32),
             ("qT", [P, HEADS, SEQ], F32), ("klT", [P, HEADS, SEQ], F32), ("kl_row", [P, TB, D], F32),
             ("v_row", [P, TB, D], F32), ("g_row", [P, TB, D], F32), ("o_row", [P, TB, D], F32),
             ("state", [P, NCH, D], F32), ("att", [P, TB, D], F32), ("norm_t", [P, D], F32),
             ("first", [P, SEQ], F32), ("tmp", [P, SEQ], F32), ("mask_att", [P, P], I32),
             ("mask_first", [P, CHUNK], F32), ("lb_t", [P, 2, HEADS], F32), ("lb_m", [P, HEADS], F32),
             ("lb_f", [P, HEADS], F32), ("lb_1", [P, HEADS], F32), ("ssq", [P, TB, HEADS], F32),
             ("pos_i", [P, TB], I32), ("pos_f", [P, TB], F32), ("freq", [P, HALF], F32),
             ("ang", [P, TB, HALF], F32), ("rnd", [P, TB, HALF], F32), ("red", [P, TB, HALF], F32),
             ("ones_f", [P, P], F32)],
            [("keys_hi", [P, NHC, P], F32R), ("keys_lo", [P, NHC, P], F32R),
             ("q_hi", [P, 2, SEQ], F32R), ("q_lo", [P, 2, SEQ], F32R),
             ("sc", [P, 2, TB, NKEYS], F32), ("sc_cut", [P, TB, NKEYS], F32),
             ("idx_u", [P, TB, NHC, TOPK], U32),
             ("val", [P, TB, NHC, TOPK], F32), ("idx", [P, TB, NHC, TOPK], F32),
             ("cand", [P, HEADS, TOPK * TOPK], F32), ("cand_cut", [P, HEADS, TOPK * TOPK], F32),
             ("top_s", [P, TB, HEADS, TOPK], F32), ("top_j", [P, TB, HEADS, TOPK], U32),
             ("j_int", [P, 2, HEADS * TOPK], U32), ("j_f", [P, 2, HEADS * TOPK], F32),
             ("pick", [P, HEADS * TOPK, TOPK], F32), ("picked", [P, HEADS * TOPK, TOPK], F32),
             ("key_sel", [P, TB, 2, HEADS * TOPK], F32), ("gate", [P, TB, HEADS, TOPK], F32),
             ("gsum", [P, TB, HEADS], F32)],
            [("q_row", [P, TB, D], F32), ("kv_row", [P, TB, 2, KVH * HD], F32),
             ("k2_row", [P, TB, KVH, 2, HD], F32), ("aqT", [P, DC, SEQ], F32),
             ("k2T", [P, KVH, SEQ], F32), ("rt", [P, 4, QH, HALF], F32),
             ("logit", [P, 2, GRP, 2 * P], F32), ("prob", [P, 2, GRP, 2 * P], F32),
             ("probT", [P, 2, GRP, 2, P], F32), ("bias_att", [P, 2 * P], F32),
             ("rmax", [P, 2, GRP], F32), ("nmax", [P, 2, GRP], F32), ("rsum", [P, 2, GRP], F32),
             ("sexp", [P, 2, GRP], F32), ("rnorm", [P, 2, GRP], F32), ("ao_row", [P, TB, D], F32)],
        )
        B = type("Big", (), big)

        acc = ctx.enter_context(nc.psum_tensor("acc", [P, TB, D], F32))
        wk = ctx.enter_context(nc.psum_tensor("wk", [P, 4, 512], F32))

        raw_in = [sem(f"raw_in{i}") for i in range(RAW)]
        hi_ready, lo_ready, unit_done = sem("hi_ready"), sem("lo_ready"), sem("unit_done")
        dve_own, act_own, pool_own = sem("dve_own"), sem("act_own"), sem("pool_own")
        x_in, xT_in, small_in, par_in, norm_in = (
            sem("x_in"), sem("xT_in"), sem("small_in"), sem("par_in"), sem("norm_in"))
        consts = sem("consts")
        xT_hi_ready, xT_ready = sem("xT_hi_ready"), sem("xT_ready")
        lb_shift, lb_exp = sem("lb_shift"), sem("lb_exp")
        angles, tables = sem("angles"), sem("tables")
        proj_read, row_read = sem("proj_read"), sem("row_read")
        decays = sem("decays")
        kl_turned, kl_read = sem("kl_turned"), sem("kl_read")
        att_raw, att_ready = sem("att_raw"), sem("att_ready")
        delta, state_ready = sem("delta"), sem("state_ready")
        o_sum, o_copied, o_sq, o_rms = sem("o_sum"), sem("o_copied"), sem("o_sq"), sem("o_rms")
        row_ready, turned, turn_hi, turn_lo = (
            sem("row_ready"), sem("turned"), sem("turn_hi"), sem("turn_lo"))
        var_ready, rstd_ready = sem("var_ready"), sem("rstd_ready")
        q_hi_ready, q_lo_ready, sc_ready, sc_copied, sc_done = (
            sem("q_hi_ready"), sem("q_lo_ready"), sem("sc_ready"), sem("sc_copied"), sem("sc_done"))
        gate_in, gate_exp, choice_ready, choice_turned, choice_read = (
            sem("gate_in"), sem("gate_exp"), sem("choice_ready"), sem("choice_turned"), sem("choice_read"))
        onehots, gate_mm, gate_read = sem("onehots"), sem("gate_mm"), sem("gate_read")
        act_ready, w_ready, tile_done = sem("act_ready"), sem("w_ready"), sem("tile_done")
        aq_read, akv_read, roped, a_turned, a_turn_read = (
            sem("aq_read"), sem("akv_read"), sem("roped"), sem("a_turned"), sem("a_turn_read"))
        logits, shifted, probs, p_turned, p_read, a_out, a_norm = (
            sem("logits"), sem("shifted"), sem("probs"), sem("p_turned"), sem("p_read"), sem("a_out"),
            sem("a_norm"))
        stored = sem("stored")

        block = ctx.enter_context(nc.Block())

        def split_hi(act, c, i=0):
            if type(i) is int and c + RING * i >= N_UNITS:
                return
            act.wait_ge(raw_in[c % RAW], 16 * (c // RAW + 1) + 32 * i)
            if type(i) is not int:
                act.wait_ge(unit_done, consumed(c) + RING * (i - 1))
            elif c >= RING:
                act.wait_ge(unit_done, consumed(c - RING) + RING * i)
            dst = hi[:, c % RING, :]
            for k in U_KEYS:
                if c in (k, k + 1):
                    dst = B.keys_hi[:, (c - k) * 8:(c - k) * 8 + 8, :]
                    src = raw[:, c % RAW, :].rearrange("p (a b) -> p a b", a=8)
                    act.activation(dst, src, ACT.Copy).then_inc(hi_ready, 1)
                    return
            act.activation(dst, raw[:, c % RAW, :], ACT.Copy).then_inc(hi_ready, 1)

        def split_lo(dve, c, i=0):
            if type(i) is int and c + RING * i >= N_UNITS:
                return
            dve.wait_ge(hi_ready, c + 1 + RING * i)
            for k in U_KEYS:
                if c in (k, k + 1):
                    part = slice((c - k) * 8, (c - k) * 8 + 8)
                    src = raw[:, c % RAW, :].rearrange("p (a b) -> p a b", a=8)
                    dve.tensor_tensor(B.keys_lo[:, part, :], src, B.keys_hi[:, part, :].bitcast(F32),
                                      ALU.subtract).then_inc(lo_ready, 1)
                    return
            dve.tensor_tensor(lo[:, c % RING, :], raw[:, c % RAW, :], hi[:, c % RING, :].bitcast(F32),
                              ALU.subtract).then_inc(lo_ready, 1)

        @block.sync
        def _(sp):
            n_units = N_UNITS if stages > 90 else STOP_UNITS.get(stages, N_UNITS)
            for c in range(RING):
                if c >= RAW:
                    sp.wait_ge(lo_ready, c - RAW + 1)
                sp.dma_start(raw[:, c % RAW, :], stream[c]).then_inc(raw_in[c % RAW], 16)
            with sp.Fori(1, n_units // RING) as i:
                for c in range(RING):
                    sp.wait_ge(lo_ready, c - RAW + 1 + RING * i)
                    sp.dma_start(raw[:, c % RAW, :], stream[bass.ds(c + RING * i, 1)].rearrange(
                        "o p f -> (o p) f")).then_inc(raw_in[c % RAW], 16)
            sp.wait_ge(row_ready, {1: 4, 2: 6, 3: 8}.get(stages, 10))
            sp.dma_start(out, h_row[:]).then_inc(stored, 16)
            sp.wait_ge(stored, 16)

        @block.gpsimd
        def _(pool):
            own = Chain(pool, pool_own)
            pool.dma_start(h_row[:], x).then_inc(x_in, 16)
            pool.dma_start(B.lb_t[:], lb).then_inc(small_in, 16)
            pool.dma_start(B.pos_i[:], positions).then_inc(small_in, 16)
            pool.dma_start(sink_t[:], sinks.partition_broadcast(P)).then_inc(small_in, 16)
            pool.dma_start(B.norm_t[:], norm_w.partition_broadcast(P)).then_inc(norm_in, 16)
            own(pool.memset(ident[:], 0.0))
            own(pool.affine_select(out=ident[:], in_=ident[:], compare_op=ALU.not_equal, fill=1.0, base=0,
                                   pattern=[[-1, P]], channel_multiplier=1))
            own(pool.iota(iota[:], pattern=[[1, P]], base=0, channel_multiplier=0,
                          allow_small_or_imprecise_dtypes=True))
            own(pool.memset(B.ones_f[:], 1.0))
            m3 = B.ones_f[:].rearrange("p (c i) -> p c i", c=CPB)
            own(pool.affine_select(out=m3, in_=m3, compare_op=ALU.is_ge, fill=0.0, base=0,
                                   pattern=[[CHUNK, CPB], [1, CHUNK]], channel_multiplier=-1))
            own(pool.affine_select(out=m3, in_=m3, compare_op=ALU.is_ge, fill=0.0, base=0,
                                   pattern=[[-CHUNK, CPB], [0, CHUNK]], channel_multiplier=1))
            own(pool.tensor_copy(B.mask_att[:], B.ones_f[:]))
            own(pool.memset(B.mask_first[:], 1.0))
            own(pool.affine_select(out=B.mask_first[:], in_=B.mask_first[:], compare_op=ALU.is_equal,
                                   fill=0.0, base=0, pattern=[[1, CHUNK]], channel_multiplier=0))
            for k in range(HALF):
                own(pool.memset(B.freq[:, k:k + 1], float(np.float32(THETA) ** np.float32(-2 * k / ROPE))))
            pool.memset(B.att[:], 0.0).then_inc(consts, 1)
            for k in range(min(2 * DEPTH, stages)):
                if k % 2 == 0:
                    pool.wait_ge(unit_done, consumed((U_O0, U_O1)[k // 2]))
                else:
                    pool.wait_ge(unit_done, consumed(U_D[k // 2] + 2 * NKEYS - 1))
                for a in range(2):
                    pool.dma_start(ln_par[:, a, :], ln[k, a:a + 1, :].rearrange("a d -> (a d)")
                                   .partition_broadcast(P)).then_inc(par_in, 16)
                if k == 1 and stages > 2:
                    own(pool.memset(B.bias_att[:], 0.0))
                    own(pool.affine_select(out=B.bias_att[:], in_=B.bias_att[:], compare_op=ALU.is_ge,
                                           fill=LOWEST, base=P, pattern=[[-1, 2 * P]],
                                           channel_multiplier=1))
                    pool.affine_select(out=B.bias_att[:], in_=B.bias_att[:], compare_op=ALU.is_ge,
                                       fill=LOWEST, base=-1, pattern=[[1, 2 * P]],
                                       channel_multiplier=-1).then_inc(consts, 1)

        @block.tensor
        def _(pe):
            def col_unit(c, i, bank):
                pe.wait_ge(lo_ready, c + 1 + RING * i)
                s = c % RING
                for dc in range(DC):
                    wh, wl = hi[:, s, dc * P:(dc + 1) * P], lo[:, s, dc * P:(dc + 1) * P]
                    o = wk[:, bank, 0:SEQ]
                    pe.matmul(o, wh, hT_hi[:, dc, :], start=(dc == 0), stop=False)
                    pe.matmul(o, wh, hT_lo[:, dc, :], start=False, stop=False)
                    last = pe.matmul(o, wl, hT_hi[:, dc, :], start=False, stop=(dc == DC - 1))
                last.then_inc(unit_done, 1)

            def row_units(u, dsts):
                for k in range(4):
                    pe.wait_ge(lo_ready, u + k + 1)
                    s = (u + k) % RING
                    for j in range(2):
                        dc = 2 * k + j
                        wh, wl = hi[:, s, j * 512:(j + 1) * 512], lo[:, s, j * 512:(j + 1) * 512]
                        for tb in range(TB):
                            hh, hl = hT_hi[:, dc, tb * P:(tb + 1) * P], hT_lo[:, dc, tb * P:(tb + 1) * P]
                            pe.matmul(dsts[tb], hh, wh, start=(dc == 0), stop=False)
                            pe.matmul(dsts[tb], hh, wl, start=False, stop=False)
                            last = pe.matmul(dsts[tb], hl, wh, start=False, stop=(dc == DC - 1))
                    last.then_inc(unit_done, 1)

            def turn(n, src, rows=None):
                for g in range(4):
                    tb, half = divmod(g, 2)
                    if half == 0 and rows is not None:
                        pe.wait_ge(row_ready, rows + tb + 1)
                    for b in range(4):
                        dc = 4 * half + b
                        last = pe.transpose(wk[:, g, b * P:(b + 1) * P], src[:, tb, dc * P:(dc + 1) * P],
                                            ident[:])
                    last.then_inc(turned, 1)
                pe.wait_ge(turn_lo, 4 * n + 4)

            def hgrn():
                pe.wait_ge(consts, 1)
                pe.wait_ge(xT_ready, 1)
                for c in range(4):
                    col_unit(U_F + c, 0, c)
                with pe.Fori(1, 4) as i:
                    for c in range(4):
                        pe.wait_ge(proj_read, c - 3 + 4 * i)
                        col_unit(U_F + c, i, c)
                for g in range(4):
                    if g == 0:
                        pe.wait_ge(proj_read, 2 * DC)
                    if g >= 2:
                        pe.wait_ge(row_read, g - 1)
                    row_units(U_I + 4 * g, [wk[:, 2 * (g % 2) + tb, :] for tb in range(TB)])
                pe.wait_ge(decays, HEADS)
                pe.wait_ge(row_read, 4)
                for g in range(4):
                    tb, half = divmod(g, 2)
                    for b in range(4):
                        last = pe.transpose(wk[:, g, b * P:(b + 1) * P],
                                            B.klT[:, 4 * half + b, tb * P:(tb + 1) * P], ident[:])
                    last.then_inc(kl_turned, 1)
                for g in range(4):
                    tb, half = divmod(g, 2)
                    for b in range(4):
                        h, t = 4 * half + b, slice(tb * P, (tb + 1) * P)
                        last = pe.matmul(acc[:, tb, h * P:(h + 1) * P], B.kT[:, h, t], B.qT[:, h, t],
                                         start=True, stop=True)
                    last.then_inc(att_raw, 1)
                pe.wait_ge(kl_read, 4)
                for c in range(NCH - 1):
                    tb, r = c // CPB, slice(c % CPB * CHUNK, (c % CPB + 1) * CHUNK)
                    if c >= 2:
                        pe.wait_ge(state_ready, c - 1)
                    for h in range(HEADS):
                        f = slice(h * P, (h + 1) * P)
                        last = pe.matmul(wk[:, 2 * (c % 2) + h // 4, h % 4 * P:(h % 4 + 1) * P],
                                         B.kl_row[r, tb, f], B.v_row[r, tb, f], start=True, stop=True)
                    last.then_inc(delta, 1)
                pe.wait_ge(att_ready, 4)
                for tb in range(TB):
                    pe.wait_ge(state_ready, min(CPB * (tb + 1), NCH) - 1)
                    for h in range(HEADS):
                        f = slice(h * P, (h + 1) * P)
                        last = pe.matmul(acc[:, tb, f], B.att[:, tb, f], B.v_row[:, tb, f], start=True,
                                         stop=False, skip_group_check=True)
                        for c in range(CPB):
                            n = CPB * tb + c
                            if n == 0:
                                continue
                            last = pe.matmul(acc[c * CHUNK:(c + 1) * CHUNK, tb, f],
                                             B.qT[:, h, n * CHUNK:(n + 1) * CHUNK], B.state[:, n, f],
                                             start=False, stop=True, skip_group_check=True)
                    last.then_inc(o_sum, 1)
                turn(0, B.o_row, 0)
                for g in range(2):
                    row_units(U_O0 + 4 * g, [acc[:, tb, g * 512:(g + 1) * 512] for tb in range(TB)])
                turn(1, h_row, 2)

            def scores(l, c, i):
                n = NHC * l + c
                pe.wait_ge(q_lo_ready, n + 1 + 4 * i)
                if n >= 2 or type(i) is not int:
                    pe.wait_ge(sc_copied, n - 1 + 4 * i)
                for tb in range(TB):
                    t = slice(tb * P, (tb + 1) * P)
                    qh, ql = B.q_hi[:, c % 2, t], B.q_lo[:, c % 2, t]
                    at = c + 4 * i
                    kh = B.keys_hi[:, bass.ds(at, 1), :].rearrange("p o k -> p (o k)")
                    kl = B.keys_lo[:, bass.ds(at, 1), :].rearrange("p o k -> p (o k)")
                    o = wk[:, 2 + c % 2, t]
                    pe.matmul(o, qh, kh, start=True, stop=False)
                    pe.matmul(o, qh, kl, start=False, stop=False)
                    last = pe.matmul(o, ql, kh, start=False, stop=True)
                last.then_inc(sc_ready, 1)

            def choice_step(l, c, i):
                n = NHC * l + c
                if n >= 2 or type(i) is not int:
                    pe.wait_ge(q_lo_ready, n - 1 + 4 * i)
                col_unit(U_PQ[l] + c, i, c % 2)
                if c >= 1:
                    scores(l, c - 1, i)

            def peer(l):
                for c in range(4):
                    choice_step(l, c, 0)
                with pe.Fori(1, 4) as i:
                    for c in range(4):
                        if c == 0:
                            pe.wait_ge(q_lo_ready, NHC * l - 1 + 4 * i)
                            col_unit(U_PQ[l], i, 0)
                            scores(l, 3, i - 1)
                        else:
                            choice_step(l, c, i)
                scores(l, 3, 3)
                for tb in range(TB):
                    pe.wait_ge(choice_ready, TB * l + tb + 1)
                    if tb == 0:
                        pe.wait_ge(sc_copied, NHC * (l + 1))
                    for a, src in enumerate((B.gate[:, tb].rearrange("p h k -> p (h k)"),
                                             B.key_sel[:, tb, 0, :], B.key_sel[:, tb, 1, :])):
                        last = pe.transpose(wk[:, tb, a * P:(a + 1) * P], src, ident[:])
                    last.then_inc(choice_turned, 1)
                pe.wait_ge(choice_read, TB * (l + 1))

                def gate_step(c, i):
                    n = 64 * l + c
                    pe.wait_ge(onehots, n + 1 + 4 * i)
                    if n >= 4 or type(i) is not int:
                        pe.wait_ge(gate_read, n - 3 + 4 * i)
                    for b in range(4):
                        last = pe.matmul(wk[:, c, b * P:(b + 1) * P], onehot2[:, c % 2, b, :],
                                         onehot1[:, c % 2, b, :], start=True, stop=True)
                    last.then_inc(gate_mm, 1)

                for c in range(4):
                    gate_step(c, 0)
                with pe.Fori(1, 16) as i:
                    for c in range(4):
                        gate_step(c, i)

                def up(c, i, n):
                    if NKEYS * l + n >= 4:
                        pe.wait_ge(act_ready, NKEYS * l + n - 3)
                    col_unit(c, i, n % 4)

                def down(c, i, n, slot, first, final):
                    pe.wait_ge(lo_ready, c + 1 + RING * i)
                    pe.wait_ge(w_ready, NKEYS * l + n + 1)
                    s = c % RING
                    for tb in range(TB):
                        wh, wl = w_hi[:, slot, tb * P:(tb + 1) * P], w_lo[:, slot, tb * P:(tb + 1) * P]
                        for half in range(2):
                            f = slice(half * 512, (half + 1) * 512)
                            pe.matmul(acc[:, tb, f], wh, hi[:, s, f], start=first, stop=False)
                            pe.matmul(acc[:, tb, f], wh, lo[:, s, f], start=False, stop=False)
                            last = pe.matmul(acc[:, tb, f], wl, hi[:, s, f], start=False, stop=final)
                    last.then_inc(unit_done, 1)

                u = U_D[l]
                pe.wait_ge(gate_read, 64 * (l + 1))
                up(u, 0, 0)
                up(u + 1, 0, 1)
                down(u + 2, 0, 0, 0, True, False)
                with pe.Fori(0, TRIPS) as i:
                    for b in range(TILES_LOOP):
                        n = 1 + b
                        c = u + 3 + 2 * b
                        pe.wait_ge(act_ready, max(NKEYS * l + n - 2, 1) + 4 * i)
                        col_unit(c, 2 * i, (n + 1) % 4)
                        down(c + 1, 2 * i, n + 4 * i, n % 2, False, False)
                n = NKEYS - 3
                c = u + 2 * n + 1
                for m in (n, n + 1):
                    up(c, 0, m + 1)
                    down(c + 1, 0, m, m % 2, False, False)
                    c += 2
                down(c, 0, NKEYS - 1, (NKEYS - 1) % 2, False, True)

            def attention():
                row_units(U_KV, [wk[:, tb, :] for tb in range(TB)])
                for g in range(2):
                    if g == 1:
                        pe.wait_ge(akv_read, 1)
                    row_units(U_WQ + 4 * g, [wk[:, 2 - 2 * g + tb, :] for tb in range(TB)])
                pe.wait_ge(aq_read, 2)
                for tb in range(TB):
                    pe.wait_ge(roped, tb + 1)
                    for half in range(3):
                        g = 3 * tb + half
                        if g >= 4:
                            pe.wait_ge(a_turn_read, g - 3)
                        for b in range(4):
                            src = (B.q_row[:, tb, (4 * half + b) * P:(4 * half + b + 1) * P] if half < 2
                                   else B.k2_row[:, tb, b].rearrange("p r d -> p (r d)"))
                            last = pe.transpose(wk[:, g % 4, b * P:(b + 1) * P], src, ident[:])
                        last.then_inc(a_turned, 1)
                pe.wait_ge(a_turn_read, 6)

                def logit_step(n):
                    tb, kv = divmod(n, KVH)
                    if n >= 1:
                        pe.wait_ge(shifted, n)
                    for j in range(GRP):
                        h = GRP * kv + head_at(j)
                        r = slice(h % 2 * HD, (h % 2 + 1) * HD)
                        lhs = B.aqT[r, h // 2, tb * P:(tb + 1) * P]
                        keys = slice(0, 2 * P) if tb else slice(0, P)
                        o = acc[:, 0, j * 256 + (0 if tb else P):(j + 1) * 256]
                        last = pe.matmul(o, lhs, B.k2T[r, kv, keys], start=True, stop=True)
                    last.then_inc(logits, 1)

                def value_step(n):
                    tb, kv = divmod(n, KVH)
                    pe.wait_ge(probs, n + 1)
                    parts = (0, 1) if tb else (1,)
                    if n >= 2:
                        pe.wait_ge(p_read, n - 1)
                    for j in range(GRP):
                        for part in parts:
                            o = wk[:, 2 * (n % 2) + j // 2, (j % 2 * 2 + part) * P:(j % 2 * 2 + part + 1) * P]
                            last = pe.transpose(o, B.prob[:, n % 2, j, part * P:(part + 1) * P], ident[:])
                    last.then_inc(p_turned, 1)

                def out_step(n):
                    tb, kv = divmod(n, KVH)
                    parts = (0, 1) if tb else (1,)
                    pe.wait_ge(p_read, n + 1)
                    if n >= 2:
                        pe.wait_ge(a_norm, n - 1)
                    for j in range(GRP):
                        g = head_at(j)
                        for part in parts:
                            last = pe.matmul(acc[:, 1, (n % 2) * 512 + g * HD:(n % 2) * 512 + (g + 1) * HD],
                                             B.probT[:, n % 2, j, part, :],
                                             B.kv_row[:, tb - 1 + part, 1, kv * HD:(kv + 1) * HD],
                                             start=(part == parts[0]), stop=(part == 1))
                    last.then_inc(a_out, 1)

                for n in range(TB * KVH + 1):
                    if n < TB * KVH:
                        logit_step(n)
                    if n >= 1:
                        value_step(n - 1)
                        out_step(n - 1)
                pe.wait_ge(a_norm, TB * KVH)
                turn(3, B.ao_row)
                for g in range(2):
                    row_units(U_O1 + 4 * g, [acc[:, tb, g * 512:(g + 1) * 512] for tb in range(TB)])
                turn(4, h_row, 6)

            hgrn()
            if stages > 1:
                peer(0)
            if stages > 2:
                turn(2, h_row, 4)
                attention()
            if stages > 3:
                peer(1)

        @block.scalar
        def _(act):
            own = Chain(act, act_own)

            def turn_step(n):
                for g in range(4):
                    tb, half = divmod(g, 2)
                    act.wait_ge(turned, 4 * n + g + 1)
                    act.activation(hT_hi[:, 4 * half:4 * half + 4, tb * P:(tb + 1) * P],
                                   wk[:, g, :].rearrange("p (b t) -> p b t", b=4),
                                   ACT.Copy).then_inc(turn_hi, 1)

            def norm_step(k):
                act.wait_ge(var_ready, k + 1)
                act.activation(rstd[:], rinv[:], ACT.Sqrt).then_inc(rstd_ready, 1)

            def hgrn():
                xt_raw = B.o_row[:].rearrange("p a b -> p (a b)")
                act.dma_start(xt_raw, xT).then_inc(xT_in, 16)
                split_hi(act, 0)
                act.wait_ge(xT_in, 16)
                act.activation(hT_hi[:].rearrange("p c t -> p (c t)"), xt_raw, ACT.Copy).then_inc(
                    xT_hi_ready, 1)
                split_hi(act, 1)
                act.wait_ge(lb_shift, 1)
                act.activation(B.lb_t[:], B.lb_t[:], ACT.Exp).then_inc(lb_exp, 1)
                act.wait_ge(angles, 1)
                act.activation(sin_t[:], B.red[:], ACT.Sin).then_inc(tables, 1)
                act.wait_ge(angles, 2)
                act.activation(cos_t[:], B.ang[:], ACT.Sin).then_inc(tables, 1)
                for c in range(DC):
                    split_hi(act, U_F + c + AHEAD)
                    act.wait_ge(unit_done, U_F + c + 1)
                    act.activation(B.fT[:, c, :], wk[:, c % 4, 0:SEQ], ACT.Sigmoid).then_inc(proj_read, 1)
                with act.Fori(0, 2) as i:
                    for c in range(4):
                        split_hi(act, U_Q + c + AHEAD, i)
                        act.wait_ge(unit_done, U_Q + c + 1 + RING * i)
                        act.activation(B.qT[:, bass.ds(4 * i + c, 1), :].rearrange("p o t -> p (o t)"),
                                       wk[:, c, 0:SEQ], ACT.Silu).then_inc(proj_read, 1)
                for g in range(4):
                    for k in range(4):
                        split_hi(act, U_I + 4 * g + k + AHEAD)
                    act.wait_ge(unit_done, U_I + 4 * g + 4)
                    dst, func = (B.v_row, ACT.Copy) if g < 2 else (B.g_row, ACT.Silu)
                    act.activation(dst[:, :, g % 2 * 512:(g % 2 + 1) * 512],
                                   wk[:, 2 * (g % 2):2 * (g % 2) + 2, :], func).then_inc(row_read, 1)
                for g in range(4):
                    tb, half = divmod(g, 2)
                    act.wait_ge(kl_turned, g + 1)
                    act.activation(B.kl_row[:, tb, half * 512:(half + 1) * 512], wk[:, g, :],
                                   ACT.Copy).then_inc(kl_read, 1)
                for tb in range(TB):
                    act.wait_ge(o_sum, tb + 1)
                    act.activation(B.o_row[:, tb, :], acc[:, tb, :], ACT.Copy).then_inc(o_copied, 1)
                    act.wait_ge(o_sq, tb + 1)
                    act.activation(B.ssq[:, tb, :], B.ssq[:, tb, :], ACT.Sqrt).then_inc(o_rms, 1)
                turn_step(0)
                for u in range(U_O0, U_O0 + DC):
                    split_hi(act, u + AHEAD)
                norm_step(0)
                turn_step(1)

            def peer(l):
                for c in (U_KEYS[l] + 2, U_KEYS[l] + 3):
                    split_hi(act, c)

                def q_step(c, i):
                    n = NHC * l + c
                    act.wait_ge(unit_done, consumed(U_PQ[l] + c) + RING * i)
                    if n >= 2 or type(i) is not int:
                        act.wait_ge(sc_ready, n - 1 + 4 * i)
                    act.activation(B.q_hi[:, c % 2, :], wk[:, c % 2, 0:SEQ], ACT.Copy).then_inc(
                        q_hi_ready, 1)

                def s_step(c, i):
                    n = NHC * l + c
                    act.wait_ge(sc_ready, n + 1 + 4 * i)
                    if n >= 2 or type(i) is not int:
                        act.wait_ge(sc_done, n - 1 + 4 * i)
                    act.activation(B.sc[:, c % 2].rearrange("p b k -> p (b k)"),
                                   wk[:, 2 + c % 2, 0:SEQ], ACT.Copy).then_inc(sc_copied, 1)

                for c in range(4):
                    split_hi(act, U_PQ[l] + c + AHEAD)
                    q_step(c, 0)
                    if c:
                        s_step(c - 1, 0)
                with act.Fori(1, 4) as i:
                    for c in range(4):
                        split_hi(act, U_PQ[l] + c + AHEAD, i)
                        if c == 0:
                            act.wait_ge(unit_done, consumed(U_PQ[l]) + RING * i)
                            act.wait_ge(sc_ready, NHC * l - 1 + 4 * i)
                            act.activation(B.q_hi[:, 0, :], wk[:, 0, 0:SEQ], ACT.Copy).then_inc(
                                q_hi_ready, 1)
                            s_step(3, i - 1)
                        else:
                            q_step(c, i)
                            s_step(c - 1, i)
                s_step(3, 3)
                for tb in range(TB):
                    act.wait_ge(gate_in, TB * l + tb + 1)
                    act.activation(B.gate[:, tb], B.gate[:, tb], ACT.Exp).then_inc(gate_exp, 1)
                for tb in range(TB):
                    act.wait_ge(choice_turned, TB * l + tb + 1)
                    t = slice(tb * P, (tb + 1) * P)
                    act.activation(gateT[:, t], wk[:, tb, 0:P], ACT.Copy)
                    act.activation(key1T[:, t], wk[:, tb, P:2 * P], ACT.Copy)
                    act.activation(key2T[:, t], wk[:, tb, 2 * P:3 * P], ACT.Copy).then_inc(choice_read, 1)
                with act.Fori(0, 16) as i:
                    for c in range(4):
                        act.wait_ge(gate_mm, 64 * l + c + 1 + 4 * i)
                        act.activation(B.gates[:, bass.ds(16 * i + 4 * c, 4), :].rearrange(
                            "p t k -> p (t k)"), wk[:, c, :], ACT.Copy).then_inc(gate_read, 1)

                def gelu(n, i, c, ci):
                    act.wait_ge(unit_done, consumed(c) + RING * ci)
                    if NKEYS * l + n >= 2:
                        act.wait_ge(w_ready, NKEYS * l + n - 1 + 4 * i)
                    act.activation(gelu_a[:, n % 2, :], wk[:, n % 4, 0:SEQ], ACT.Gelu).then_inc(
                        act_ready, 1)

                u = U_D[l]
                split_hi(act, u + 2)
                gelu(0, 0, u, 0)
                split_hi(act, u + 3)
                split_hi(act, u + 4)
                with act.Fori(0, TRIPS) as i:
                    for b in range(TILES_LOOP):
                        n, c = 1 + b, u + 3 + 2 * b
                        if b == 0:
                            act.wait_ge(unit_done, consumed(u + 1) + 8 * i)
                            act.wait_ge(w_ready, NKEYS * l + 1 + 4 * i)
                            act.activation(gelu_a[:, 1, :], wk[:, 1, 0:SEQ], ACT.Gelu).then_inc(
                                act_ready, 1)
                        else:
                            gelu(n, i, c - 2, 2 * i)
                        split_hi(act, c + 2, 2 * i)
                        split_hi(act, c + 3, 2 * i)
                c = u + 2 * (NKEYS - 3) + 1
                for n in range(NKEYS - 3, NKEYS):
                    gelu(n, 0, c - 2, 0)
                    split_hi(act, c + 2)
                    if n < NKEYS - 1:
                        split_hi(act, c + 3)
                    c += 2
                norm_step(2 * l + 1)

            def attention():
                for u in range(U_KV, U_KV + 4):
                    split_hi(act, u + AHEAD)
                act.wait_ge(unit_done, consumed(U_KV + 3))
                act.activation(B.kv_row[:].rearrange("p b s f -> p b (s f)"), wk[:, 0:2, :],
                               ACT.Copy).then_inc(akv_read, 1)
                for g in range(2):
                    for k in range(4):
                        split_hi(act, U_WQ + 4 * g + k + AHEAD)
                    act.wait_ge(unit_done, consumed(U_WQ + 4 * g + 3))
                    act.activation(B.q_row[:, :, g * 512:(g + 1) * 512],
                                   wk[:, 2 - 2 * g:4 - 2 * g, :], ACT.Copy).then_inc(aq_read, 1)
                for tb in range(TB):
                    for half in range(3):
                        g = 3 * tb + half
                        act.wait_ge(a_turned, g + 1)
                        dst = (B.aqT[:, 4 * half:4 * half + 4, tb * P:(tb + 1) * P] if half < 2
                               else B.k2T[:, :, tb * P:(tb + 1) * P])
                        act.activation(dst, wk[:, g % 4, :].rearrange("p (b t) -> p b t", b=4),
                                       ACT.Copy).then_inc(a_turn_read, 1)
                for n in range(TB * KVH):
                    tb, kv = divmod(n, KVH)
                    first = 0 if tb else P
                    act.wait_ge(shifted, n + 1)
                    if n >= 2:
                        act.wait_ge(p_turned, n - 1)
                    for j in range(GRP):
                        act.activation(B.prob[:, n % 2, j, first:], B.logit[:, n % 2, j, first:], ACT.Exp,
                                       bias=B.nmax[:, n % 2, j:j + 1],
                                       accum_out=B.rsum[:, n % 2, j:j + 1])
                    last = act.activation(B.sexp[:, n % 2, :], B.sexp[:, n % 2, :], ACT.Exp)
                    last.then_inc(probs, 1)
                turn_step(3)
                for u in range(U_O1, U_O1 + DC):
                    split_hi(act, u + AHEAD)
                norm_step(2)
                turn_step(4)

            hgrn()
            if stages > 1:
                peer(0)
            if stages > 2:
                turn_step(2)
                attention()
            if stages > 3:
                peer(1)

        @block.vector
        def _(dve):
            own = Chain(dve, dve_own)

            def turn_step(n):
                for g in range(4):
                    tb, half = divmod(g, 2)
                    t = slice(tb * P, (tb + 1) * P)
                    dve.wait_ge(turn_hi, 4 * n + g + 1)
                    dve.tensor_tensor(hT_lo[:, 4 * half:4 * half + 4, t],
                                      wk[:, g, :].rearrange("p (b t) -> p b t", b=4),
                                      hT_hi[:, 4 * half:4 * half + 4, t].bitcast(F32),
                                      ALU.subtract).then_inc(turn_lo, 1)

            def layer_norm(k, u_last):
                dve.wait_ge(unit_done, consumed(u_last))
                for tb in range(TB):
                    own(dve.scalar_tensor_tensor(h_row[:, tb, :], h_row[:, tb, :], ALPHA, acc[:, tb, :],
                                                 ALU.mult, ALU.add))
                    dve.bn_stats(stats[:, tb, 0, :], h_row[:, tb, 0:512])
                    own(dve.bn_stats(stats[:, tb, 1, :], h_row[:, tb, 512:1024]))
                    own(dve.bn_aggr(mean_var[:, tb, :], stats[:, tb].rearrange("p a b -> p (a b)")))
                own(dve.tensor_scalar(rinv[:], mean_var[:, :, 1], LN_EPS, None, ALU.add))
                dve.reciprocal(rinv[:], rinv[:]).then_inc(var_ready, 1)
                dve.wait_ge(rstd_ready, k + 1)
                for tb in range(TB):
                    own(dve.tensor_scalar(h_row[:, tb, :], h_row[:, tb, :], mean_var[:, tb, 0:1],
                                          rstd[:, tb:tb + 1], ALU.subtract, ALU.mult))
                    if tb == 0:
                        dve.wait_ge(par_in, 32 * (k + 1))
                    own(dve.tensor_tensor(h_row[:, tb, :], h_row[:, tb, :], ln_par[:, 0, :], ALU.mult))
                    dve.tensor_tensor(h_row[:, tb, :], h_row[:, tb, :], ln_par[:, 1, :],
                                      ALU.add).then_inc(row_ready, 1)

            def hgrn():
                dve.wait_ge(consts, 1)
                split_lo(dve, 0)
                xt_raw = B.o_row[:].rearrange("p a b -> p (a b)")
                dve.wait_ge(xT_hi_ready, 1)
                dve.tensor_tensor(hT_lo[:].rearrange("p c t -> p (c t)"), xt_raw,
                                  hT_hi[:].rearrange("p c t -> p (c t)").bitcast(F32),
                                  ALU.subtract).then_inc(xT_ready, 1)
                split_lo(dve, 1)
                dve.wait_ge(small_in, 48)
                own(dve.tensor_tensor(B.lb_m[:], B.lb_t[:, 0, :], B.lb_t[:, 1, :], ALU.max))
                dve.tensor_tensor(B.lb_t[:], B.lb_t[:], B.lb_m[:].unsqueeze(1).broadcast_to([P, 2, HEADS]),
                                  ALU.subtract).then_inc(lb_shift, 1)
                own(dve.tensor_copy(B.pos_f[:], B.pos_i[:]))
                for tb in range(TB):
                    last = dve.tensor_scalar(B.ang[:, tb, :], B.freq[:], B.pos_f[:, tb:tb + 1], None,
                                             ALU.mult)
                own(last)
                for n, (quarter, dst) in enumerate(((0.0, B.red), (0.25, B.ang))):
                    own(dve.tensor_scalar(B.rnd[:], B.ang[:], 1.0 / TWO_PI, quarter, ALU.mult, ALU.add))
                    own(dve.tensor_scalar(B.rnd[:], B.rnd[:], ROUND, None, ALU.add))
                    own(dve.tensor_scalar(B.rnd[:], B.rnd[:], ROUND, None, ALU.subtract))
                    own(dve.scalar_tensor_tensor(dst[:], B.rnd[:], -C1, B.ang[:], ALU.mult, ALU.add))
                    own(dve.scalar_tensor_tensor(dst[:], B.rnd[:], -C2, dst[:], ALU.mult, ALU.add))
                    own(dve.scalar_tensor_tensor(dst[:], B.rnd[:], -C3, dst[:], ALU.mult, ALU.add))
                    own(dve.tensor_scalar(dst[:], dst[:], quarter * TWO_PI, PI_IN, ALU.add, ALU.min))
                    dve.tensor_scalar(dst[:], dst[:], -PI_IN, None, ALU.max).then_inc(angles, 1)
                dve.wait_ge(lb_exp, 1)
                own(dve.tensor_tensor(B.lb_m[:], B.lb_t[:, 0, :], B.lb_t[:, 1, :], ALU.add))
                own(dve.reciprocal(B.lb_m[:], B.lb_m[:]))
                dve.tensor_tensor(B.lb_1[:], B.lb_t[:, 1, :], B.lb_m[:], ALU.mult)
                own(dve.tensor_tensor(B.lb_f[:], B.lb_t[:, 0, :], B.lb_m[:], ALU.mult))
                with dve.Fori(0, 2) as i:
                    for c in range(4):
                        split_lo(dve, U_F + c + AHEAD, i)
                with dve.Fori(0, 2) as i:
                    own.enter(i, 4)
                    for c in range(4):
                        split_lo(dve, U_Q + c + AHEAD, i)
                        dve.wait_ge(proj_read, U_F + c + 1 + 4 * i)
                        f = B.fT[:, bass.ds(4 * i + c, 1), :].rearrange("p o t -> p (o t)")
                        k = B.kT[:, bass.ds(4 * i + c, 1), :].rearrange("p o t -> p (o t)")
                        own(dve.tensor_scalar(f, f, B.lb_1[:, bass.ds(4 * i + c, 1)],
                                              B.lb_f[:, bass.ds(4 * i + c, 1)], ALU.mult, ALU.add))
                        dve.tensor_scalar(k, f, -1.0, 1.0, ALU.mult, ALU.add)
                    own.leave(2)
                for h in range(HEADS):
                    split_lo(dve, U_I + h + AHEAD)
                    f, k, dec, q, kl = (t[:, h, :] for t in (B.fT, B.kT, B.decT, B.qT, B.klT))

                    def chunks(ap):
                        return ap.rearrange("p (n s) -> p n s", s=CHUNK)

                    own(dve.tensor_tensor(chunks(B.first[:]), chunks(f),
                                          B.mask_first[:].unsqueeze(1).broadcast_to([P, NCH, CHUNK]),
                                          ALU.mult))
                    own(dve.tensor_tensor_scan(dec, f, B.first[:], 0.0, ALU.mult, ALU.max))
                    own(dve.reciprocal(B.tmp[:], dec))
                    own(dve.tensor_tensor(k, k, B.tmp[:], ALU.mult))
                    dve.wait_ge(proj_read, DC + h + 1)
                    end = chunks(dec)[:, :, CHUNK - 1:CHUNK].broadcast_to([P, NCH, CHUNK])
                    dve.tensor_tensor(chunks(kl), chunks(k), end, ALU.mult)
                    dve.tensor_tensor(q, q, dec, ALU.mult).then_inc(decays, 1)
                for u in range(U_G, U_G + DC):
                    split_lo(dve, u + AHEAD)
                dve.wait_ge(norm_in, 16)
                dve.wait_ge(row_read, 4)
                for tb in range(TB):
                    dve.tensor_tensor(B.g_row[:, tb, :], B.g_row[:, tb, :], B.norm_t[:], ALU.mult)
                for g in range(4):
                    tb, half = divmod(g, 2)
                    dve.wait_ge(att_raw, g + 1)
                    part = slice(half * 512, (half + 1) * 512)
                    dve.copy_predicated(
                        B.att[:, tb, part].rearrange("p (h t) -> p h t", h=4),
                        B.mask_att[:].unsqueeze(1).broadcast_to([P, 4, P]),
                        acc[:, tb, part].rearrange("p (h t) -> p h t", h=4)).then_inc(att_ready, 1)
                for c in range(NCH - 1):
                    dve.wait_ge(delta, c + 1)
                    new = wk[:, 2 * (c % 2):2 * (c % 2) + 2, :].rearrange("p a b -> p (a b)")
                    if c == 0:
                        dve.tensor_copy(B.state[:, 1, :], new).then_inc(state_ready, 1)
                        continue
                    dve.wait_ge(state_ready, c)
                    for h in range(HEADS):
                        f = slice(h * P, (h + 1) * P)
                        last = dve.scalar_tensor_tensor(
                            B.state[:, c + 1, f], B.state[:, c, f],
                            B.decT[:, h, (c + 1) * CHUNK - 1:(c + 1) * CHUNK], new[:, f], ALU.mult, ALU.add)
                    last.then_inc(state_ready, 1)
                sq = B.klT[:].rearrange("p h t -> p (h t)")[:, 0:D]
                for tb in range(TB):
                    dve.wait_ge(o_copied, tb + 1)
                    own(dve.tensor_tensor(sq, B.o_row[:, tb, :], B.o_row[:, tb, :], ALU.mult))
                    own(dve.tensor_reduce(B.ssq[:, tb, :], sq.rearrange("p (h e) -> p h e", h=HEADS), AX,
                                          ALU.add))
                    own(dve.tensor_scalar(B.ssq[:, tb, :], B.ssq[:, tb, :], 1.0 / P, RMS_EPS, ALU.mult,
                                          ALU.add))
                    dve.reciprocal(B.ssq[:, tb, :], B.ssq[:, tb, :]).then_inc(o_sq, 1)
                    dve.wait_ge(o_rms, tb + 1)
                    for h in range(HEADS):
                        f = slice(h * P, (h + 1) * P)
                        last = dve.scalar_tensor_tensor(B.o_row[:, tb, f], B.o_row[:, tb, f],
                                                        B.ssq[:, tb, h:h + 1], B.g_row[:, tb, f],
                                                        ALU.mult, ALU.mult)
                    last.then_inc(row_ready, 1)
                turn_step(0)
                for u in range(U_O0, U_O0 + DC):
                    split_lo(dve, u + AHEAD)
                dve.wait_ge(x_in, 16)
                layer_norm(0, U_O0 + DC - 1)
                turn_step(1)

            def peer(l):
                for c in (U_KEYS[l] + 2, U_KEYS[l] + 3):
                    split_lo(dve, c)

                def q_step(c):
                    dve.wait_ge(q_hi_ready, NHC * l + c + 1)
                    dve.tensor_tensor(B.q_lo[:, c % 2, :], wk[:, c % 2, 0:SEQ],
                                      B.q_hi[:, c % 2, :].bitcast(F32), ALU.subtract).then_inc(
                        q_lo_ready, 1)

                def top_step(c):
                    dve.wait_ge(sc_copied, NHC * l + c + 1)
                    s = B.sc[:, c % 2]
                    v, ix = B.val[:, :, c, :], B.idx_u[:, :, c, :]
                    for tb in range(TB):
                        last = dve.max(v[:, tb, 0:8], s[:, tb, :])
                    own(last)
                    for tb in range(TB):
                        dve.max_index(ix[:, tb, 0:8], v[:, tb, 0:8], s[:, tb, :])
                        last = dve.match_replace(B.sc_cut[:, tb, :], v[:, tb, 0:8], s[:, tb, :], LOWEST)
                    last.then_inc(sc_done, 1)
                    dve.wait_ge(sc_done, NHC * l + c + 1)
                    for tb in range(TB):
                        last = dve.max(v[:, tb, 8:16], B.sc_cut[:, tb, :])
                    own(last)
                    for tb in range(TB):
                        last = dve.max_index(ix[:, tb, 8:16], v[:, tb, 8:16], B.sc_cut[:, tb, :])
                    own(last)

                for c in range(NHC):
                    split_lo(dve, U_PQ[l] + c + AHEAD)
                    q_step(c)
                    if c:
                        top_step(c - 1)
                top_step(NHC - 1)
                own(dve.tensor_copy(B.idx[:], B.idx_u[:]))

                for tb in range(TB):
                    v4 = B.val[:, tb].rearrange("p (h c) k -> p h c k", c=2)
                    for h in range(HEADS):
                        last = dve.tensor_tensor(
                            B.cand[:, h, :].rearrange("p (a b) -> p a b", a=TOPK),
                            v4[:, h, 0, :].unsqueeze(2).broadcast_to([P, TOPK, TOPK]),
                            v4[:, h, 1, :].unsqueeze(1).broadcast_to([P, TOPK, TOPK]), ALU.add)
                    own(last)
                    for h in range(HEADS):
                        last = dve.max(B.top_s[:, tb, h, 0:8], B.cand[:, h, :])
                    own(last)
                    for h in range(HEADS):
                        dve.max_index(B.top_j[:, tb, h, 0:8], B.top_s[:, tb, h, 0:8], B.cand[:, h, :])
                        last = dve.match_replace(B.cand_cut[:, h, :], B.top_s[:, tb, h, 0:8],
                                                 B.cand[:, h, :], LOWEST)
                    own(last)
                    for h in range(HEADS):
                        last = dve.max(B.top_s[:, tb, h, 8:16], B.cand_cut[:, h, :])
                    own(last)
                    for h in range(HEADS):
                        last = dve.max_index(B.top_j[:, tb, h, 8:16], B.top_s[:, tb, h, 8:16],
                                             B.cand_cut[:, h, :])
                    own(last)
                    dve.tensor_tensor(B.gate[:, tb], B.top_s[:, tb],
                                      B.top_s[:, tb, :, 0:1].broadcast_to([P, HEADS, TOPK]),
                                      ALU.subtract).then_inc(gate_in, 1)
                    j = B.top_j[:, tb].rearrange("p h k -> p (h k)")
                    dve.tensor_scalar(B.j_int[:, 0, :], j, 4, None, ALU.logical_shift_right)
                    own(dve.tensor_scalar(B.j_int[:, 1, :], j, 15, None, ALU.bitwise_and))
                    own(dve.tensor_copy(B.j_f[:], B.j_int[:]))
                    i4 = B.idx[:, tb].rearrange("p (h c) k -> p h c k", c=2)
                    for c in range(2):
                        own(dve.tensor_tensor(
                            B.pick[:], iota[:, 0:TOPK].unsqueeze(1).broadcast_to([P, HEADS * TOPK, TOPK]),
                            B.j_f[:, c, :].unsqueeze(2).broadcast_to([P, HEADS * TOPK, TOPK]),
                            ALU.is_equal))
                        own(dve.tensor_tensor(
                            B.picked[:].rearrange("p (h k) a -> p h k a", h=HEADS),
                            B.pick[:].rearrange("p (h k) a -> p h k a", h=HEADS),
                            i4[:, :, c, :].unsqueeze(2).broadcast_to([P, HEADS, TOPK, TOPK]), ALU.mult))
                        own(dve.tensor_reduce(B.key_sel[:, tb, c, :], B.picked[:], AX, ALU.add))
                    dve.wait_ge(gate_exp, TB * l + tb + 1)
                    own(dve.tensor_reduce(B.gsum[:, tb, :], B.gate[:, tb], AX, ALU.add))
                    own(dve.reciprocal(B.gsum[:, tb, :], B.gsum[:, tb, :]))
                    dve.tensor_tensor(B.gate[:, tb], B.gate[:, tb],
                                      B.gsum[:, tb, :].unsqueeze(2).broadcast_to([P, HEADS, TOPK]),
                                      ALU.mult).then_inc(choice_ready, 1)

                dve.wait_ge(choice_read, TB * (l + 1))

                def onehot_step(c, i):
                    n = 64 * l + c
                    if n >= 2 or type(i) is not int:
                        dve.wait_ge(gate_mm, n - 1 + 4 * i)
                    for b in range(4):
                        t = bass.ds(16 * i + 4 * c + b, 1)
                        dve.tensor_scalar(onehot2[:, c % 2, b, :], iota[:], key2T[:, t], None,
                                          ALU.is_equal)
                        last = dve.tensor_scalar(onehot1[:, c % 2, b, :], iota[:], key1T[:, t],
                                                 gateT[:, t], ALU.is_equal, ALU.mult)
                    last.then_inc(onehots, 1)

                for c in range(4):
                    onehot_step(c, 0)
                with dve.Fori(1, 16) as i:
                    for c in range(4):
                        onehot_step(c, i)

                def weigh(n, i):
                    dve.wait_ge(act_ready, NKEYS * l + n + 1 + 4 * i)
                    if n:
                        dve.wait_ge(w_ready, NKEYS * l + n + 4 * i)
                    at = bass.ds(n + 4 * i, 1)
                    g = B.gates[:, :, at].rearrange("p t o -> p (t o)")
                    dve.tensor_tensor(w_full[:], gelu_a[:, n % 2, :], g, ALU.mult)
                    own(dve.tensor_tensor(w_hi[:, n % 2, :], gelu_a[:, n % 2, :], g, ALU.mult))
                    dve.tensor_tensor(w_lo[:, n % 2, :], w_full[:], w_hi[:, n % 2, :].bitcast(F32),
                                      ALU.subtract).then_inc(w_ready, 1)

                u = U_D[l]
                dve.wait_ge(gate_read, 64 * (l + 1))
                split_lo(dve, u + 2)
                weigh(0, 0)
                split_lo(dve, u + 3)
                split_lo(dve, u + 4)
                with dve.Fori(0, TRIPS) as i:
                    own.enter(i, TILES_LOOP)
                    for b in range(TILES_LOOP):
                        n, c = 1 + b, u + 3 + 2 * b
                        dve.wait_ge(unit_done, consumed(c - 3) + 8 * i)
                        weigh(n, i)
                        split_lo(dve, c + 2, 2 * i)
                        split_lo(dve, c + 3, 2 * i)
                    own.leave(TRIPS)
                c = u + 2 * (NKEYS - 3) + 1
                for n in range(NKEYS - 3, NKEYS):
                    dve.wait_ge(unit_done, consumed(c - 3))
                    weigh(n, 0)
                    split_lo(dve, c + 2)
                    if n < NKEYS - 1:
                        split_lo(dve, c + 3)
                    c += 2
                layer_norm(2 * l + 1, u + 2 * NKEYS - 1)

            def attention():
                for u in range(U_KV, U_KV + 4):
                    split_lo(dve, u + AHEAD)
                for u in range(U_WQ, U_WQ + 8):
                    split_lo(dve, u + AHEAD)

                def rope(v):
                    n = v.shape[1]
                    c = cos_t[:, tb].unsqueeze(1).broadcast_to([P, n, HALF])
                    s = sin_t[:, tb].unsqueeze(1).broadcast_to([P, n, HALF])
                    a, b = v[:, :, 0:HALF], v[:, :, HALF:ROPE]
                    dve.tensor_tensor(B.rt[:, 0, 0:n, :], a, c, ALU.mult)
                    dve.tensor_tensor(B.rt[:, 1, 0:n, :], b, s, ALU.mult)
                    dve.tensor_tensor(B.rt[:, 2, 0:n, :], b, c, ALU.mult)
                    own(dve.tensor_tensor(B.rt[:, 3, 0:n, :], a, s, ALU.mult))
                    dve.tensor_tensor(a, B.rt[:, 0, 0:n, :], B.rt[:, 1, 0:n, :], ALU.subtract)
                    return dve.tensor_tensor(b, B.rt[:, 2, 0:n, :], B.rt[:, 3, 0:n, :], ALU.add)

                dve.wait_ge(tables, 2)
                dve.wait_ge(akv_read, 1)
                for tb in range(TB):
                    if tb:
                        dve.wait_ge(roped, tb)
                    k = B.kv_row[:, tb, 0, :].rearrange("p (h d) -> p h d", h=KVH)
                    own(rope(k))
                    for r in range(2):
                        dve.tensor_copy(B.k2_row[:, tb, :, r, :], k)
                    if tb == 0:
                        dve.wait_ge(aq_read, 2)
                    rope(B.q_row[:, tb, :].rearrange("p (h d) -> p h d", h=QH)).then_inc(roped, 1)

                def normalize(n):
                    tb, kv = divmod(n, KVH)
                    dve.wait_ge(a_out, n + 1)
                    dve.tensor_tensor(
                        B.ao_row[:, tb, kv * GRP * HD:(kv + 1) * GRP * HD].rearrange(
                            "p (a b d) -> p a b d", a=2, b=2),
                        acc[:, 1, (n % 2) * 512:(n % 2) * 512 + GRP * HD].rearrange(
                            "p (a b d) -> p a b d", a=2, b=2),
                        B.rnorm[:, n % 2, :].rearrange("p (b a) -> p a b", b=2).unsqueeze(3).broadcast_to(
                            [P, 2, 2, HD]), ALU.mult).then_inc(a_norm, 1)

                dve.wait_ge(consts, 2)
                for n in range(TB * KVH + 1):
                    if n < TB * KVH:
                        tb, kv = divmod(n, KVH)
                        s, first = n % 2, (0 if tb else P)
                        dve.wait_ge(logits, n + 1)
                        if n >= 2:
                            dve.wait_ge(probs, n - 1)
                        lg = B.logit[:, s, :, first:]
                        own(dve.scalar_tensor_tensor(
                            lg, acc[:, 0, :].rearrange("p (g k) -> p g k", g=GRP)[:, :, first:], HD ** -0.5,
                            B.bias_att[:, first:].unsqueeze(1).broadcast_to([P, GRP, 2 * P - first]),
                            ALU.mult, ALU.add))
                        own(dve.tensor_reduce(B.rmax[:, s, :], lg, AX, ALU.max))
                        sink = sink_t[:, GRP * kv:GRP * (kv + 1)].rearrange("p (a b) -> p b a", a=2)
                        m22 = B.rmax[:, s, :].rearrange("p (b a) -> p b a", b=2)
                        own(dve.tensor_tensor(m22, m22, sink, ALU.max))
                        dve.tensor_tensor(B.sexp[:, s, :].rearrange("p (b a) -> p b a", b=2), sink, m22,
                                          ALU.subtract)
                        dve.tensor_scalar(B.nmax[:, s, :], B.rmax[:, s, :], -1.0, None,
                                          ALU.mult).then_inc(shifted, 1)
                    if n >= 1:
                        m = n - 1
                        tb, kv = divmod(m, KVH)
                        dve.wait_ge(p_turned, m + 1)
                        if m >= 2:
                            dve.wait_ge(a_out, m - 1)
                        w = wk[:, 2 * (m % 2):2 * (m % 2) + 2, :].rearrange(
                            "p a (g r t) -> p (a g) r t", g=2, r=2)
                        if tb:
                            dve.tensor_copy(B.probT[:, m % 2], w).then_inc(p_read, 1)
                        else:
                            dve.tensor_copy(B.probT[:, m % 2, :, 1, :], w[:, :, 1, :]).then_inc(p_read, 1)
                        own(dve.tensor_tensor(B.rnorm[:, m % 2, :], B.rsum[:, m % 2, :],
                                              B.sexp[:, m % 2, :], ALU.add))
                        own(dve.reciprocal(B.rnorm[:, m % 2, :], B.rnorm[:, m % 2, :]))
                        normalize(m)
                turn_step(3)
                for u in range(U_O1, U_O1 + DC):
                    split_lo(dve, u + AHEAD)
                layer_norm(2, U_O1 + DC - 1)
                turn_step(4)

            hgrn()
            if stages > 1:
                peer(0)
            if stages > 2:
                turn_step(2)
                attention()
            if stages > 3:
                peer(1)


def col_blocks(w):
    return w.reshape(DC, P, -1, P).transpose(2, 1, 0, 3).reshape(-1, P, UNIT)


def row_blocks(w):
    return w.reshape(DC // 2, 2, P, -1, 512).transpose(3, 0, 2, 1, 4).reshape(-1, P, UNIT)


def peer_units(w_q, keys, u_tab, v_tab):
    k = keys.reshape(2, NHC // 2, NKEYS, P).transpose(0, 3, 1, 2).reshape(2, P, UNIT)
    up = u_tab.reshape(NKEYS, P, DC, P).transpose(0, 3, 2, 1).reshape(NKEYS, P, UNIT)
    down = v_tab.reshape(NKEYS, P, D)
    dense = np.empty((2 * NKEYS, P, UNIT), up.dtype)
    dense[0] = up[0]
    dense[1:-1:2] = up[1:]
    dense[2::2] = down[:-1]
    dense[-1] = down[-1]
    return [k, col_blocks(w_q), dense]


def kernel(x, positions, hg_w_in, hg_lb, hg_norm_w, hg_w_o, sw_w_q, sw_sinks, sw_w_o, w_kv, peer_w_q,
           peer_sub_keys, peer_u, peer_v, ln_mix_g, ln_mix_b, ln_ffn_g, ln_ffn_b):
    import concourse.bacc as bacc
    from concourse.bass_utils import run_bass_kernel_spmd

    w_in = hg_w_in[0]
    stream = np.concatenate(
        [col_blocks(w_in[:, D:2 * D]), col_blocks(w_in[:, 0:D]), row_blocks(w_in[:, 2 * D:]),
         row_blocks(hg_w_o[0])]
        + peer_units(peer_w_q[0], peer_sub_keys[0], peer_u[0], peer_v[0])
        + [row_blocks(w_kv), row_blocks(sw_w_q[0]), row_blocks(sw_w_o[0])]
        + peer_units(peer_w_q[1], peer_sub_keys[1], peer_u[1], peer_v[1]))
    assert stream.shape == (N_UNITS, P, UNIT)
    arrays = {
        "x": x.reshape(TB, P, D).transpose(1, 0, 2),
        "xT": x.reshape(SEQ, DC, P).transpose(2, 1, 0).reshape(P, DC * SEQ),
        "positions": positions.reshape(TB, P).transpose(1, 0),
        "stream": stream,
        "lb": hg_lb.reshape(2, HEADS, P).transpose(2, 0, 1),
        "norm_w": hg_norm_w.reshape(D),
        "sinks": sw_sinks.reshape(QH),
        "ln": np.stack([np.stack([g[l], b[l]]) for l in range(DEPTH)
                        for g, b in ((ln_mix_g, ln_mix_b), (ln_ffn_g, ln_ffn_b))]),
    }
    nc = bacc.Bacc("TRN2", target_bir_lowering=False, num_devices=1)
    arrays = {f"{k}_dram": np.ascontiguousarray(a) for k, a in arrays.items()}
    args = [nc.dram_tensor(k, a.shape, mybir.dt.from_np(a.dtype), kind="ExternalInput").ap()
            for k, a in arrays.items()]
    out = nc.dram_tensor("out_dram", (P, TB, D), F32, kind="ExternalOutput").ap()
    build(nc, *args, out)
    r = run_bass_kernel_spmd(nc, [arrays], core_ids=[0])
    return np.asarray(r.results[0]["out_dram"]).transpose(1, 0, 2).reshape(1, SEQ, D)
```

```python
from contextlib import ExitStack

import numpy as np

import concourse.bass as bass
from concourse import mybir

F32 = mybir.dt.float32
F32R = mybir.dt.float32r
BF16 = mybir.dt.bfloat16
I32 = mybir.dt.int32
U32 = mybir.dt.uint32
ALU = mybir.AluOpType
ACT = mybir.ActivationFunctionType
AX = mybir.AxisListType.X

P = 128
D = 1024
SEQ = 256
TB = SEQ // P
DC = D // P
HEADS = 8
CHUNK = 32
NCH = SEQ // CHUNK
CPB = P // CHUNK
QH = 16
KVH = 4
GRP = QH // KVH
HD = D // QH
ROPE = HD // 4
HALF = ROPE // 2
THETA = 500000.0
TOPK = 16
NKEYS = 128
NHC = 2 * HEADS
DEPTH = 2
ALPHA = (2.0 * DEPTH) ** 0.25
LN_EPS = 1e-5
RMS_EPS = 1e-6
LOWEST = -3.0e38
TWO_PI = 6.283185307179586
C1 = 6.28125
C2 = 0.0019350051879882812
C3 = TWO_PI - C1 - C2
PI_IN = 3.1415925
ROUND = 12582912.0

UNIT = 1024
RAW = 4
RING = 4
AHEAD = 2
U_F = 0
U_Q = U_F + DC
U_I = U_Q + DC
U_G = U_I + DC
U_O0 = U_G + DC
U_PQ0 = U_O0 + DC
U_EARLY0 = U_PQ0 + NHC
U_KV = U_EARLY0 + 2 * NKEYS
U_WQ = U_KV + DC // 2
U_O1 = U_WQ + DC
U_PQ1 = U_O1 + DC
U_EARLY1 = U_PQ1 + NHC
N_UNITS = U_EARLY1 + 2 * NKEYS
EARLY = 24
EARLY_EXP = 4
TILES_LOOP = 4
TRIPS = (NKEYS - EARLY - 4) // TILES_LOOP
U_PQ = (U_PQ0, U_PQ1)
U_EARLY = (U_EARLY0, U_EARLY1)
U_DOWN = tuple(u + EARLY for u in U_EARLY)
U_REST = tuple(u + 2 * EARLY for u in U_EARLY)
U_END = tuple(u + 2 * NKEYS for u in U_EARLY)
OH = 8
QT = 512 // NKEYS
GATE_TRIPS = SEQ // (4 * QT)


STOP_UNITS = {1: U_PQ0 + 4, 2: U_KV + 4, 3: U_PQ1 + 4}


def head_at(j):
    return 2 * (j % 2) + j // 2


class Chain:

    def __init__(self, eng, sem):
        self.eng, self.sem, self.n, self.more = eng, sem, 0, 0

    def __call__(self, ins):
        self.n += 1
        ins.then_inc(self.sem, 1)
        self.eng.wait_ge(self.sem, self.n + self.more)

    def enter(self, i, per_trip):
        self.start, self.per_trip, self.more = self.n, per_trip, i * per_trip

    def leave(self, trips):
        assert self.n - self.start == self.per_trip, (self.n - self.start, self.per_trip)
        self.n, self.more = self.start + self.per_trip * trips, 0


def build(nc, xT, positions, stream, keys, lb, norm_w, sinks, ln, out, stages=99):
    with ExitStack() as ctx:
        def sb(name, shape, dt=F32):
            return ctx.enter_context(nc.sbuf_tensor(name, shape, dt))

        def sem(name):
            return ctx.enter_context(nc.semaphore(name))

        raw = sb("raw", [P, RAW, UNIT])
        hT_hi = sb("hT_hi", [P, DC, SEQ], F32R)
        hT_lo = sb("hT_lo", [P, DC, SEQ], F32R)
        gateT = sb("gateT", [P, SEQ])
        key1T = sb("key1T", [P, SEQ], BF16)
        iota_b = sb("iota_b", [P, NKEYS, OH], BF16)
        key2T = sb("key2T", [P, SEQ])
        ident = sb("ident", [P, P])
        iota = sb("iota", [P, P])
        alpha_hi = sb("alpha_hi", [P, P], F32R)
        alpha_lo = sb("alpha_lo", [P, P], F32R)
        cos_t = sb("cos_t", [P, TB, HALF])
        sin_t = sb("sin_t", [P, TB, HALF])
        sink_t = sb("sink_t", [P, QH])
        stats = sb("stats", [P, TB, 2, 6])
        mean_var = sb("mean_var", [P, TB, 2])
        rstd = sb("rstd", [P, TB])
        rinv = sb("rinv", [P, TB])

        def overlaid(*groups):
            sizes = []
            keep = {}
            for g in groups:
                inner = ExitStack()
                for name, shape, dt in g:
                    keep[name] = inner.enter_context(nc.sbuf_tensor(name, shape, dt))
                sizes.append(sum(int(np.prod(s[1:])) * (2 if dt == BF16 else 4) for _, s, dt in g))
                inner.close()
            ctx.enter_context(nc.sbuf_tensor(f"room_{groups[0][0][0]}", [P, max(sizes) // 4], F32))
            return keep

        front = [P, RING - 2, UNIT]
        his = overlaid([("hi", [P, RING, UNIT], F32R)],
                       [("hi_front", front, F32), ("onehot2", [P, 2, OH, NKEYS], F32)])
        los = overlaid([("lo", [P, RING, UNIT], F32R)],
                       [("lo_front", front, F32), ("weighted", [P, 4, QT, NKEYS], F32)])
        hi, lo, onehot2, weighted = his["hi"], los["lo"], his["onehot2"], los["weighted"]

        small = overlaid(
            [("onehot1", [P, 2, NKEYS, OH], BF16)],
            [("gelu_a", [P, 2, SEQ], F32), ("w_full", [P, SEQ], F32), ("w_hi", [P, 2, SEQ], F32R),
             ("w_lo", [P, 2, SEQ], F32R)],
            [("ln_par", [P, 2, D], F32)],
        )
        onehot1, gelu_a = small["onehot1"], small["gelu_a"]
        w_full, w_hi, w_lo, ln_par = small["w_full"], small["w_hi"], small["w_lo"], small["ln_par"]

        big = overlaid(
            [("gates", [P, NKEYS, SEQ], F32)],
            [("fT", [P, HEADS, SEQ], F32), ("kT", [P, HEADS, SEQ], F32), ("decT", [P, HEADS, SEQ], F32),
             ("qT", [P, HEADS, SEQ], F32), ("klT", [P, HEADS, SEQ], F32), ("kl_row", [P, TB, D], F32),
             ("v_row", [P, TB, D], F32), ("g_row", [P, TB, D], F32), ("o_row", [P, TB, D], F32),
             ("state", [P, NCH, D], F32), ("att", [P, TB, D], F32), ("norm_t", [P, D], F32),
             ("first", [P, SEQ], F32), ("tmp", [P, SEQ], F32), ("mask_att", [P, P], I32),
             ("mask_first", [P, CHUNK], F32), ("lb_t", [P, 2, HEADS], F32), ("lb_m", [P, HEADS], F32),
             ("lb_f", [P, HEADS], F32), ("lb_1", [P, HEADS], F32), ("ssq", [P, TB, HEADS], F32),
             ("pos_i", [P, TB], I32), ("pos_f", [P, TB], F32), ("freq", [P, HALF], F32),
             ("ang", [P, TB, HALF], F32), ("rnd", [P, TB, HALF], F32), ("red", [P, TB, HALF], F32),
             ("ones_f", [P, P], F32)],
            [("h_row", [P, TB, D], F32), ("act_room", [P, EARLY * SEQ - TB * D], F32),
             ("keys_t", [P, NHC, NKEYS], F32), ("q_t", [P, 2, SEQ], F32),
             ("sc", [P, 2, TB, NKEYS], F32), ("sc_cut", [P, TB, NKEYS], F32),
             ("idx_u", [P, TB, NHC, TOPK], U32),
             ("val", [P, TB, NHC, TOPK], F32), ("idx", [P, TB, NHC, TOPK], F32),
             ("cand", [P, HEADS, TOPK * TOPK], F32), ("cand_cut", [P, HEADS, TOPK * TOPK], F32),
             ("top_s", [P, TB, HEADS, TOPK], F32), ("top_j", [P, TB, HEADS, TOPK], U32),
             ("j_int", [P, 2, HEADS * TOPK], U32), ("j_f", [P, 2, HEADS * TOPK], F32),
             ("pick", [P, HEADS * TOPK, TOPK], F32), ("picked", [P, HEADS * TOPK, TOPK], F32),
             ("key_sel", [P, TB, 2, HEADS * TOPK], F32), ("gate", [P, TB, HEADS, TOPK], F32),
             ("gsum", [P, TB, HEADS], F32)],
            [("h_room", [P, TB, D], F32), ("q_row", [P, TB, D], F32), ("kv_row", [P, TB, 2, KVH * HD], F32),
             ("k2_row", [P, TB, KVH, 2, HD], F32), ("aqT", [P, DC, SEQ], F32),
             ("k2T", [P, KVH, SEQ], F32), ("rt", [P, 4, QH, HALF], F32),
             ("logit", [P, 2, GRP, 2 * P], F32), ("prob", [P, 2, GRP, 2 * P], F32),
             ("probT", [P, 2, GRP, 2, P], F32), ("bias_att", [P, 2 * P], F32),
             ("rmax", [P, 2, GRP], F32), ("nmax", [P, 2, GRP], F32), ("rsum", [P, 2, GRP], F32),
             ("sexp", [P, 2, GRP], F32), ("rnorm", [P, 2, GRP], F32), ("ao_row", [P, TB, D], F32)],
        )
        B = type("Big", (), big)
        h_row = B.h_row

        acc = ctx.enter_context(nc.psum_tensor("acc", [P, TB, D], F32))
        wk = ctx.enter_context(nc.psum_tensor("wk", [P, 4, 512], F32))

        raw_in = [sem(f"raw_in{i}") for i in range(RAW)]
        hi_ready, lo_ready, unit_done = sem("hi_ready"), sem("lo_ready"), sem("unit_done")
        dve_own, act_own, pool_own = sem("dve_own"), sem("act_own"), sem("pool_own")
        xT_in, small_in, par_in, norm_in, keys_in = (
            sem("xT_in"), sem("small_in"), sem("par_in"), sem("norm_in"), sem("keys_in"))
        consts = sem("consts")
        alpha_hi_ready, alpha_ready = sem("alpha_hi_ready"), sem("alpha_ready")
        xT_hi_ready, xT_ready = sem("xT_hi_ready"), sem("xT_ready")
        lb_shift, lb_exp = sem("lb_shift"), sem("lb_exp")
        angles, tables = sem("angles"), sem("tables")
        proj_read, row_read = sem("proj_read"), sem("row_read")
        decays = sem("decays")
        kl_turned, kl_read = sem("kl_turned"), sem("kl_read")
        att_raw, att_ready = sem("att_raw"), sem("att_ready")
        delta, state_ready = sem("delta"), sem("state_ready")
        o_sum, o_copied, o_sq, o_rms = sem("o_sum"), sem("o_copied"), sem("o_sq"), sem("o_rms")
        row_ready, turned, turn_hi, turn_lo = (
            sem("row_ready"), sem("turned"), sem("turn_hi"), sem("turn_lo"))
        var_ready, rstd_ready = sem("var_ready"), sem("rstd_ready")
        q_ready, sc_ready, sc_copied, sc_done = (
            sem("q_ready"), sem("sc_ready"), sem("sc_copied"), sem("sc_done"))
        gate_in, gate_exp, choice_ready, choice_turned, choice_read = (
            sem("gate_in"), sem("gate_exp"), sem("choice_ready"), sem("choice_turned"), sem("choice_read"))
        onehot1_ready, onehot2_ready = sem("onehot1_ready"), sem("onehot2_ready")
        weighted_pool, weighted_act = sem("weighted_pool"), sem("weighted_act")
        gate_mm, gate_read, early_weighed = sem("gate_mm"), sem("gate_read"), sem("early_weighed")
        w_hi_ready = sem("w_hi_ready")
        act_ready, w_ready, tile_done = sem("act_ready"), sem("w_ready"), sem("tile_done")
        aq_read, akv_read, roped, a_turned, a_turn_read = (
            sem("aq_read"), sem("akv_read"), sem("roped"), sem("a_turned"), sem("a_turn_read"))
        logits, shifted, probs, p_turned, p_read, a_out, a_norm = (
            sem("logits"), sem("shifted"), sem("probs"), sem("p_turned"), sem("p_read"), sem("a_out"),
            sem("a_norm"))
        stored = sem("stored")

        block = ctx.enter_context(nc.Block())

        def split_hi(act, c, i=0):
            if type(i) is int and c + RING * i >= N_UNITS:
                return
            act.wait_ge(raw_in[c % RAW], 16 * (c // RAW + 1) + 16 * i)
            if type(i) is not int or c >= RING:
                act.wait_ge(unit_done, c - RING + 1 + RING * i)
            act.activation(hi[:, c % RING, :], raw[:, c % RAW, :], ACT.Copy).then_inc(hi_ready, 1)

        def split_lo(eng, c, i=0):
            if type(i) is int and c + RING * i >= N_UNITS:
                return
            eng.wait_ge(hi_ready, c + 1 + RING * i)
            eng.tensor_tensor(lo[:, c % RING, :], raw[:, c % RAW, :], hi[:, c % RING, :].bitcast(F32),
                              ALU.subtract).then_inc(lo_ready, 1)

        @block.sync
        def _(sp):
            n_units = N_UNITS if stages > 90 else STOP_UNITS.get(stages, N_UNITS)
            for c in range(RING):
                sp.dma_start(raw[:, c % RAW, :], stream[c]).then_inc(raw_in[c % RAW], 16)
            with sp.Fori(1, n_units // RING) as i:
                for c in range(RING):
                    sp.wait_ge(lo_ready, c - RAW + 1 + RING * i)
                    sp.dma_start(raw[:, c % RAW, :], stream[bass.ds(c + RING * i, 1)].rearrange(
                        "o p f -> (o p) f")).then_inc(raw_in[c % RAW], 16)
            sp.wait_ge(row_ready, {1: 4, 2: 6, 3: 8}.get(stages, 10))
            sp.dma_start(out, h_row[:]).then_inc(stored, 16)
            sp.wait_ge(stored, 16)

        @block.gpsimd
        def _(pool):
            own = Chain(pool, pool_own)
            pool.dma_start(B.lb_t[:], lb).then_inc(small_in, 16)
            pool.dma_start(B.pos_i[:], positions).then_inc(small_in, 16)
            pool.dma_start(sink_t[:], sinks.partition_broadcast(P)).then_inc(small_in, 16)
            pool.dma_start(B.norm_t[:], norm_w.partition_broadcast(P)).then_inc(norm_in, 16)
            own(pool.memset(ident[:], 0.0))
            own(pool.affine_select(out=ident[:], in_=ident[:], compare_op=ALU.not_equal, fill=1.0, base=0,
                                   pattern=[[-1, P]], channel_multiplier=1))
            own(pool.iota(iota[:], pattern=[[1, P]], base=0, channel_multiplier=0,
                          allow_small_or_imprecise_dtypes=True))
            own(pool.memset(B.ones_f[:], 1.0))
            m3 = B.ones_f[:].rearrange("p (c i) -> p c i", c=CPB)
            own(pool.affine_select(out=m3, in_=m3, compare_op=ALU.is_ge, fill=0.0, base=0,
                                   pattern=[[CHUNK, CPB], [1, CHUNK]], channel_multiplier=-1))
            own(pool.affine_select(out=m3, in_=m3, compare_op=ALU.is_ge, fill=0.0, base=0,
                                   pattern=[[-CHUNK, CPB], [0, CHUNK]], channel_multiplier=1))
            own(pool.tensor_copy(B.mask_att[:], B.ones_f[:]))
            own(pool.memset(B.mask_first[:], 1.0))
            own(pool.affine_select(out=B.mask_first[:], in_=B.mask_first[:], compare_op=ALU.is_equal,
                                   fill=0.0, base=0, pattern=[[1, CHUNK]], channel_multiplier=0))
            for k in range(HALF):
                own(pool.memset(B.freq[:, k:k + 1], float(np.float32(THETA) ** np.float32(-2 * k / ROPE))))
            pool.memset(B.att[:], 0.0).then_inc(consts, 1)

            def weigh_onehots(l):
                def step(c, i):
                    n = 4 * GATE_TRIPS * l + c
                    pool.wait_ge(onehot1_ready, 2 * GATE_TRIPS * l + c // 2 + 1 + 2 * i)
                    if n >= 4 or type(i) is not int:
                        pool.wait_ge(gate_mm, n - 3 + 4 * i)
                    gate = gateT[:, bass.ds(4 * QT * i + QT * c, QT)]
                    pool.tensor_tensor(
                        weighted[:, c],
                        onehot1[:, c // 2, :, c % 2 * QT:(c % 2 + 1) * QT].rearrange("p k t -> p t k"),
                        gate.unsqueeze(2).broadcast_to([P, QT, NKEYS]), ALU.mult).then_inc(
                        weighted_pool, 1)

                pool.wait_ge(choice_read, TB * (l + 1))
                for c in range(3):
                    step(c, 0)
                with pool.Fori(1, GATE_TRIPS) as i:
                    for c in range(3):
                        step(c, i)

            for k in range(min(2 * DEPTH, stages)):
                if k % 2 == 0:
                    pool.wait_ge(unit_done, (U_O0, U_O1)[k // 2] + 1)
                    pool.dma_start(B.keys_t[:], keys[k // 2]).then_inc(keys_in, 16)
                else:
                    pool.wait_ge(unit_done, U_END[k // 2])
                for a in range(2):
                    pool.dma_start(ln_par[:, a, :], ln[k, a:a + 1, :].rearrange("a d -> (a d)")
                                   .partition_broadcast(P)).then_inc(par_in, 16)
                if k % 2 == 0 and stages > k + 1:
                    pool.wait_ge(lo_ready, U_PQ[k // 2] + AHEAD)
                    with pool.Fori(0, (NHC + EARLY) // RING) as i:
                        for c in range(RING):
                            split_lo(pool, U_PQ[k // 2] + AHEAD + c, i)
                    weigh_onehots(k // 2)
                if k == 1 and stages > 2:
                    own(pool.memset(B.bias_att[:], 0.0))
                    own(pool.affine_select(out=B.bias_att[:], in_=B.bias_att[:], compare_op=ALU.is_ge,
                                           fill=LOWEST, base=P, pattern=[[-1, 2 * P]],
                                           channel_multiplier=1))
                    pool.affine_select(out=B.bias_att[:], in_=B.bias_att[:], compare_op=ALU.is_ge,
                                       fill=LOWEST, base=-1, pattern=[[1, 2 * P]],
                                       channel_multiplier=-1).then_inc(consts, 1)

        @block.tensor
        def _(pe):
            def col_unit(c, i, bank):
                pe.wait_ge(lo_ready, c + 1 + RING * i)
                s = c % RING
                for dc in range(DC):
                    wh, wl = hi[:, s, dc * P:(dc + 1) * P], lo[:, s, dc * P:(dc + 1) * P]
                    o = wk[:, bank, 0:SEQ]
                    pe.matmul(o, wh, hT_hi[:, dc, :], start=(dc == 0), stop=False)
                    pe.matmul(o, wh, hT_lo[:, dc, :], start=False, stop=False)
                    last = pe.matmul(o, wl, hT_hi[:, dc, :], start=False, stop=(dc == DC - 1))
                last.then_inc(unit_done, 1)

            def residual(tb):
                t = slice(tb * P, (tb + 1) * P)
                for dc in range(DC):
                    o = acc[:, tb, dc * P:(dc + 1) * P]
                    pe.matmul(o, hT_hi[:, dc, t], alpha_hi[:], start=(dc % 4 == 0), stop=False,
                              skip_group_check=True)
                    pe.matmul(o, hT_hi[:, dc, t], alpha_lo[:], start=False, stop=False,
                              skip_group_check=True)
                    pe.matmul(o, hT_lo[:, dc, t], alpha_hi[:], start=False, stop=False,
                              skip_group_check=True)

            def row_units(u, dsts, start=True):
                for k in range(4):
                    pe.wait_ge(lo_ready, u + k + 1)
                    s = (u + k) % RING
                    for j in range(2):
                        dc = 2 * k + j
                        wh, wl = hi[:, s, j * 512:(j + 1) * 512], lo[:, s, j * 512:(j + 1) * 512]
                        for tb in range(TB):
                            hh, hl = hT_hi[:, dc, tb * P:(tb + 1) * P], hT_lo[:, dc, tb * P:(tb + 1) * P]
                            pe.matmul(dsts[tb], hh, wh, start=(start and dc == 0), stop=False,
                                      skip_group_check=True)
                            pe.matmul(dsts[tb], hh, wl, start=False, stop=False, skip_group_check=True)
                            last = pe.matmul(dsts[tb], hl, wh, start=False, stop=(dc == DC - 1),
                                             skip_group_check=True)
                    last.then_inc(unit_done, 1)

            def turn(n, src, rows=None):
                for g in range(4):
                    tb, half = divmod(g, 2)
                    if half == 0 and rows is not None:
                        pe.wait_ge(row_ready, rows + tb + 1)
                    for b in range(4):
                        dc = 4 * half + b
                        last = pe.transpose(wk[:, g, b * P:(b + 1) * P], src[:, tb, dc * P:(dc + 1) * P],
                                            ident[:])
                    last.then_inc(turned, 1)
                pe.wait_ge(turn_lo, 4 * n + 4)

            def hgrn():
                pe.wait_ge(consts, 1)
                pe.wait_ge(xT_ready, 1)
                for c in range(4):
                    col_unit(U_F + c, 0, c)
                with pe.Fori(1, 4) as i:
                    for c in range(4):
                        pe.wait_ge(proj_read, c - 3 + 4 * i)
                        col_unit(U_F + c, i, c)
                for g in range(4):
                    if g == 0:
                        pe.wait_ge(proj_read, 2 * DC)
                    if g >= 2:
                        pe.wait_ge(row_read, g - 1)
                    row_units(U_I + 4 * g, [wk[:, 2 * (g % 2) + tb, :] for tb in range(TB)])
                pe.wait_ge(decays, HEADS)
                pe.wait_ge(row_read, 4)
                for g in range(4):
                    tb, half = divmod(g, 2)
                    for b in range(4):
                        last = pe.transpose(wk[:, g, b * P:(b + 1) * P],
                                            B.klT[:, 4 * half + b, tb * P:(tb + 1) * P], ident[:])
                    last.then_inc(kl_turned, 1)
                for g in range(4):
                    tb, half = divmod(g, 2)
                    for b in range(4):
                        h, t = 4 * half + b, slice(tb * P, (tb + 1) * P)
                        last = pe.matmul(acc[:, tb, h * P:(h + 1) * P], B.kT[:, h, t], B.qT[:, h, t],
                                         start=True, stop=True)
                    last.then_inc(att_raw, 1)
                pe.wait_ge(kl_read, 4)
                for c in range(NCH - 1):
                    tb, r = c // CPB, slice(c % CPB * CHUNK, (c % CPB + 1) * CHUNK)
                    if c >= 2:
                        pe.wait_ge(state_ready, c - 1)
                    for h in range(HEADS):
                        f = slice(h * P, (h + 1) * P)
                        last = pe.matmul(wk[:, 2 * (c % 2) + h // 4, h % 4 * P:(h % 4 + 1) * P],
                                         B.kl_row[r, tb, f], B.v_row[r, tb, f], start=True, stop=True)
                    last.then_inc(delta, 1)
                pe.wait_ge(att_ready, 4)
                for tb in range(TB):
                    pe.wait_ge(state_ready, min(CPB * (tb + 1), NCH) - 1)
                    for h in range(HEADS):
                        f = slice(h * P, (h + 1) * P)
                        last = pe.matmul(acc[:, tb, f], B.att[:, tb, f], B.v_row[:, tb, f], start=True,
                                         stop=False, skip_group_check=True)
                        for c in range(CPB):
                            n = CPB * tb + c
                            if n == 0:
                                continue
                            last = pe.matmul(acc[c * CHUNK:(c + 1) * CHUNK, tb, f],
                                             B.qT[:, h, n * CHUNK:(n + 1) * CHUNK], B.state[:, n, f],
                                             start=False, stop=True, skip_group_check=True)
                    last.then_inc(o_sum, 1)
                pe.wait_ge(o_copied, TB)
                pe.wait_ge(alpha_ready, 1)
                for tb in range(TB):
                    residual(tb)
                turn(0, B.o_row, 0)
                for g in range(2):
                    row_units(U_O0 + 4 * g, [acc[:, tb, g * 512:(g + 1) * 512] for tb in range(TB)], False)
                turn(1, h_row, 2)

            def scores(l, c, i):
                n = NHC * l + c
                pe.wait_ge(q_ready, n + 1 + 4 * i)
                if n >= 2 or type(i) is not int:
                    pe.wait_ge(sc_copied, n - 1 + 4 * i)
                key = B.keys_t[:, bass.ds(c + 4 * i, 1), :].rearrange("p o k -> p (o k)")
                for tb in range(TB):
                    t = slice(tb * P, (tb + 1) * P)
                    last = pe.matmul(wk[:, 2 + c % 2, t], B.q_t[:, c % 2, t], key, start=True, stop=True)
                last.then_inc(sc_ready, 1)

            def choice_step(l, c, i):
                n = NHC * l + c
                if n >= 2 or type(i) is not int:
                    pe.wait_ge(q_ready, n - 1 + 4 * i)
                col_unit(U_PQ[l] + c, i, c % 2)
                if c >= 1:
                    scores(l, c - 1, i)

            def peer(l):
                for c in range(4):
                    if c == 1:
                        pe.wait_ge(keys_in, 16 * (l + 1))
                    choice_step(l, c, 0)
                with pe.Fori(1, 4) as i:
                    for c in range(4):
                        if c == 0:
                            pe.wait_ge(q_ready, NHC * l - 1 + 4 * i)
                            col_unit(U_PQ[l], i, 0)
                            scores(l, 3, i - 1)
                        else:
                            choice_step(l, c, i)
                scores(l, 3, 3)
                for tb in range(TB):
                    residual(tb)
                pe.wait_ge(q_ready, NHC * (l + 1))
                pe.wait_ge(sc_copied, NHC * (l + 1))
                for c in range(4):
                    col_unit(U_EARLY[l] + c, 0, c)
                with pe.Fori(1, EARLY // 4) as i:
                    for c in range(4):
                        pe.wait_ge(act_ready, NKEYS * l + c - 3 + 4 * i)
                        col_unit(U_EARLY[l] + c, i, c)
                pe.wait_ge(act_ready, NKEYS * l + EARLY)
                for tb in range(TB):
                    pe.wait_ge(choice_ready, TB * l + tb + 1)
                    for a, src in enumerate((B.gate[:, tb].rearrange("p h k -> p (h k)"),
                                             B.key_sel[:, tb, 0, :], B.key_sel[:, tb, 1, :])):
                        last = pe.transpose(wk[:, tb, a * P:(a + 1) * P], src, ident[:])
                    last.then_inc(choice_turned, 1)
                def gate_step(c, i):
                    n = 4 * GATE_TRIPS * l + c
                    pe.wait_ge(onehot2_ready, 2 * GATE_TRIPS * l + c // 2 + 1 + 2 * i)
                    if c < 3:
                        pe.wait_ge(weighted_pool, 3 * GATE_TRIPS * l + c + 1 + 3 * i)
                    else:
                        pe.wait_ge(weighted_act, GATE_TRIPS * l + 1 + i)
                    if n >= 4 or type(i) is not int:
                        pe.wait_ge(gate_read, n - 3 + 4 * i)
                        pe.wait_ge(early_weighed, 2 * GATE_TRIPS * l + c // 2 - 1 + 2 * i)
                    for b in range(QT):
                        last = pe.matmul(wk[:, c, b * P:(b + 1) * P], onehot2[:, c // 2, c % 2 * QT + b, :],
                                         weighted[:, c, b, :], start=True, stop=True)
                    last.then_inc(gate_mm, 1)

                pe.wait_ge(choice_read, TB * (l + 1))
                for c in range(4):
                    gate_step(c, 0)
                with pe.Fori(1, GATE_TRIPS) as i:
                    for c in range(4):
                        gate_step(c, i)

                def down(c, i, n, slot, final=False):
                    pe.wait_ge(lo_ready, c + 1 + RING * i)
                    pe.wait_ge(w_ready, NKEYS * l + n + 1)
                    s = c % RING
                    for tb in range(TB):
                        wh, wl = w_hi[:, slot, tb * P:(tb + 1) * P], w_lo[:, slot, tb * P:(tb + 1) * P]
                        for half in range(2):
                            f = slice(half * 512, (half + 1) * 512)
                            pe.matmul(acc[:, tb, f], wh, hi[:, s, f], start=False, stop=False,
                                      skip_group_check=True)
                            pe.matmul(acc[:, tb, f], wh, lo[:, s, f], start=False, stop=False,
                                      skip_group_check=True)
                            last = pe.matmul(acc[:, tb, f], wl, hi[:, s, f], start=False, stop=final,
                                             skip_group_check=True)
                    last.then_inc(unit_done, 1)

                with pe.Fori(0, EARLY // 4) as i:
                    for c in range(4):
                        down(U_DOWN[l] + c, i, c + 4 * i, c % 2)
                u = U_REST[l]
                pe.wait_ge(gate_read, 4 * GATE_TRIPS * (l + 1))
                pe.wait_ge(early_weighed, 2 * GATE_TRIPS * (l + 1))
                col_unit(u, 0, EARLY % 4)
                col_unit(u + 1, 0, (EARLY + 1) % 4)
                down(u + 2, 0, EARLY, 0)
                with pe.Fori(0, TRIPS) as i:
                    for b in range(TILES_LOOP):
                        n = EARLY + 1 + b
                        c = u + 3 + 2 * b
                        pe.wait_ge(act_ready, NKEYS * l + n - 2 + 4 * i)
                        col_unit(c, 2 * i, (n + 1) % 4)
                        down(c + 1, 2 * i, n + 4 * i, n % 2)
                c = U_END[l] - 5
                for n in (NKEYS - 3, NKEYS - 2):
                    pe.wait_ge(act_ready, NKEYS * l + n - 2)
                    col_unit(c, 0, (n + 1) % 4)
                    down(c + 1, 0, n, n % 2)
                    c += 2
                down(c, 0, NKEYS - 1, (NKEYS - 1) % 2, True)

            def attention():
                row_units(U_KV, [wk[:, tb, :] for tb in range(TB)])
                for g in range(2):
                    if g == 1:
                        pe.wait_ge(akv_read, 1)
                    row_units(U_WQ + 4 * g, [wk[:, 2 - 2 * g + tb, :] for tb in range(TB)])
                pe.wait_ge(aq_read, 2)
                for tb in range(TB):
                    pe.wait_ge(roped, tb + 1)
                    for half in range(3):
                        g = 3 * tb + half
                        if g >= 4:
                            pe.wait_ge(a_turn_read, g - 3)
                        for b in range(4):
                            src = (B.q_row[:, tb, (4 * half + b) * P:(4 * half + b + 1) * P] if half < 2
                                   else B.k2_row[:, tb, b].rearrange("p r d -> p (r d)"))
                            last = pe.transpose(wk[:, g % 4, b * P:(b + 1) * P], src, ident[:])
                        last.then_inc(a_turned, 1)
                pe.wait_ge(a_turn_read, 6)

                def logit_step(n):
                    tb, kv = divmod(n, KVH)
                    if n >= 1:
                        pe.wait_ge(shifted, n)
                    for j in range(GRP):
                        h = GRP * kv + head_at(j)
                        r = slice(h % 2 * HD, (h % 2 + 1) * HD)
                        lhs = B.aqT[r, h // 2, tb * P:(tb + 1) * P]
                        keys = slice(0, 2 * P) if tb else slice(0, P)
                        o = acc[:, 0, j * 256 + (0 if tb else P):(j + 1) * 256]
                        last = pe.matmul(o, lhs, B.k2T[r, kv, keys], start=True, stop=True)
                    last.then_inc(logits, 1)

                def value_step(n):
                    tb, kv = divmod(n, KVH)
                    pe.wait_ge(probs, n + 1)
                    parts = (0, 1) if tb else (1,)
                    if n >= 2:
                        pe.wait_ge(p_read, n - 1)
                    for j in range(GRP):
                        for part in parts:
                            o = wk[:, 2 * (n % 2) + j // 2, (j % 2 * 2 + part) * P:(j % 2 * 2 + part + 1) * P]
                            last = pe.transpose(o, B.prob[:, n % 2, j, part * P:(part + 1) * P], ident[:])
                    last.then_inc(p_turned, 1)

                def out_step(n):
                    tb, kv = divmod(n, KVH)
                    parts = (0, 1) if tb else (1,)
                    pe.wait_ge(p_read, n + 1)
                    if n >= 2:
                        pe.wait_ge(a_norm, n - 1)
                    for j in range(GRP):
                        g = head_at(j)
                        for part in parts:
                            last = pe.matmul(acc[:, 1, (n % 2) * 512 + g * HD:(n % 2) * 512 + (g + 1) * HD],
                                             B.probT[:, n % 2, j, part, :],
                                             B.kv_row[:, tb - 1 + part, 1, kv * HD:(kv + 1) * HD],
                                             start=(part == parts[0]), stop=(part == 1))
                    last.then_inc(a_out, 1)

                for n in range(TB * KVH + 1):
                    if n < TB * KVH:
                        logit_step(n)
                    else:
                        pe.wait_ge(shifted, n)
                        residual(0)
                    if n >= 1:
                        value_step(n - 1)
                        out_step(n - 1)
                pe.wait_ge(a_norm, TB * KVH)
                residual(1)
                turn(3, B.ao_row)
                for g in range(2):
                    row_units(U_O1 + 4 * g, [acc[:, tb, g * 512:(g + 1) * 512] for tb in range(TB)], False)
                turn(4, h_row, 6)

            hgrn()
            if stages > 1:
                peer(0)
            if stages > 2:
                turn(2, h_row, 4)
                attention()
            if stages > 3:
                peer(1)

        @block.scalar
        def _(act):
            own = Chain(act, act_own)

            def turn_step(n):
                for g in range(4):
                    tb, half = divmod(g, 2)
                    act.wait_ge(turned, 4 * n + g + 1)
                    act.activation(hT_hi[:, 4 * half:4 * half + 4, tb * P:(tb + 1) * P],
                                   wk[:, g, :].rearrange("p (b t) -> p b t", b=4),
                                   ACT.Copy).then_inc(turn_hi, 1)

            def norm_step(k):
                act.wait_ge(var_ready, k + 1)
                act.activation(rstd[:], rinv[:], ACT.Sqrt).then_inc(rstd_ready, 1)

            def hgrn():
                xt_raw = B.o_row[:].rearrange("p a b -> p (a b)")
                act.dma_start(xt_raw, xT).then_inc(xT_in, 16)
                split_hi(act, 0)
                act.wait_ge(xT_in, 16)
                act.activation(hT_hi[:].rearrange("p c t -> p (c t)"), xt_raw, ACT.Copy).then_inc(
                    xT_hi_ready, 1)
                split_hi(act, 1)
                act.wait_ge(consts, 1)
                act.activation(alpha_hi[:], ident[:], ACT.Copy, scale=ALPHA).then_inc(alpha_hi_ready, 1)
                act.wait_ge(lb_shift, 1)
                act.activation(B.lb_t[:], B.lb_t[:], ACT.Exp).then_inc(lb_exp, 1)
                act.wait_ge(angles, 1)
                act.activation(sin_t[:], B.red[:], ACT.Sin).then_inc(tables, 1)
                act.wait_ge(angles, 2)
                act.activation(cos_t[:], B.ang[:], ACT.Sin).then_inc(tables, 1)
                for c in range(DC):
                    split_hi(act, U_F + c + AHEAD)
                    act.wait_ge(unit_done, U_F + c + 1)
                    act.activation(B.fT[:, c, :], wk[:, c % 4, 0:SEQ], ACT.Sigmoid).then_inc(proj_read, 1)
                with act.Fori(0, 2) as i:
                    for c in range(4):
                        split_hi(act, U_Q + c + AHEAD, i)
                        act.wait_ge(unit_done, U_Q + c + 1 + RING * i)
                        act.activation(B.qT[:, bass.ds(4 * i + c, 1), :].rearrange("p o t -> p (o t)"),
                                       wk[:, c, 0:SEQ], ACT.Silu).then_inc(proj_read, 1)
                for g in range(4):
                    for k in range(4):
                        split_hi(act, U_I + 4 * g + k + AHEAD)
                    act.wait_ge(unit_done, U_I + 4 * g + 4)
                    dst, func = (B.v_row, ACT.Copy) if g < 2 else (B.g_row, ACT.Silu)
                    act.activation(dst[:, :, g % 2 * 512:(g % 2 + 1) * 512],
                                   wk[:, 2 * (g % 2):2 * (g % 2) + 2, :], func).then_inc(row_read, 1)
                for g in range(4):
                    tb, half = divmod(g, 2)
                    act.wait_ge(kl_turned, g + 1)
                    act.activation(B.kl_row[:, tb, half * 512:(half + 1) * 512], wk[:, g, :],
                                   ACT.Copy).then_inc(kl_read, 1)
                for tb in range(TB):
                    act.wait_ge(o_sum, tb + 1)
                    act.activation(B.o_row[:, tb, :], acc[:, tb, :], ACT.Copy).then_inc(o_copied, 1)
                    act.wait_ge(o_sq, tb + 1)
                    act.activation(B.ssq[:, tb, :], B.ssq[:, tb, :], ACT.Sqrt).then_inc(o_rms, 1)
                turn_step(0)
                for u in range(U_O0, U_O0 + DC):
                    split_hi(act, u + AHEAD)
                norm_step(0)
                turn_step(1)

            def peer(l):
                def q_step(c, i):
                    n = NHC * l + c
                    act.wait_ge(unit_done, U_PQ[l] + c + 1 + RING * i)
                    if n >= 2 or type(i) is not int:
                        act.wait_ge(sc_ready, n - 1 + 4 * i)
                    act.activation(B.q_t[:, c % 2, :], wk[:, c % 2, 0:SEQ], ACT.Copy).then_inc(
                        q_ready, 1)

                def s_step(c, i):
                    n = NHC * l + c
                    act.wait_ge(sc_ready, n + 1 + 4 * i)
                    if n >= 2 or type(i) is not int:
                        act.wait_ge(sc_done, n - 1 + 4 * i)
                    act.activation(B.sc[:, c % 2].rearrange("p b k -> p (b k)"),
                                   wk[:, 2 + c % 2, 0:SEQ], ACT.Copy).then_inc(sc_copied, 1)

                for c in range(4):
                    split_hi(act, U_PQ[l] + c + AHEAD)
                    q_step(c, 0)
                    if c:
                        s_step(c - 1, 0)
                with act.Fori(1, 4) as i:
                    for c in range(4):
                        split_hi(act, U_PQ[l] + c + AHEAD, i)
                        if c == 0:
                            act.wait_ge(unit_done, U_PQ[l] + 1 + RING * i)
                            act.wait_ge(sc_ready, NHC * l - 1 + 4 * i)
                            act.activation(B.q_t[:, 0, :], wk[:, 0, 0:SEQ], ACT.Copy).then_inc(
                                q_ready, 1)
                            s_step(3, i - 1)
                        else:
                            q_step(c, i)
                            s_step(c - 1, i)
                s_step(3, 3)
                for tb, (first, last) in enumerate(((0, EARLY_EXP), (EARLY_EXP, EARLY // 4))):
                    with act.Fori(first, last) as i:
                        for c in range(4):
                            split_hi(act, U_EARLY[l] + c + AHEAD, i)
                            act.wait_ge(unit_done, U_EARLY[l] + c + 1 + RING * i)
                            act.activation(B.gates[:, bass.ds(4 * i + c, 1), :].rearrange(
                                "p o t -> p (o t)"), wk[:, c, 0:SEQ], ACT.Gelu).then_inc(act_ready, 1)
                    act.wait_ge(gate_in, TB * l + tb + 1)
                    act.activation(B.gate[:, tb], B.gate[:, tb], ACT.Exp).then_inc(gate_exp, 1)
                for tb in range(TB):
                    act.wait_ge(choice_turned, TB * l + tb + 1)
                    t = slice(tb * P, (tb + 1) * P)
                    act.activation(gateT[:, t], wk[:, tb, 0:P], ACT.Copy)
                    act.activation(key1T[:, t], wk[:, tb, P:2 * P], ACT.Copy)
                    act.activation(key2T[:, t], wk[:, tb, 2 * P:3 * P], ACT.Copy).then_inc(choice_read, 1)

                def gate_trip(i):
                    n = 4 * GATE_TRIPS * l
                    act.wait_ge(onehot1_ready, 2 * GATE_TRIPS * l + 2 + 2 * i)
                    if l > 0 or type(i) is not int:
                        act.wait_ge(gate_mm, n + 4 * i)
                    for b in range(QT):
                        last = act.activation(weighted[:, 3, b, :], onehot1[:, 1, :, QT + b], ACT.Copy,
                                              scale=gateT[:, bass.ds(4 * QT * i + 3 * QT + b, 1)])
                    last.then_inc(weighted_act, 1)
                    for c in range(4):
                        act.wait_ge(gate_mm, n + c + 1 + 4 * i)
                        act.activation(
                            B.gates[:, EARLY:, bass.ds(4 * QT * i + QT * c, QT)],
                            wk[:, c, :].rearrange("p (t k) -> p k t", t=QT)[:, EARLY:, :],
                            ACT.Copy).then_inc(gate_read, 1)

                gate_trip(0)
                with act.Fori(1, GATE_TRIPS) as i:
                    gate_trip(i)

                def gelu(n, i, c, ci):
                    act.wait_ge(unit_done, c + 1 + RING * ci)
                    act.wait_ge(w_ready, NKEYS * l + n - 1 + 4 * i)
                    act.activation(gelu_a[:, n % 2, :], wk[:, n % 4, 0:SEQ], ACT.Gelu).then_inc(
                        act_ready, 1)

                act.wait_ge(early_weighed, 2 * GATE_TRIPS * (l + 1))
                with act.Fori(0, EARLY // 4) as i:
                    for c in range(4):
                        act.wait_ge(unit_done, U_DOWN[l] + c - 1 + RING * i)
                        act.activation(w_hi[:, c % 2, :], B.gates[:, bass.ds(4 * i + c, 1), :].rearrange(
                            "p o t -> p (o t)"), ACT.Copy).then_inc(w_hi_ready, 1)
                        split_hi(act, U_DOWN[l] + c + AHEAD, i)
                u = U_REST[l]
                split_hi(act, u + 2)
                gelu(EARLY, 0, u, 0)
                split_hi(act, u + 3)
                split_hi(act, u + 4)
                with act.Fori(0, TRIPS) as i:
                    for b in range(TILES_LOOP):
                        n, c = EARLY + 1 + b, u + 3 + 2 * b
                        gelu(n, i, c - 2, 2 * i)
                        split_hi(act, c + 2, 2 * i)
                        split_hi(act, c + 3, 2 * i)
                c = U_END[l] - 5
                for n in range(NKEYS - 3, NKEYS):
                    gelu(n, 0, c - 2, 0)
                    split_hi(act, c + 2)
                    if n < NKEYS - 1:
                        split_hi(act, c + 3)
                    c += 2
                norm_step(2 * l + 1)

            def attention():
                for u in range(U_KV, U_KV + 4):
                    split_hi(act, u + AHEAD)
                act.wait_ge(unit_done, U_KV + 4)
                act.activation(B.kv_row[:].rearrange("p b s f -> p b (s f)"), wk[:, 0:2, :],
                               ACT.Copy).then_inc(akv_read, 1)
                for g in range(2):
                    for k in range(4):
                        split_hi(act, U_WQ + 4 * g + k + AHEAD)
                    act.wait_ge(unit_done, U_WQ + 4 * g + 4)
                    act.activation(B.q_row[:, :, g * 512:(g + 1) * 512],
                                   wk[:, 2 - 2 * g:4 - 2 * g, :], ACT.Copy).then_inc(aq_read, 1)
                for tb in range(TB):
                    for half in range(3):
                        g = 3 * tb + half
                        act.wait_ge(a_turned, g + 1)
                        dst = (B.aqT[:, 4 * half:4 * half + 4, tb * P:(tb + 1) * P] if half < 2
                               else B.k2T[:, :, tb * P:(tb + 1) * P])
                        act.activation(dst, wk[:, g % 4, :].rearrange("p (b t) -> p b t", b=4),
                                       ACT.Copy).then_inc(a_turn_read, 1)
                for n in range(TB * KVH):
                    tb, kv = divmod(n, KVH)
                    first = 0 if tb else P
                    act.wait_ge(shifted, n + 1)
                    if n >= 2:
                        act.wait_ge(p_turned, n - 1)
                    for j in range(GRP):
                        act.activation(B.prob[:, n % 2, j, first:], B.logit[:, n % 2, j, first:], ACT.Exp,
                                       bias=B.nmax[:, n % 2, j:j + 1],
                                       accum_out=B.rsum[:, n % 2, j:j + 1])
                    last = act.activation(B.sexp[:, n % 2, :], B.sexp[:, n % 2, :], ACT.Exp)
                    last.then_inc(probs, 1)
                turn_step(3)
                for u in range(U_O1, U_O1 + DC):
                    split_hi(act, u + AHEAD)
                norm_step(2)
                turn_step(4)

            hgrn()
            if stages > 1:
                peer(0)
            if stages > 2:
                turn_step(2)
                attention()
            if stages > 3:
                peer(1)

        @block.vector
        def _(dve):
            own = Chain(dve, dve_own)

            def turn_step(n):
                for g in range(4):
                    tb, half = divmod(g, 2)
                    t = slice(tb * P, (tb + 1) * P)
                    dve.wait_ge(turn_hi, 4 * n + g + 1)
                    dve.tensor_tensor(hT_lo[:, 4 * half:4 * half + 4, t],
                                      wk[:, g, :].rearrange("p (b t) -> p b t", b=4),
                                      hT_hi[:, 4 * half:4 * half + 4, t].bitcast(F32),
                                      ALU.subtract).then_inc(turn_lo, 1)

            def layer_norm(k, u_last):
                dve.wait_ge(unit_done, u_last + 1)
                for tb in range(TB):
                    dve.bn_stats(stats[:, tb, 0, :], acc[:, tb, 0:512])
                    own(dve.bn_stats(stats[:, tb, 1, :], acc[:, tb, 512:1024]))
                    own(dve.bn_aggr(mean_var[:, tb, :], stats[:, tb].rearrange("p a b -> p (a b)")))
                own(dve.tensor_scalar(rinv[:], mean_var[:, :, 1], LN_EPS, None, ALU.add))
                dve.reciprocal(rinv[:], rinv[:]).then_inc(var_ready, 1)
                dve.wait_ge(rstd_ready, k + 1)
                for tb in range(TB):
                    own(dve.tensor_scalar(h_row[:, tb, :], acc[:, tb, :], mean_var[:, tb, 0:1],
                                          rstd[:, tb:tb + 1], ALU.subtract, ALU.mult))
                    if tb == 0:
                        dve.wait_ge(par_in, 32 * (k + 1))
                    own(dve.tensor_tensor(h_row[:, tb, :], h_row[:, tb, :], ln_par[:, 0, :], ALU.mult))
                    dve.tensor_tensor(h_row[:, tb, :], h_row[:, tb, :], ln_par[:, 1, :],
                                      ALU.add).then_inc(row_ready, 1)

            def hgrn():
                dve.wait_ge(consts, 1)
                split_lo(dve, 0)
                xt_raw = B.o_row[:].rearrange("p a b -> p (a b)")
                dve.wait_ge(xT_hi_ready, 1)
                dve.tensor_tensor(hT_lo[:].rearrange("p c t -> p (c t)"), xt_raw,
                                  hT_hi[:].rearrange("p c t -> p (c t)").bitcast(F32),
                                  ALU.subtract).then_inc(xT_ready, 1)
                split_lo(dve, 1)
                dve.wait_ge(alpha_hi_ready, 1)
                dve.scalar_tensor_tensor(alpha_lo[:], ident[:], ALPHA, alpha_hi[:].bitcast(F32), ALU.mult,
                                         ALU.subtract).then_inc(alpha_ready, 1)
                dve.wait_ge(small_in, 48)
                own(dve.tensor_tensor(B.lb_m[:], B.lb_t[:, 0, :], B.lb_t[:, 1, :], ALU.max))
                dve.tensor_tensor(B.lb_t[:], B.lb_t[:], B.lb_m[:].unsqueeze(1).broadcast_to([P, 2, HEADS]),
                                  ALU.subtract).then_inc(lb_shift, 1)
                dve.tensor_copy(iota_b[:], iota[:].unsqueeze(2).broadcast_to([P, NKEYS, OH]))
                own(dve.tensor_copy(B.pos_f[:], B.pos_i[:]))
                for tb in range(TB):
                    last = dve.tensor_scalar(B.ang[:, tb, :], B.freq[:], B.pos_f[:, tb:tb + 1], None,
                                             ALU.mult)
                own(last)
                for n, (quarter, dst) in enumerate(((0.0, B.red), (0.25, B.ang))):
                    own(dve.tensor_scalar(B.rnd[:], B.ang[:], 1.0 / TWO_PI, quarter, ALU.mult, ALU.add))
                    own(dve.tensor_scalar(B.rnd[:], B.rnd[:], ROUND, None, ALU.add))
                    own(dve.tensor_scalar(B.rnd[:], B.rnd[:], ROUND, None, ALU.subtract))
                    own(dve.scalar_tensor_tensor(dst[:], B.rnd[:], -C1, B.ang[:], ALU.mult, ALU.add))
                    own(dve.scalar_tensor_tensor(dst[:], B.rnd[:], -C2, dst[:], ALU.mult, ALU.add))
                    own(dve.scalar_tensor_tensor(dst[:], B.rnd[:], -C3, dst[:], ALU.mult, ALU.add))
                    own(dve.tensor_scalar(dst[:], dst[:], quarter * TWO_PI, PI_IN, ALU.add, ALU.min))
                    dve.tensor_scalar(dst[:], dst[:], -PI_IN, None, ALU.max).then_inc(angles, 1)
                dve.wait_ge(lb_exp, 1)
                own(dve.tensor_tensor(B.lb_m[:], B.lb_t[:, 0, :], B.lb_t[:, 1, :], ALU.add))
                own(dve.reciprocal(B.lb_m[:], B.lb_m[:]))
                dve.tensor_tensor(B.lb_1[:], B.lb_t[:, 1, :], B.lb_m[:], ALU.mult)
                own(dve.tensor_tensor(B.lb_f[:], B.lb_t[:, 0, :], B.lb_m[:], ALU.mult))
                with dve.Fori(0, 2) as i:
                    for c in range(4):
                        split_lo(dve, U_F + c + AHEAD, i)
                with dve.Fori(0, 2) as i:
                    own.enter(i, 4)
                    for c in range(4):
                        split_lo(dve, U_Q + c + AHEAD, i)
                        dve.wait_ge(proj_read, U_F + c + 1 + 4 * i)
                        f = B.fT[:, bass.ds(4 * i + c, 1), :].rearrange("p o t -> p (o t)")
                        k = B.kT[:, bass.ds(4 * i + c, 1), :].rearrange("p o t -> p (o t)")
                        own(dve.tensor_scalar(f, f, B.lb_1[:, bass.ds(4 * i + c, 1)],
                                              B.lb_f[:, bass.ds(4 * i + c, 1)], ALU.mult, ALU.add))
                        dve.tensor_scalar(k, f, -1.0, 1.0, ALU.mult, ALU.add)
                    own.leave(2)
                for h in range(HEADS):
                    split_lo(dve, U_I + h + AHEAD)
                    f, k, dec, q, kl = (t[:, h, :] for t in (B.fT, B.kT, B.decT, B.qT, B.klT))

                    def chunks(ap):
                        return ap.rearrange("p (n s) -> p n s", s=CHUNK)

                    own(dve.tensor_tensor(chunks(B.first[:]), chunks(f),
                                          B.mask_first[:].unsqueeze(1).broadcast_to([P, NCH, CHUNK]),
                                          ALU.mult))
                    own(dve.tensor_tensor_scan(dec, f, B.first[:], 0.0, ALU.mult, ALU.max))
                    own(dve.reciprocal(B.tmp[:], dec))
                    own(dve.tensor_tensor(k, k, B.tmp[:], ALU.mult))
                    dve.wait_ge(proj_read, DC + h + 1)
                    end = chunks(dec)[:, :, CHUNK - 1:CHUNK].broadcast_to([P, NCH, CHUNK])
                    dve.tensor_tensor(chunks(kl), chunks(k), end, ALU.mult)
                    dve.tensor_tensor(q, q, dec, ALU.mult).then_inc(decays, 1)
                for u in range(U_G, U_G + DC):
                    split_lo(dve, u + AHEAD)
                dve.wait_ge(norm_in, 16)
                dve.wait_ge(row_read, 4)
                for tb in range(TB):
                    dve.tensor_tensor(B.g_row[:, tb, :], B.g_row[:, tb, :], B.norm_t[:], ALU.mult)
                for g in range(4):
                    tb, half = divmod(g, 2)
                    dve.wait_ge(att_raw, g + 1)
                    part = slice(half * 512, (half + 1) * 512)
                    dve.copy_predicated(
                        B.att[:, tb, part].rearrange("p (h t) -> p h t", h=4),
                        B.mask_att[:].unsqueeze(1).broadcast_to([P, 4, P]),
                        acc[:, tb, part].rearrange("p (h t) -> p h t", h=4)).then_inc(att_ready, 1)
                for c in range(NCH - 1):
                    dve.wait_ge(delta, c + 1)
                    new = wk[:, 2 * (c % 2):2 * (c % 2) + 2, :].rearrange("p a b -> p (a b)")
                    if c == 0:
                        dve.tensor_copy(B.state[:, 1, :], new).then_inc(state_ready, 1)
                        continue
                    dve.wait_ge(state_ready, c)
                    for h in range(HEADS):
                        f = slice(h * P, (h + 1) * P)
                        last = dve.scalar_tensor_tensor(
                            B.state[:, c + 1, f], B.state[:, c, f],
                            B.decT[:, h, (c + 1) * CHUNK - 1:(c + 1) * CHUNK], new[:, f], ALU.mult, ALU.add)
                    last.then_inc(state_ready, 1)
                sq = B.klT[:].rearrange("p h t -> p (h t)")[:, 0:D]
                for tb in range(TB):
                    dve.wait_ge(o_copied, tb + 1)
                    own(dve.tensor_tensor(sq, B.o_row[:, tb, :], B.o_row[:, tb, :], ALU.mult))
                    own(dve.tensor_reduce(B.ssq[:, tb, :], sq.rearrange("p (h e) -> p h e", h=HEADS), AX,
                                          ALU.add))
                    own(dve.tensor_scalar(B.ssq[:, tb, :], B.ssq[:, tb, :], 1.0 / P, RMS_EPS, ALU.mult,
                                          ALU.add))
                    dve.reciprocal(B.ssq[:, tb, :], B.ssq[:, tb, :]).then_inc(o_sq, 1)
                    dve.wait_ge(o_rms, tb + 1)
                    for h in range(HEADS):
                        f = slice(h * P, (h + 1) * P)
                        last = dve.scalar_tensor_tensor(B.o_row[:, tb, f], B.o_row[:, tb, f],
                                                        B.ssq[:, tb, h:h + 1], B.g_row[:, tb, f],
                                                        ALU.mult, ALU.mult)
                    last.then_inc(row_ready, 1)
                turn_step(0)
                for u in range(U_O0, U_O0 + DC):
                    split_lo(dve, u + AHEAD)
                layer_norm(0, U_O0 + DC - 1)
                turn_step(1)

            def peer(l):
                def top_step(c):
                    dve.wait_ge(sc_copied, NHC * l + c + 1)
                    s = B.sc[:, c % 2]
                    v, ix = B.val[:, :, c, :], B.idx_u[:, :, c, :]
                    for tb in range(TB):
                        last = dve.max(v[:, tb, 0:8], s[:, tb, :])
                    own(last)
                    for tb in range(TB):
                        dve.max_index(ix[:, tb, 0:8], v[:, tb, 0:8], s[:, tb, :])
                        last = dve.match_replace(B.sc_cut[:, tb, :], v[:, tb, 0:8], s[:, tb, :], LOWEST)
                    last.then_inc(sc_done, 1)
                    dve.wait_ge(sc_done, NHC * l + c + 1)
                    for tb in range(TB):
                        last = dve.max(v[:, tb, 8:16], B.sc_cut[:, tb, :])
                    own(last)
                    for tb in range(TB):
                        last = dve.max_index(ix[:, tb, 8:16], v[:, tb, 8:16], B.sc_cut[:, tb, :])
                    own(last)

                for c in range(NHC):
                    top_step(c)
                own(dve.tensor_copy(B.idx[:], B.idx_u[:]))

                for tb in range(TB):
                    v4 = B.val[:, tb].rearrange("p (h c) k -> p h c k", c=2)
                    for h in range(HEADS):
                        last = dve.tensor_tensor(
                            B.cand[:, h, :].rearrange("p (a b) -> p a b", a=TOPK),
                            v4[:, h, 0, :].unsqueeze(2).broadcast_to([P, TOPK, TOPK]),
                            v4[:, h, 1, :].unsqueeze(1).broadcast_to([P, TOPK, TOPK]), ALU.add)
                    own(last)
                    for h in range(HEADS):
                        last = dve.max(B.top_s[:, tb, h, 0:8], B.cand[:, h, :])
                    own(last)
                    for h in range(HEADS):
                        dve.max_index(B.top_j[:, tb, h, 0:8], B.top_s[:, tb, h, 0:8], B.cand[:, h, :])
                        last = dve.match_replace(B.cand_cut[:, h, :], B.top_s[:, tb, h, 0:8],
                                                 B.cand[:, h, :], LOWEST)
                    own(last)
                    for h in range(HEADS):
                        last = dve.max(B.top_s[:, tb, h, 8:16], B.cand_cut[:, h, :])
                    own(last)
                    for h in range(HEADS):
                        last = dve.max_index(B.top_j[:, tb, h, 8:16], B.top_s[:, tb, h, 8:16],
                                             B.cand_cut[:, h, :])
                    own(last)
                    dve.tensor_tensor(B.gate[:, tb], B.top_s[:, tb],
                                      B.top_s[:, tb, :, 0:1].broadcast_to([P, HEADS, TOPK]),
                                      ALU.subtract).then_inc(gate_in, 1)
                    j = B.top_j[:, tb].rearrange("p h k -> p (h k)")
                    dve.tensor_scalar(B.j_int[:, 0, :], j, 4, None, ALU.logical_shift_right)
                    own(dve.tensor_scalar(B.j_int[:, 1, :], j, 15, None, ALU.bitwise_and))
                    own(dve.tensor_copy(B.j_f[:], B.j_int[:]))
                    i4 = B.idx[:, tb].rearrange("p (h c) k -> p h c k", c=2)
                    for c in range(2):
                        own(dve.tensor_tensor(
                            B.pick[:], iota[:, 0:TOPK].unsqueeze(1).broadcast_to([P, HEADS * TOPK, TOPK]),
                            B.j_f[:, c, :].unsqueeze(2).broadcast_to([P, HEADS * TOPK, TOPK]),
                            ALU.is_equal))
                        own(dve.tensor_tensor(
                            B.picked[:].rearrange("p (h k) a -> p h k a", h=HEADS),
                            B.pick[:].rearrange("p (h k) a -> p h k a", h=HEADS),
                            i4[:, :, c, :].unsqueeze(2).broadcast_to([P, HEADS, TOPK, TOPK]), ALU.mult))
                        own(dve.tensor_reduce(B.key_sel[:, tb, c, :], B.picked[:], AX, ALU.add))
                for tb in range(TB):
                    dve.wait_ge(gate_exp, TB * l + tb + 1)
                    own(dve.tensor_reduce(B.gsum[:, tb, :], B.gate[:, tb], AX, ALU.add))
                    own(dve.reciprocal(B.gsum[:, tb, :], B.gsum[:, tb, :]))
                    dve.tensor_tensor(B.gate[:, tb], B.gate[:, tb],
                                      B.gsum[:, tb, :].unsqueeze(2).broadcast_to([P, HEADS, TOPK]),
                                      ALU.mult).then_inc(choice_ready, 1)

                dve.wait_ge(choice_read, TB * (l + 1))

                def weigh_early(c, i):
                    dve.wait_ge(gate_read, 4 * GATE_TRIPS * l + 2 * c + 2 + 4 * i)
                    t = bass.ds(4 * QT * i + 2 * QT * c, 2 * QT)
                    acts = B.gates[:, 0:EARLY, t]
                    dve.tensor_tensor(
                        acts, acts, wk[:, 2 * c:2 * c + 2, :].rearrange("p b (t k) -> p k (b t)", t=QT)[
                            :, 0:EARLY, :], ALU.mult).then_inc(early_weighed, 1)

                def onehot_step(c, i):
                    n = 4 * GATE_TRIPS * l + 2 * c
                    later = l > 0 or type(i) is not int
                    if later:
                        dve.wait_ge(weighted_pool, 3 * GATE_TRIPS * l - 1 + c + 3 * i)
                        if c == 1:
                            dve.wait_ge(weighted_act, GATE_TRIPS * l + i)
                    t = bass.ds(4 * QT * i + OH * c, OH)
                    dve.tensor_tensor(onehot1[:, c], iota_b[:],
                                      key1T[:, t].unsqueeze(1).broadcast_to([P, NKEYS, OH]),
                                      ALU.is_equal).then_inc(onehot1_ready, 1)
                    if later:
                        dve.wait_ge(gate_mm, n - 2 + 4 * i)
                    dve.tensor_tensor(onehot2[:, c], iota[:].unsqueeze(1).broadcast_to([P, OH, NKEYS]),
                                      key2T[:, t].unsqueeze(2).broadcast_to([P, OH, NKEYS]),
                                      ALU.is_equal).then_inc(onehot2_ready, 1)
                    if type(i) is not int:
                        weigh_early(c, i - 1)

                for c in range(2):
                    onehot_step(c, 0)
                with dve.Fori(1, GATE_TRIPS) as i:
                    for c in range(2):
                        onehot_step(c, i)
                for c in range(2):
                    weigh_early(c, GATE_TRIPS - 1)

                def weigh(n, i):
                    dve.wait_ge(act_ready, NKEYS * l + n + 1 + 4 * i)
                    dve.wait_ge(w_ready, NKEYS * l + n + 4 * i)
                    at = bass.ds(n + 4 * i, 1)
                    g = B.gates[:, at, :].rearrange("p o t -> p (o t)")
                    dve.tensor_tensor(w_full[:], gelu_a[:, n % 2, :], g, ALU.mult)
                    own(dve.tensor_tensor(w_hi[:, n % 2, :], gelu_a[:, n % 2, :], g, ALU.mult))
                    dve.tensor_tensor(w_lo[:, n % 2, :], w_full[:], w_hi[:, n % 2, :].bitcast(F32),
                                      ALU.subtract).then_inc(w_ready, 1)

                dve.wait_ge(lo_ready, U_DOWN[l] + AHEAD)
                with dve.Fori(0, EARLY // 4) as i:
                    for c in range(4):
                        dve.wait_ge(w_hi_ready, EARLY * l + c + 1 + 4 * i)
                        dve.tensor_tensor(w_lo[:, c % 2, :], B.gates[:, bass.ds(4 * i + c, 1), :].rearrange(
                            "p o t -> p (o t)"), w_hi[:, c % 2, :].bitcast(F32), ALU.subtract).then_inc(
                            w_ready, 1)
                        split_lo(dve, U_DOWN[l] + c + AHEAD, i)
                u = U_REST[l]
                split_lo(dve, u + 2)
                dve.wait_ge(unit_done, U_DOWN[l] + EARLY - 1)
                weigh(EARLY, 0)
                split_lo(dve, u + 3)
                split_lo(dve, u + 4)
                with dve.Fori(0, TRIPS) as i:
                    own.enter(i, TILES_LOOP)
                    for b in range(TILES_LOOP):
                        n, c = EARLY + 1 + b, u + 3 + 2 * b
                        dve.wait_ge(unit_done, c - 2 + 8 * i)
                        weigh(n, i)
                        split_lo(dve, c + 2, 2 * i)
                        split_lo(dve, c + 3, 2 * i)
                    own.leave(TRIPS)
                c = U_END[l] - 5
                for n in range(NKEYS - 3, NKEYS):
                    dve.wait_ge(unit_done, c - 2)
                    weigh(n, 0)
                    split_lo(dve, c + 2)
                    if n < NKEYS - 1:
                        split_lo(dve, c + 3)
                    c += 2
                layer_norm(2 * l + 1, U_END[l] - 1)

            def attention():
                for u in range(U_KV, U_KV + 4):
                    split_lo(dve, u + AHEAD)
                for u in range(U_WQ, U_WQ + 8):
                    split_lo(dve, u + AHEAD)

                def rope(v):
                    n = v.shape[1]
                    c = cos_t[:, tb].unsqueeze(1).broadcast_to([P, n, HALF])
                    s = sin_t[:, tb].unsqueeze(1).broadcast_to([P, n, HALF])
                    a, b = v[:, :, 0:HALF], v[:, :, HALF:ROPE]
                    dve.tensor_tensor(B.rt[:, 0, 0:n, :], a, c, ALU.mult)
                    dve.tensor_tensor(B.rt[:, 1, 0:n, :], b, s, ALU.mult)
                    dve.tensor_tensor(B.rt[:, 2, 0:n, :], b, c, ALU.mult)
                    own(dve.tensor_tensor(B.rt[:, 3, 0:n, :], a, s, ALU.mult))
                    dve.tensor_tensor(a, B.rt[:, 0, 0:n, :], B.rt[:, 1, 0:n, :], ALU.subtract)
                    return dve.tensor_tensor(b, B.rt[:, 2, 0:n, :], B.rt[:, 3, 0:n, :], ALU.add)

                dve.wait_ge(tables, 2)
                dve.wait_ge(akv_read, 1)
                for tb in range(TB):
                    if tb:
                        dve.wait_ge(roped, tb)
                    k = B.kv_row[:, tb, 0, :].rearrange("p (h d) -> p h d", h=KVH)
                    own(rope(k))
                    for r in range(2):
                        dve.tensor_copy(B.k2_row[:, tb, :, r, :], k)
                    if tb == 0:
                        dve.wait_ge(aq_read, 2)
                    rope(B.q_row[:, tb, :].rearrange("p (h d) -> p h d", h=QH)).then_inc(roped, 1)

                def normalize(n):
                    tb, kv = divmod(n, KVH)
                    dve.wait_ge(a_out, n + 1)
                    dve.tensor_tensor(
                        B.ao_row[:, tb, kv * GRP * HD:(kv + 1) * GRP * HD].rearrange(
                            "p (a b d) -> p a b d", a=2, b=2),
                        acc[:, 1, (n % 2) * 512:(n % 2) * 512 + GRP * HD].rearrange(
                            "p (a b d) -> p a b d", a=2, b=2),
                        B.rnorm[:, n % 2, :].rearrange("p (b a) -> p a b", b=2).unsqueeze(3).broadcast_to(
                            [P, 2, 2, HD]), ALU.mult).then_inc(a_norm, 1)

                dve.wait_ge(consts, 2)
                for n in range(TB * KVH + 1):
                    if n < TB * KVH:
                        tb, kv = divmod(n, KVH)
                        s, first = n % 2, (0 if tb else P)
                        dve.wait_ge(logits, n + 1)
                        if n >= 2:
                            dve.wait_ge(probs, n - 1)
                        lg = B.logit[:, s, :, first:]
                        own(dve.scalar_tensor_tensor(
                            lg, acc[:, 0, :].rearrange("p (g k) -> p g k", g=GRP)[:, :, first:], HD ** -0.5,
                            B.bias_att[:, first:].unsqueeze(1).broadcast_to([P, GRP, 2 * P - first]),
                            ALU.mult, ALU.add))
                        own(dve.tensor_reduce(B.rmax[:, s, :], lg, AX, ALU.max))
                        sink = sink_t[:, GRP * kv:GRP * (kv + 1)].rearrange("p (a b) -> p b a", a=2)
                        m22 = B.rmax[:, s, :].rearrange("p (b a) -> p b a", b=2)
                        own(dve.tensor_tensor(m22, m22, sink, ALU.max))
                        dve.tensor_tensor(B.sexp[:, s, :].rearrange("p (b a) -> p b a", b=2), sink, m22,
                                          ALU.subtract)
                        dve.tensor_scalar(B.nmax[:, s, :], B.rmax[:, s, :], -1.0, None,
                                          ALU.mult).then_inc(shifted, 1)
                    if n >= 1:
                        m = n - 1
                        tb, kv = divmod(m, KVH)
                        dve.wait_ge(p_turned, m + 1)
                        if m >= 2:
                            dve.wait_ge(a_out, m - 1)
                        w = wk[:, 2 * (m % 2):2 * (m % 2) + 2, :].rearrange(
                            "p a (g r t) -> p (a g) r t", g=2, r=2)
                        if tb:
                            dve.tensor_copy(B.probT[:, m % 2], w).then_inc(p_read, 1)
                        else:
                            dve.tensor_copy(B.probT[:, m % 2, :, 1, :], w[:, :, 1, :]).then_inc(p_read, 1)
                        own(dve.tensor_tensor(B.rnorm[:, m % 2, :], B.rsum[:, m % 2, :],
                                              B.sexp[:, m % 2, :], ALU.add))
                        own(dve.reciprocal(B.rnorm[:, m % 2, :], B.rnorm[:, m % 2, :]))
                        normalize(m)
                turn_step(3)
                for u in range(U_O1, U_O1 + DC):
                    split_lo(dve, u + AHEAD)
                layer_norm(2, U_O1 + DC - 1)
                turn_step(4)

            hgrn()
            if stages > 1:
                peer(0)
            if stages > 2:
                turn_step(2)
                attention()
            if stages > 3:
                peer(1)


def col_blocks(w):
    return w.reshape(DC, P, -1, P).transpose(2, 1, 0, 3).reshape(-1, P, UNIT)


def row_blocks(w):
    return w.reshape(DC // 2, 2, P, -1, 512).transpose(3, 0, 2, 1, 4).reshape(-1, P, UNIT)


def peer_units(w_q, u_tab, v_tab):
    up = u_tab.reshape(NKEYS, P, DC, P).transpose(0, 3, 2, 1).reshape(NKEYS, P, UNIT)
    down = v_tab.reshape(NKEYS, P, D)
    rest = np.empty((2 * (NKEYS - EARLY), P, UNIT), up.dtype)
    rest[0] = up[EARLY]
    rest[1:-1:2] = up[EARLY + 1:]
    rest[2::2] = down[EARLY:-1]
    rest[-1] = down[-1]
    return [col_blocks(w_q), up[:EARLY], down[:EARLY], rest]


def kernel(x, positions, hg_w_in, hg_lb, hg_norm_w, hg_w_o, sw_w_q, sw_sinks, sw_w_o, w_kv, peer_w_q,
           peer_sub_keys, peer_u, peer_v, ln_mix_g, ln_mix_b, ln_ffn_g, ln_ffn_b):
    import concourse.bacc as bacc
    from concourse.bass_utils import run_bass_kernel_spmd

    w_in = hg_w_in[0]
    stream = np.concatenate(
        [col_blocks(w_in[:, D:2 * D]), col_blocks(w_in[:, 0:D]), row_blocks(w_in[:, 2 * D:]),
         row_blocks(hg_w_o[0])]
        + peer_units(peer_w_q[0], peer_u[0], peer_v[0])
        + [row_blocks(w_kv), row_blocks(sw_w_q[0]), row_blocks(sw_w_o[0])]
        + peer_units(peer_w_q[1], peer_u[1], peer_v[1]))
    assert stream.shape == (N_UNITS, P, UNIT)
    arrays = {
        "xT": x.reshape(SEQ, DC, P).transpose(2, 1, 0).reshape(P, DC * SEQ),
        "positions": positions.reshape(TB, P).transpose(1, 0),
        "stream": stream,
        "keys": peer_sub_keys.reshape(DEPTH, NHC, NKEYS, P).transpose(0, 3, 1, 2),
        "lb": hg_lb.reshape(2, HEADS, P).transpose(2, 0, 1),
        "norm_w": hg_norm_w.reshape(D),
        "sinks": sw_sinks.reshape(QH),
        "ln": np.stack([np.stack([g[l], b[l]]) for l in range(DEPTH)
                        for g, b in ((ln_mix_g, ln_mix_b), (ln_ffn_g, ln_ffn_b))]),
    }
    nc = bacc.Bacc("TRN2", target_bir_lowering=False, num_devices=1)
    arrays = {f"{k}_dram": np.ascontiguousarray(a) for k, a in arrays.items()}
    args = [nc.dram_tensor(k, a.shape, mybir.dt.from_np(a.dtype), kind="ExternalInput").ap()
            for k, a in arrays.items()]
    out = nc.dram_tensor("out_dram", (P, TB, D), F32, kind="ExternalOutput").ap()
    build(nc, *args, out)
    r = run_bass_kernel_spmd(nc, [arrays], core_ids=[0])
    return np.asarray(r.results[0]["out_dram"]).transpose(1, 0, 2).reshape(1, SEQ, D)
```

```python
from contextlib import ExitStack

import numpy as np

import concourse.bass as bass
from concourse import mybir

F32 = mybir.dt.float32
F32R = mybir.dt.float32r
BF16 = mybir.dt.bfloat16
I32 = mybir.dt.int32
U32 = mybir.dt.uint32
ALU = mybir.AluOpType
ACT = mybir.ActivationFunctionType
AX = mybir.AxisListType.X

P = 128
D = 1024
SEQ = 256
TB = SEQ // P
DC = D // P
HEADS = 8
CHUNK = 32
NCH = SEQ // CHUNK
CPB = P // CHUNK
QH = 16
KVH = 4
GRP = QH // KVH
HD = D // QH
ROPE = HD // 4
HALF = ROPE // 2
THETA = 500000.0
TOPK = 16
NKEYS = 128
NHC = 2 * HEADS
DEPTH = 2
ALPHA = (2.0 * DEPTH) ** 0.25
LN_EPS = 1e-5
RMS_EPS = 1e-6
LOWEST = -3.0e38
TWO_PI = 6.283185307179586
C1 = 6.28125
C2 = 0.0019350051879882812
C3 = TWO_PI - C1 - C2
PI_IN = 3.1415925
ROUND = 12582912.0

UNIT = 1024
RAW = 4
RING = 4
AHEAD = 2
U_F = 0
U_Q = U_F + DC
U_I = U_Q + DC
U_G = U_I + DC
U_O0 = U_G + DC
U_PQ0 = U_O0 + DC
U_EARLY0 = U_PQ0 + NHC
U_KV = U_EARLY0 + 2 * NKEYS
U_WQ = U_KV + DC // 2
U_O1 = U_WQ + DC
U_PQ1 = U_O1 + DC
U_EARLY1 = U_PQ1 + NHC
N_UNITS = U_EARLY1 + 2 * NKEYS
EARLY = 24
EARLY_EXP = 4
TILES_LOOP = 4
TRIPS = (NKEYS - EARLY - 4) // TILES_LOOP
U_PQ = (U_PQ0, U_PQ1)
U_EARLY = (U_EARLY0, U_EARLY1)
U_DOWN = tuple(u + EARLY for u in U_EARLY)
U_REST = tuple(u + 2 * EARLY for u in U_EARLY)
U_END = tuple(u + 2 * NKEYS for u in U_EARLY)
OH = 8
QT = 512 // NKEYS
GATE_TRIPS = SEQ // (4 * QT)


STOP_UNITS = {1: U_PQ0 + 4, 2: U_KV + 4, 3: U_PQ1 + 4}


def head_at(j):
    return 2 * (j % 2) + j // 2


class Chain:

    def __init__(self, eng, sem):
        self.eng, self.sem, self.n, self.more = eng, sem, 0, 0

    def __call__(self, ins):
        self.n += 1
        ins.then_inc(self.sem, 1)
        self.eng.wait_ge(self.sem, self.n + self.more)

    def enter(self, i, per_trip):
        self.start, self.per_trip, self.more = self.n, per_trip, i * per_trip

    def leave(self, trips):
        assert self.n - self.start == self.per_trip, (self.n - self.start, self.per_trip)
        self.n, self.more = self.start + self.per_trip * trips, 0


def build(nc, xT, positions, stream, keys, lb, norm_w, sinks, ln, out, stages=99):
    with ExitStack() as ctx:
        def sb(name, shape, dt=F32):
            return ctx.enter_context(nc.sbuf_tensor(name, shape, dt))

        def sem(name):
            return ctx.enter_context(nc.semaphore(name))

        raw = sb("raw", [P, RAW, UNIT])
        hT_hi = sb("hT_hi", [P, DC, SEQ], F32R)
        hT_lo = sb("hT_lo", [P, DC, SEQ], F32R)
        gateT = sb("gateT", [P, SEQ])
        key1T = sb("key1T", [P, SEQ], BF16)
        iota_b = sb("iota_b", [P, NKEYS, OH], BF16)
        key2T = sb("key2T", [P, SEQ])
        ident = sb("ident", [P, P])
        iota = sb("iota", [P, P])
        ident_pad = sb("ident_pad", [P, 3, P], F32R)
        cos_t = sb("cos_t", [P, TB, HALF])
        sin_t = sb("sin_t", [P, TB, HALF])
        sink_t = sb("sink_t", [P, QH])
        stats = sb("stats", [P, TB, 2, 6])
        mean_var = sb("mean_var", [P, TB, 2])
        rstd = sb("rstd", [P, TB])
        rinv = sb("rinv", [P, TB])
        var_eps = sb("var_eps", [P, TB])

        def overlaid(*groups):
            sizes = []
            keep = {}
            for g in groups:
                inner = ExitStack()
                for name, shape, dt in g:
                    keep[name] = inner.enter_context(nc.sbuf_tensor(name, shape, dt))
                sizes.append(sum(int(np.prod(s[1:])) * (2 if dt == BF16 else 4) for _, s, dt in g))
                inner.close()
            ctx.enter_context(nc.sbuf_tensor(f"room_{groups[0][0][0]}", [P, max(sizes) // 4], F32))
            return keep

        front = [P, RING - 2, UNIT]
        his = overlaid([("hi", [P, RING, UNIT], F32R)],
                       [("hi_front", front, F32), ("onehot2", [P, 2, OH, NKEYS], F32)])
        los = overlaid([("lo", [P, RING, UNIT], F32R)],
                       [("lo_front", front, F32), ("weighted", [P, 4, QT, NKEYS], F32)])
        hi, lo, onehot2, weighted = his["hi"], los["lo"], his["onehot2"], los["weighted"]

        small = overlaid(
            [("onehot1", [P, 2, NKEYS, OH], BF16)],
            [("gelu_a", [P, 2, SEQ], F32), ("w_full", [P, SEQ], F32), ("w_hi", [P, 2, SEQ], F32R),
             ("w_lo", [P, 2, SEQ], F32R)],
        )
        onehot1, gelu_a = small["onehot1"], small["gelu_a"]
        w_full, w_hi, w_lo = small["w_full"], small["w_hi"], small["w_lo"]

        big = overlaid(
            [("gates", [P, NKEYS, SEQ], F32)],
            [("fT", [P, HEADS, SEQ], F32), ("kT", [P, HEADS, SEQ], F32), ("decT", [P, HEADS, SEQ], F32),
             ("qT", [P, HEADS, SEQ], F32), ("klT", [P, HEADS, SEQ], F32), ("kl_row", [P, TB, D], F32),
             ("v_row", [P, TB, D], F32), ("g_row", [P, TB, D], F32), ("o_row", [P, TB, D], F32),
             ("state", [P, NCH, D], F32), ("att", [P, TB, D], F32), ("norm_t", [P, D], F32),
             ("first", [P, SEQ], F32), ("tmp", [P, SEQ], F32), ("mask_att", [P, P], I32),
             ("mask_first", [P, CHUNK], F32), ("lb_t", [P, 2, HEADS], F32), ("lb_m", [P, HEADS], F32),
             ("lb_f", [P, HEADS], F32), ("lb_1", [P, HEADS], F32), ("ssq", [P, TB, HEADS], F32),
             ("pos_i", [P, TB], I32), ("pos_f", [P, TB], F32), ("freq", [P, HALF], F32),
             ("ang", [P, TB, HALF], F32), ("rnd", [P, TB, HALF], F32), ("red", [P, TB, HALF], F32),
             ("ones_f", [P, P], F32)],
            [("h_row", [P, TB, D], F32), ("ln_par", [P, 2, D], F32),
             ("act_room", [P, EARLY * SEQ - 2 * TB * D], F32),
             ("keys_t", [P, NHC, NKEYS], F32), ("q_t", [P, 2, SEQ], F32),
             ("sc", [P, 2, TB, NKEYS], F32), ("sc_cut", [P, TB, NKEYS], F32),
             ("idx_u", [P, TB, NHC, TOPK], U32),
             ("val", [P, TB, NHC, TOPK], F32), ("idx", [P, TB, NHC, TOPK], F32),
             ("cand", [P, HEADS, TOPK * TOPK], F32), ("cand_cut", [P, HEADS, TOPK * TOPK], F32),
             ("top_s", [P, TB, HEADS, TOPK], F32), ("top_j", [P, TB, HEADS, TOPK], U32),
             ("j_int", [P, 2, HEADS * TOPK], U32), ("j_f", [P, 2, HEADS * TOPK], F32),
             ("pick", [P, HEADS * TOPK, TOPK], F32), ("picked", [P, HEADS * TOPK, TOPK], F32),
             ("key_sel", [P, TB, 2, HEADS * TOPK], F32), ("gate", [P, TB, HEADS, TOPK], F32),
             ("gsum", [P, TB, HEADS], F32)],
            [("h_room", [P, TB, D], F32), ("q_row", [P, TB, D], F32), ("kv_row", [P, TB, 2, KVH * HD], F32),
             ("k2_row", [P, TB, KVH, 2, HD], F32), ("aqT", [P, DC, SEQ], F32),
             ("k2T", [P, KVH, SEQ], F32), ("rt", [P, 4, QH, HALF], F32),
             ("logit", [P, 2, GRP, 2 * P], F32), ("prob", [P, 2, GRP, 2 * P], F32),
             ("probT", [P, 2, GRP, 2, P], F32), ("bias_att", [P, 2 * P], F32),
             ("rmax", [P, 2, GRP], F32), ("nmax", [P, 2, GRP], F32), ("rsum", [P, 3, GRP], F32),
             ("sexp", [P, 3, GRP], F32), ("rnorm", [P, 2, GRP], F32), ("ao_row", [P, TB, D], F32)],
        )
        B = type("Big", (), big)
        h_row, ln_par = B.h_row, B.ln_par

        acc = ctx.enter_context(nc.psum_tensor("acc", [P, TB, D], F32))
        wk = ctx.enter_context(nc.psum_tensor("wk", [P, 4, 512], F32))

        raw_in = [sem(f"raw_in{i}") for i in range(RAW)]
        hi_ready, lo_ready, unit_done = sem("hi_ready"), sem("lo_ready"), sem("unit_done")
        dve_own, act_own, pool_own = sem("dve_own"), sem("act_own"), sem("pool_own")
        xT_in = [sem(f"xT_in{k}") for k in range(4)]
        small_in, par_in, norm_in, keys_in = (
            sem("small_in"), sem("par_in"), sem("norm_in"), sem("keys_in"))
        consts = sem("consts")
        ident_ready = sem("ident_ready")
        xT_hi_ready, xT_ready = sem("xT_hi_ready"), sem("xT_ready")
        lb_shift, lb_exp = sem("lb_shift"), sem("lb_exp")
        angles, tables = sem("angles"), sem("tables")
        proj_read, row_read = sem("proj_read"), sem("row_read")
        decays = sem("decays")
        kl_turned, kl_read = sem("kl_turned"), sem("kl_read")
        att_raw, att_ready = sem("att_raw"), sem("att_ready")
        delta, state_ready = sem("delta"), sem("state_ready")
        o_sum, o_copied, o_sq, o_rms = sem("o_sum"), sem("o_copied"), sem("o_sq"), sem("o_rms")
        row_ready, turned, turn_hi, turn_lo = (
            sem("row_ready"), sem("turned"), sem("turn_hi"), sem("turn_lo"))
        sum_block0, var_ready, rstd_ready = sem("sum_block0"), sem("var_ready"), sem("rstd_ready")
        q_ready, sc_ready, sc_copied, sc_done = (
            sem("q_ready"), sem("sc_ready"), sem("sc_copied"), sem("sc_done"))
        gate_in, gate_exp, choice_ready, choice_turned, choice_read = (
            sem("gate_in"), sem("gate_exp"), sem("choice_ready"), sem("choice_turned"), sem("choice_read"))
        onehot1_ready, onehot2_ready = sem("onehot1_ready"), sem("onehot2_ready")
        weighted_pool, weighted_act = sem("weighted_pool"), sem("weighted_act")
        gate_mm, gate_read, early_weighed = sem("gate_mm"), sem("gate_read"), sem("early_weighed")
        w_hi_ready = sem("w_hi_ready")
        act_ready, w_ready, tile_done = sem("act_ready"), sem("w_ready"), sem("tile_done")
        aq_read, akv_read, roped, a_turned, a_turn_read = (
            sem("aq_read"), sem("akv_read"), sem("roped"), sem("a_turned"), sem("a_turn_read"))
        logits, shifted, probs, p_turned, p_read, a_out, a_norm = (
            sem("logits"), sem("shifted"), sem("probs"), sem("p_turned"), sem("p_read"), sem("a_out"),
            sem("a_norm"))
        stored = sem("stored")

        block = ctx.enter_context(nc.Block())

        def split_hi(act, c, i=0):
            if type(i) is int and c + RING * i >= N_UNITS:
                return
            act.wait_ge(raw_in[c % RAW], 16 * (c // RAW + 1) + 16 * i)
            if type(i) is not int or c >= RING:
                act.wait_ge(unit_done, c - RING + 1 + RING * i)
            act.activation(hi[:, c % RING, :], raw[:, c % RAW, :], ACT.Copy).then_inc(hi_ready, 1)

        def split_lo(eng, c, i=0):
            if type(i) is int and c + RING * i >= N_UNITS:
                return
            eng.wait_ge(hi_ready, c + 1 + RING * i)
            eng.tensor_tensor(lo[:, c % RING, :], raw[:, c % RAW, :], hi[:, c % RING, :].bitcast(F32),
                              ALU.subtract).then_inc(lo_ready, 1)

        @block.sync
        def _(sp):
            n_units = N_UNITS if stages > 90 else STOP_UNITS.get(stages, N_UNITS)
            for c in range(RING):
                sp.dma_start(raw[:, c % RAW, :], stream[c]).then_inc(raw_in[c % RAW], 16)
                if c == 0:
                    xt_raw = B.o_row[:].rearrange("p a b -> p (a b)").rearrange("p (c t) -> p c t", c=DC)
                    for k in range(4):
                        sp.dma_start(xt_raw[:, 2 * k:2 * k + 2, :], xT[:, 2 * k:2 * k + 2, :]).then_inc(
                            xT_in[k], 16)
            with sp.Fori(1, n_units // RING) as i:
                for c in range(RING):
                    sp.wait_ge(lo_ready, c - RAW + 1 + RING * i)
                    sp.dma_start(raw[:, c % RAW, :], stream[bass.ds(c + RING * i, 1)].rearrange(
                        "o p f -> (o p) f")).then_inc(raw_in[c % RAW], 16)
            sp.wait_ge(row_ready, {1: 4, 2: 6, 3: 8}.get(stages, 10))
            sp.dma_start(out, h_row[:]).then_inc(stored, 16)
            sp.wait_ge(stored, 16)

        @block.gpsimd
        def _(pool):
            own = Chain(pool, pool_own)
            pool.dma_start(B.lb_t[:], lb).then_inc(small_in, 16)
            pool.dma_start(B.pos_i[:], positions).then_inc(small_in, 16)
            pool.dma_start(sink_t[:], sinks.partition_broadcast(P)).then_inc(small_in, 16)
            pool.dma_start(B.norm_t[:], norm_w.partition_broadcast(P)).then_inc(norm_in, 16)
            own(pool.memset(ident[:], 0.0))
            own(pool.affine_select(out=ident[:], in_=ident[:], compare_op=ALU.not_equal, fill=1.0, base=0,
                                   pattern=[[-1, P]], channel_multiplier=1))
            own(pool.iota(iota[:], pattern=[[1, P]], base=0, channel_multiplier=0,
                          allow_small_or_imprecise_dtypes=True))
            own(pool.memset(B.ones_f[:], 1.0))
            m3 = B.ones_f[:].rearrange("p (c i) -> p c i", c=CPB)
            own(pool.affine_select(out=m3, in_=m3, compare_op=ALU.is_ge, fill=0.0, base=0,
                                   pattern=[[CHUNK, CPB], [1, CHUNK]], channel_multiplier=-1))
            own(pool.affine_select(out=m3, in_=m3, compare_op=ALU.is_ge, fill=0.0, base=0,
                                   pattern=[[-CHUNK, CPB], [0, CHUNK]], channel_multiplier=1))
            own(pool.tensor_copy(B.mask_att[:], B.ones_f[:]))
            own(pool.memset(B.mask_first[:], 1.0))
            own(pool.affine_select(out=B.mask_first[:], in_=B.mask_first[:], compare_op=ALU.is_equal,
                                   fill=0.0, base=0, pattern=[[1, CHUNK]], channel_multiplier=0))
            for k in range(HALF):
                own(pool.memset(B.freq[:, k:k + 1], float(np.float32(THETA) ** np.float32(-2 * k / ROPE))))
            pool.memset(B.att[:], 0.0).then_inc(consts, 1)

            pool.wait_ge(lo_ready, U_Q + AHEAD)
            with pool.Fori(0, (U_O0 - U_Q) // RING) as i:
                for c in range(RING):
                    split_lo(pool, U_Q + AHEAD + c, i)

            def weigh_onehots(l):
                def step(c, i):
                    n = 4 * GATE_TRIPS * l + c
                    pool.wait_ge(onehot1_ready, 2 * GATE_TRIPS * l + c // 2 + 1 + 2 * i)
                    if n >= 4 or type(i) is not int:
                        pool.wait_ge(gate_mm, n - 3 + 4 * i)
                    gate = gateT[:, bass.ds(4 * QT * i + QT * c, QT)]
                    pool.tensor_tensor(
                        weighted[:, c],
                        onehot1[:, c // 2, :, c % 2 * QT:(c % 2 + 1) * QT].rearrange("p k t -> p t k"),
                        gate.unsqueeze(2).broadcast_to([P, QT, NKEYS]), ALU.mult).then_inc(
                        weighted_pool, 1)

                pool.wait_ge(choice_read, TB * (l + 1))
                for c in range(3):
                    step(c, 0)
                with pool.Fori(1, GATE_TRIPS) as i:
                    for c in range(3):
                        step(c, i)

            for k in range(min(2 * DEPTH, stages)):
                if k % 2 == 0:
                    pool.wait_ge(unit_done, (U_O0, U_O1)[k // 2] + 1)
                    pool.dma_start(B.keys_t[:], keys[k // 2]).then_inc(keys_in, 16)
                else:
                    pool.wait_ge(unit_done, U_END[k // 2] - 8)
                for a in range(2):
                    pool.dma_start(ln_par[:, a, :], ln[k, a:a + 1, :].rearrange("a d -> (a d)")
                                   .partition_broadcast(P)).then_inc(par_in, 16)
                if k % 2 == 0 and stages > k + 1:
                    pool.wait_ge(lo_ready, U_PQ[k // 2] + AHEAD)
                    with pool.Fori(0, (NHC + EARLY) // RING) as i:
                        for c in range(RING):
                            split_lo(pool, U_PQ[k // 2] + AHEAD + c, i)
                    weigh_onehots(k // 2)
                if k == 1 and stages > 2:
                    own(pool.memset(B.bias_att[:], 0.0))
                    own(pool.affine_select(out=B.bias_att[:], in_=B.bias_att[:], compare_op=ALU.is_ge,
                                           fill=LOWEST, base=P, pattern=[[-1, 2 * P]],
                                           channel_multiplier=1))
                    pool.affine_select(out=B.bias_att[:], in_=B.bias_att[:], compare_op=ALU.is_ge,
                                       fill=LOWEST, base=-1, pattern=[[1, 2 * P]],
                                       channel_multiplier=-1).then_inc(consts, 1)

        @block.tensor
        def _(pe):
            def col_unit(c, i, bank, parts=None):
                pe.wait_ge(lo_ready, c + 1 + RING * i)
                s = c % RING
                for dc in range(DC):
                    if parts is not None and dc % 2 == 0:
                        pe.wait_ge(parts, dc // 2 + 1)
                    wh, wl = hi[:, s, dc * P:(dc + 1) * P], lo[:, s, dc * P:(dc + 1) * P]
                    o = wk[:, bank, 0:SEQ]
                    pe.matmul(o, wh, hT_hi[:, dc, :], start=(dc == 0), stop=False)
                    pe.matmul(o, wh, hT_lo[:, dc, :], start=False, stop=False)
                    last = pe.matmul(o, wl, hT_hi[:, dc, :], start=False, stop=(dc == DC - 1))
                last.then_inc(unit_done, 1)

            def residual(tb):
                t = slice(tb * P, (tb + 1) * P)
                for dc in range(DC):
                    o = acc[:, tb, dc // 2 * 2 * P:(dc // 2 + 1) * 2 * P]
                    eye = ident_pad[:, 1 - dc % 2:3 - dc % 2, :].rearrange("p a b -> p (a b)")
                    pe.matmul(o, hT_hi[:, dc, t], eye, start=(dc % 4 == 0), stop=False,
                              skip_group_check=True)
                    pe.matmul(o, hT_lo[:, dc, t], eye, start=False, stop=False, skip_group_check=True)

            def row_unit(u, k, dsts, start=True, block0=None):
                pe.wait_ge(lo_ready, u + k + 1)
                s = (u + k) % RING
                for tb in range(TB):
                    for j in range(2):
                        dc = 2 * k + j
                        wh, wl = hi[:, s, j * 512:(j + 1) * 512], lo[:, s, j * 512:(j + 1) * 512]
                        hh, hl = hT_hi[:, dc, tb * P:(tb + 1) * P], hT_lo[:, dc, tb * P:(tb + 1) * P]
                        pe.matmul(dsts[tb], hh, wh, start=(start and dc == 0), stop=False,
                                  skip_group_check=True)
                        pe.matmul(dsts[tb], hh, wl, start=False, stop=False, skip_group_check=True)
                        last = pe.matmul(dsts[tb], hl, wh, start=False, stop=(dc == DC - 1),
                                         skip_group_check=True)
                    if tb == 0 and block0 is not None:
                        last.then_inc(block0, 1)
                last.then_inc(unit_done, 1)

            def row_units(u, dsts, start=True, block0=None):
                for k in range(4):
                    row_unit(u, k, dsts, start, block0 if k == 3 else None)

            def turn(n, src, rows=None):
                for g in range(4):
                    tb, half = divmod(g, 2)
                    if half == 0 and rows is not None:
                        pe.wait_ge(row_ready, rows + tb + 1)
                    for b in range(4):
                        dc = 4 * half + b
                        last = pe.transpose(wk[:, g, b * P:(b + 1) * P], src[:, tb, dc * P:(dc + 1) * P],
                                            ident[:])
                    last.then_inc(turned, 1)
                pe.wait_ge(turn_lo, 4 * n + 4)

            def hgrn():
                for c in range(4):
                    col_unit(U_F + c, 0, c, xT_ready if c == 0 else None)
                with pe.Fori(1, 4) as i:
                    for c in range(4):
                        pe.wait_ge(proj_read, c - 3 + 4 * i)
                        col_unit(U_F + c, i, c)
                pe.wait_ge(proj_read, 2 * DC)
                for g in range(2):
                    row_units(U_I + 4 * g, [wk[:, 2 * g + tb, :] for tb in range(TB)])
                pe.wait_ge(consts, 1)
                pe.wait_ge(decays, HEADS)
                pe.wait_ge(row_read, 2)
                for g in range(4):
                    tb, half = divmod(g, 2)
                    for b in range(4):
                        last = pe.transpose(wk[:, g, b * P:(b + 1) * P],
                                            B.klT[:, 4 * half + b, tb * P:(tb + 1) * P], ident[:])
                    last.then_inc(kl_turned, 1)
                for g in range(4):
                    tb, half = divmod(g, 2)
                    for b in range(4):
                        h, t = 4 * half + b, slice(tb * P, (tb + 1) * P)
                        last = pe.matmul(acc[:, tb, h * P:(h + 1) * P], B.kT[:, h, t], B.qT[:, h, t],
                                         start=True, stop=True)
                    last.then_inc(att_raw, 1)

                def chunk_delta(c):
                    tb, r = c // CPB, slice(c % CPB * CHUNK, (c % CPB + 1) * CHUNK)
                    if c >= 2:
                        pe.wait_ge(state_ready, c - 1)
                    for h in range(HEADS):
                        f = slice(h * P, (h + 1) * P)
                        last = pe.matmul(wk[:, 2 * (c % 2) + h // 4, h % 4 * P:(h % 4 + 1) * P],
                                         B.kl_row[r, tb, f], B.v_row[r, tb, f], start=True, stop=True)
                    last.then_inc(delta, 1)

                pe.wait_ge(kl_read, 4)
                chunk_delta(0)
                chunk_delta(1)
                pe.wait_ge(att_ready, 4)
                for k in range(4):
                    row_unit(U_G, k, [acc[:, tb, 0:512] for tb in range(TB)])
                    chunk_delta(k + 2)
                chunk_delta(NCH - 2)
                pe.wait_ge(row_read, 3)
                for tb in range(TB):
                    pe.wait_ge(state_ready, min(CPB * (tb + 1), NCH) - 1)
                    for h in range(HEADS):
                        f = slice(h * P, (h + 1) * P)
                        last = pe.matmul(acc[:, tb, f], B.att[:, tb, f], B.v_row[:, tb, f], start=True,
                                         stop=False, skip_group_check=True)
                        for c in range(CPB):
                            n = CPB * tb + c
                            if n == 0:
                                continue
                            last = pe.matmul(acc[c * CHUNK:(c + 1) * CHUNK, tb, f],
                                             B.qT[:, h, n * CHUNK:(n + 1) * CHUNK], B.state[:, n, f],
                                             start=False, stop=True, skip_group_check=True)
                    last.then_inc(o_sum, 1)
                row_units(U_G + 4, [wk[:, tb, :] for tb in range(TB)])
                pe.wait_ge(o_copied, TB)
                pe.wait_ge(ident_ready, 1)
                for tb in range(TB):
                    residual(tb)
                turn(0, B.o_row, 0)
                for g in range(2):
                    row_units(U_O0 + 4 * g, [acc[:, tb, g * 512:(g + 1) * 512] for tb in range(TB)], False,
                              sum_block0 if g else None)
                turn(1, h_row, 2)

            def scores(l, c, i):
                n = NHC * l + c
                pe.wait_ge(q_ready, n + 1 + 4 * i)
                if n >= 2 or type(i) is not int:
                    pe.wait_ge(sc_copied, n - 1 + 4 * i)
                key = B.keys_t[:, bass.ds(c + 4 * i, 1), :].rearrange("p o k -> p (o k)")
                for tb in range(TB):
                    t = slice(tb * P, (tb + 1) * P)
                    last = pe.matmul(wk[:, 2 + c % 2, t], B.q_t[:, c % 2, t], key, start=True, stop=True)
                last.then_inc(sc_ready, 1)

            def choice_step(l, c, i):
                n = NHC * l + c
                if n >= 2 or type(i) is not int:
                    pe.wait_ge(q_ready, n - 1 + 4 * i)
                col_unit(U_PQ[l] + c, i, c % 2)
                if c >= 1:
                    scores(l, c - 1, i)

            def peer(l):
                for c in range(4):
                    if c == 1:
                        pe.wait_ge(keys_in, 16 * (l + 1))
                    choice_step(l, c, 0)
                with pe.Fori(1, 4) as i:
                    for c in range(4):
                        if c == 0:
                            pe.wait_ge(q_ready, NHC * l - 1 + 4 * i)
                            col_unit(U_PQ[l], i, 0)
                            scores(l, 3, i - 1)
                        else:
                            choice_step(l, c, i)
                scores(l, 3, 3)
                for tb in range(TB):
                    residual(tb)
                pe.wait_ge(q_ready, NHC * (l + 1))
                pe.wait_ge(sc_copied, NHC * (l + 1))
                for c in range(4):
                    col_unit(U_EARLY[l] + c, 0, c)
                with pe.Fori(1, EARLY // 4) as i:
                    for c in range(4):
                        pe.wait_ge(act_ready, NKEYS * l + c - 3 + 4 * i)
                        col_unit(U_EARLY[l] + c, i, c)
                pe.wait_ge(act_ready, NKEYS * l + EARLY)
                for tb in range(TB):
                    pe.wait_ge(choice_ready, TB * l + tb + 1)
                    for a, src in enumerate((B.gate[:, tb].rearrange("p h k -> p (h k)"),
                                             B.key_sel[:, tb, 0, :], B.key_sel[:, tb, 1, :])):
                        last = pe.transpose(wk[:, tb, a * P:(a + 1) * P], src, ident[:])
                    last.then_inc(choice_turned, 1)
                def gate_step(c, i):
                    n = 4 * GATE_TRIPS * l + c
                    pe.wait_ge(onehot2_ready, 2 * GATE_TRIPS * l + c // 2 + 1 + 2 * i)
                    if c < 3:
                        pe.wait_ge(weighted_pool, 3 * GATE_TRIPS * l + c + 1 + 3 * i)
                    else:
                        pe.wait_ge(weighted_act, GATE_TRIPS * l + 1 + i)
                    if n >= 4 or type(i) is not int:
                        pe.wait_ge(gate_read, n - 3 + 4 * i)
                        pe.wait_ge(early_weighed, 2 * GATE_TRIPS * l + c // 2 - 1 + 2 * i)
                    for b in range(QT):
                        last = pe.matmul(wk[:, c, b * P:(b + 1) * P], onehot2[:, c // 2, c % 2 * QT + b, :],
                                         weighted[:, c, b, :], start=True, stop=True)
                    last.then_inc(gate_mm, 1)

                pe.wait_ge(choice_read, TB * (l + 1))
                for c in range(4):
                    gate_step(c, 0)
                with pe.Fori(1, GATE_TRIPS) as i:
                    for c in range(4):
                        gate_step(c, i)

                def down(c, i, n, slot, final=False):
                    pe.wait_ge(lo_ready, c + 1 + RING * i)
                    pe.wait_ge(w_ready, NKEYS * l + n + 1)
                    s = c % RING
                    for tb in range(TB):
                        wh, wl = w_hi[:, slot, tb * P:(tb + 1) * P], w_lo[:, slot, tb * P:(tb + 1) * P]
                        for half in range(2):
                            f = slice(half * 512, (half + 1) * 512)
                            pe.matmul(acc[:, tb, f], wh, hi[:, s, f], start=False, stop=False,
                                      skip_group_check=True)
                            pe.matmul(acc[:, tb, f], wh, lo[:, s, f], start=False, stop=False,
                                      skip_group_check=True)
                            last = pe.matmul(acc[:, tb, f], wl, hi[:, s, f], start=False, stop=final,
                                             skip_group_check=True)
                        if tb == 0 and final:
                            last.then_inc(sum_block0, 1)
                    last.then_inc(unit_done, 1)

                with pe.Fori(0, EARLY // 4) as i:
                    for c in range(4):
                        down(U_DOWN[l] + c, i, c + 4 * i, c % 2)
                u = U_REST[l]
                pe.wait_ge(gate_read, 4 * GATE_TRIPS * (l + 1))
                pe.wait_ge(early_weighed, 2 * GATE_TRIPS * (l + 1))
                col_unit(u, 0, EARLY % 4)
                col_unit(u + 1, 0, (EARLY + 1) % 4)
                down(u + 2, 0, EARLY, 0)
                with pe.Fori(0, TRIPS) as i:
                    for b in range(TILES_LOOP):
                        n = EARLY + 1 + b
                        c = u + 3 + 2 * b
                        pe.wait_ge(act_ready, NKEYS * l + n - 2 + 4 * i)
                        col_unit(c, 2 * i, (n + 1) % 4)
                        down(c + 1, 2 * i, n + 4 * i, n % 2)
                c = U_END[l] - 5
                for n in (NKEYS - 3, NKEYS - 2):
                    pe.wait_ge(act_ready, NKEYS * l + n - 2)
                    col_unit(c, 0, (n + 1) % 4)
                    down(c + 1, 0, n, n % 2)
                    c += 2
                down(c, 0, NKEYS - 1, (NKEYS - 1) % 2, True)

            def attention():
                row_units(U_KV, [wk[:, tb, :] for tb in range(TB)])
                row_units(U_WQ, [acc[:, 0, tb * 512:(tb + 1) * 512] for tb in range(TB)])

                def turn_group(g, blocks):
                    bank = (g + 2) % 4
                    for b in range(4):
                        last = pe.transpose(wk[:, bank, b * P:(b + 1) * P], blocks[b], ident[:])
                    last.then_inc(a_turned, 1)

                pe.wait_ge(roped, 1)
                for tb in range(TB):
                    turn_group(tb, [B.k2_row[:, tb, b].rearrange("p r d -> p (r d)") for b in range(KVH)])
                row_units(U_WQ + 4, [acc[:, 1, tb * 512:(tb + 1) * 512] for tb in range(TB)])
                pe.wait_ge(akv_read, 1)
                for half in range(2):
                    for tb in range(TB):
                        g = TB * (1 + half) + tb
                        pe.wait_ge(roped, g)
                        if g >= 4:
                            pe.wait_ge(a_turn_read, g - 3)
                        turn_group(g, [B.q_row[:, tb, (4 * half + b) * P:(4 * half + b + 1) * P]
                                       for b in range(4)])

                def logit_step(n):
                    tb, kv = divmod(n, KVH)
                    if n == 0:
                        pe.wait_ge(a_turn_read, 4)
                        pe.wait_ge(aq_read, 2)
                    if n == 2:
                        pe.wait_ge(a_turn_read, 6)
                    if n >= 2:
                        pe.wait_ge(shifted, n - 1)
                    for j in range(GRP):
                        h = GRP * kv + head_at(j)
                        r = slice(h % 2 * HD, (h % 2 + 1) * HD)
                        lhs = B.aqT[r, h // 2, tb * P:(tb + 1) * P]
                        keys = slice(0, 2 * P) if tb else slice(0, P)
                        o = acc[:, n % 2, j * 256 + (0 if tb else P):(j + 1) * 256]
                        last = pe.matmul(o, lhs, B.k2T[r, kv, keys], start=True, stop=True)
                    last.then_inc(logits, 1)

                def value_step(n):
                    tb, kv = divmod(n, KVH)
                    pe.wait_ge(probs, n + 1)
                    parts = (0, 1) if tb else (1,)
                    if n >= 1:
                        pe.wait_ge(p_read, n)
                    for j in range(GRP):
                        for part in parts:
                            o = wk[:, j // 2, (j % 2 * 2 + part) * P:(j % 2 * 2 + part + 1) * P]
                            last = pe.transpose(o, B.prob[:, n % 2, j, part * P:(part + 1) * P], ident[:])
                    last.then_inc(p_turned, 1)

                def out_step(n):
                    tb, kv = divmod(n, KVH)
                    parts = (0, 1) if tb else (1,)
                    pe.wait_ge(p_read, n + 1)
                    if n >= 2:
                        pe.wait_ge(a_norm, n - 1)
                    for j in range(GRP):
                        g = head_at(j)
                        for part in parts:
                            last = pe.matmul(wk[:, 2 + n % 2, g * HD:(g + 1) * HD],
                                             B.probT[:, n % 2, j, part, :],
                                             B.kv_row[:, tb - 1 + part, 1, kv * HD:(kv + 1) * HD],
                                             start=(part == parts[0]), stop=(part == 1))
                    last.then_inc(a_out, 1)

                for n in range(TB * KVH + 2):
                    if n >= 2:
                        value_step(n - 2)
                    if n < TB * KVH:
                        logit_step(n)
                    if n >= TB * KVH:
                        pe.wait_ge(shifted, n - 1)
                        residual(n - TB * KVH)
                    if n >= 2:
                        out_step(n - 2)
                pe.wait_ge(a_norm, TB * KVH)
                turn(3, B.ao_row)
                for g in range(2):
                    row_units(U_O1 + 4 * g, [acc[:, tb, g * 512:(g + 1) * 512] for tb in range(TB)], False,
                              sum_block0 if g else None)
                turn(4, h_row, 6)

            hgrn()
            if stages > 1:
                peer(0)
            if stages > 2:
                turn(2, h_row, 4)
                attention()
            if stages > 3:
                peer(1)

        @block.scalar
        def _(act):
            own = Chain(act, act_own)

            def turn_step(n):
                for g in range(4):
                    tb, half = divmod(g, 2)
                    act.wait_ge(turned, 4 * n + g + 1)
                    act.activation(hT_hi[:, 4 * half:4 * half + 4, tb * P:(tb + 1) * P],
                                   wk[:, g, :].rearrange("p (b t) -> p b t", b=4),
                                   ACT.Copy).then_inc(turn_hi, 1)

            def norm_step(k):
                act.wait_ge(var_ready, k + 1)
                act.activation(rstd[:], rinv[:], ACT.Sqrt).then_inc(rstd_ready, 1)

            def hgrn():
                xt_raw = B.o_row[:].rearrange("p a b -> p (a b)").rearrange("p (c t) -> p c t", c=DC)
                split_hi(act, 0)
                for k in range(4):
                    act.wait_ge(xT_in[k], 16)
                    act.activation(hT_hi[:, 2 * k:2 * k + 2, :], xt_raw[:, 2 * k:2 * k + 2, :],
                                   ACT.Copy).then_inc(xT_hi_ready, 1)
                split_hi(act, 1)
                for c in range(DC):
                    split_hi(act, U_F + c + AHEAD)
                    act.wait_ge(unit_done, U_F + c + 1)
                    act.activation(B.fT[:, c, :], wk[:, c % 4, 0:SEQ], ACT.Sigmoid).then_inc(proj_read, 1)
                act.wait_ge(lb_shift, 1)
                act.activation(B.lb_t[:], B.lb_t[:], ACT.Exp).then_inc(lb_exp, 1)
                with act.Fori(0, 2) as i:
                    for c in range(4):
                        split_hi(act, U_Q + c + AHEAD, i)
                        act.wait_ge(unit_done, U_Q + c + 1 + RING * i)
                        act.activation(B.qT[:, bass.ds(4 * i + c, 1), :].rearrange("p o t -> p (o t)"),
                                       wk[:, c, 0:SEQ], ACT.Silu).then_inc(proj_read, 1)
                for g in range(2):
                    for k in range(4):
                        split_hi(act, U_I + 4 * g + k + AHEAD)
                    act.wait_ge(unit_done, U_I + 4 * g + 4)
                    act.activation(B.v_row[:, :, g * 512:(g + 1) * 512], wk[:, 2 * g:2 * g + 2, :],
                                   ACT.Copy).then_inc(row_read, 1)
                for g in range(4):
                    tb, half = divmod(g, 2)
                    act.wait_ge(kl_turned, g + 1)
                    act.activation(B.kl_row[:, tb, half * 512:(half + 1) * 512], wk[:, g, :],
                                   ACT.Copy).then_inc(kl_read, 1)
                for k in range(4):
                    split_hi(act, U_G + k + AHEAD)
                act.wait_ge(consts, 1)
                for a, scale in enumerate((0.0, 1.0, 0.0)):
                    last = act.activation(ident_pad[:, a, :], ident[:], ACT.Copy, scale=scale)
                last.then_inc(ident_ready, 1)
                act.wait_ge(angles, 1)
                act.activation(sin_t[:], B.red[:], ACT.Sin).then_inc(tables, 1)
                act.wait_ge(angles, 2)
                act.activation(cos_t[:], B.ang[:], ACT.Sin).then_inc(tables, 1)
                act.wait_ge(unit_done, U_G + 4)
                act.activation(B.g_row[:, :, 0:512], acc[:, :, 0:512], ACT.Silu).then_inc(row_read, 1)
                for k in range(2):
                    split_hi(act, U_G + 4 + k + AHEAD)
                for tb in range(TB):
                    act.wait_ge(o_sum, tb + 1)
                    act.activation(B.o_row[:, tb, :], acc[:, tb, :], ACT.Copy).then_inc(o_copied, 1)
                for k in range(2, 4):
                    split_hi(act, U_G + 4 + k + AHEAD)
                for tb in range(TB):
                    act.wait_ge(o_sq, tb + 1)
                    act.activation(B.ssq[:, tb, :], B.ssq[:, tb, :], ACT.Sqrt).then_inc(o_rms, 1)
                act.wait_ge(unit_done, U_G + 8)
                act.activation(B.g_row[:, :, 512:1024], wk[:, 0:2, :], ACT.Silu).then_inc(row_read, 1)
                turn_step(0)
                for u in range(U_O0, U_O0 + DC):
                    split_hi(act, u + AHEAD)
                norm_step(0)
                turn_step(1)

            def peer(l):
                def q_step(c, i):
                    n = NHC * l + c
                    act.wait_ge(unit_done, U_PQ[l] + c + 1 + RING * i)
                    if n >= 2 or type(i) is not int:
                        act.wait_ge(sc_ready, n - 1 + 4 * i)
                    act.activation(B.q_t[:, c % 2, :], wk[:, c % 2, 0:SEQ], ACT.Copy).then_inc(
                        q_ready, 1)

                def s_step(c, i):
                    n = NHC * l + c
                    act.wait_ge(sc_ready, n + 1 + 4 * i)
                    if n >= 2 or type(i) is not int:
                        act.wait_ge(sc_done, n - 1 + 4 * i)
                    act.activation(B.sc[:, c % 2].rearrange("p b k -> p (b k)"),
                                   wk[:, 2 + c % 2, 0:SEQ], ACT.Copy).then_inc(sc_copied, 1)

                for c in range(4):
                    split_hi(act, U_PQ[l] + c + AHEAD)
                    q_step(c, 0)
                    if c:
                        s_step(c - 1, 0)
                with act.Fori(1, 4) as i:
                    for c in range(4):
                        split_hi(act, U_PQ[l] + c + AHEAD, i)
                        if c == 0:
                            act.wait_ge(unit_done, U_PQ[l] + 1 + RING * i)
                            act.wait_ge(sc_ready, NHC * l - 1 + 4 * i)
                            act.activation(B.q_t[:, 0, :], wk[:, 0, 0:SEQ], ACT.Copy).then_inc(
                                q_ready, 1)
                            s_step(3, i - 1)
                        else:
                            q_step(c, i)
                            s_step(c - 1, i)
                s_step(3, 3)
                for tb, (first, last) in enumerate(((0, EARLY_EXP), (EARLY_EXP, EARLY // 4))):
                    with act.Fori(first, last) as i:
                        for c in range(4):
                            split_hi(act, U_EARLY[l] + c + AHEAD, i)
                            act.wait_ge(unit_done, U_EARLY[l] + c + 1 + RING * i)
                            act.activation(B.gates[:, bass.ds(4 * i + c, 1), :].rearrange(
                                "p o t -> p (o t)"), wk[:, c, 0:SEQ], ACT.Gelu).then_inc(act_ready, 1)
                    act.wait_ge(gate_in, TB * l + tb + 1)
                    act.activation(B.gate[:, tb], B.gate[:, tb], ACT.Exp).then_inc(gate_exp, 1)
                for tb in range(TB):
                    act.wait_ge(choice_turned, TB * l + tb + 1)
                    t = slice(tb * P, (tb + 1) * P)
                    act.activation(gateT[:, t], wk[:, tb, 0:P], ACT.Copy)
                    act.activation(key1T[:, t], wk[:, tb, P:2 * P], ACT.Copy)
                    act.activation(key2T[:, t], wk[:, tb, 2 * P:3 * P], ACT.Copy).then_inc(choice_read, 1)

                def gate_trip(i):
                    n = 4 * GATE_TRIPS * l
                    act.wait_ge(onehot1_ready, 2 * GATE_TRIPS * l + 2 + 2 * i)
                    if l > 0 or type(i) is not int:
                        act.wait_ge(gate_mm, n + 4 * i)
                    for b in range(QT):
                        last = act.activation(weighted[:, 3, b, :], onehot1[:, 1, :, QT + b], ACT.Copy,
                                              scale=gateT[:, bass.ds(4 * QT * i + 3 * QT + b, 1)])
                    last.then_inc(weighted_act, 1)
                    for c in range(4):
                        act.wait_ge(gate_mm, n + c + 1 + 4 * i)
                        act.activation(
                            B.gates[:, EARLY:, bass.ds(4 * QT * i + QT * c, QT)],
                            wk[:, c, :].rearrange("p (t k) -> p k t", t=QT)[:, EARLY:, :],
                            ACT.Copy).then_inc(gate_read, 1)

                gate_trip(0)
                with act.Fori(1, GATE_TRIPS) as i:
                    gate_trip(i)

                def gelu(n, i, c, ci):
                    act.wait_ge(unit_done, c + 1 + RING * ci)
                    act.wait_ge(w_ready, NKEYS * l + n - 1 + 4 * i)
                    act.activation(gelu_a[:, n % 2, :], wk[:, n % 4, 0:SEQ], ACT.Gelu).then_inc(
                        act_ready, 1)

                act.wait_ge(early_weighed, 2 * GATE_TRIPS * (l + 1))
                with act.Fori(0, EARLY // 4) as i:
                    for c in range(4):
                        act.wait_ge(unit_done, U_DOWN[l] + c - 1 + RING * i)
                        act.activation(w_hi[:, c % 2, :], B.gates[:, bass.ds(4 * i + c, 1), :].rearrange(
                            "p o t -> p (o t)"), ACT.Copy).then_inc(w_hi_ready, 1)
                        split_hi(act, U_DOWN[l] + c + AHEAD, i)
                u = U_REST[l]
                split_hi(act, u + 2)
                gelu(EARLY, 0, u, 0)
                split_hi(act, u + 3)
                split_hi(act, u + 4)
                with act.Fori(0, TRIPS) as i:
                    for b in range(TILES_LOOP):
                        n, c = EARLY + 1 + b, u + 3 + 2 * b
                        gelu(n, i, c - 2, 2 * i)
                        split_hi(act, c + 2, 2 * i)
                        split_hi(act, c + 3, 2 * i)
                c = U_END[l] - 5
                for n in range(NKEYS - 3, NKEYS):
                    gelu(n, 0, c - 2, 0)
                    split_hi(act, c + 2)
                    if n < NKEYS - 1:
                        split_hi(act, c + 3)
                    c += 2
                norm_step(2 * l + 1)

            def attention():
                for u in range(U_KV, U_KV + 4):
                    split_hi(act, u + AHEAD)
                act.wait_ge(unit_done, U_KV + 4)
                act.activation(B.kv_row[:, :, 0, :], wk[:, 0:2, 0:KVH * HD], ACT.Copy)
                act.activation(B.kv_row[:, :, 1, :], wk[:, 0:2, KVH * HD:], ACT.Copy,
                               scale=1.0 / ALPHA).then_inc(akv_read, 1)
                for half in range(2):
                    for k in range(4):
                        split_hi(act, U_WQ + 4 * half + k + AHEAD)
                    act.wait_ge(unit_done, U_WQ + 4 * half + 4)
                    act.activation(B.q_row[:, :, half * 512:(half + 1) * 512],
                                   acc[:, half, :].rearrange("p (b f) -> p b f", b=TB),
                                   ACT.Copy).then_inc(aq_read, 1)
                    if half == 0:
                        for tb in range(TB):
                            act.wait_ge(a_turned, tb + 1)
                            act.activation(B.k2T[:, :, tb * P:(tb + 1) * P],
                                           wk[:, 2 + tb, :].rearrange("p (b t) -> p b t", b=4),
                                           ACT.Copy).then_inc(a_turn_read, 1)
                for half in range(2):
                    for tb in range(TB):
                        g = TB * (1 + half) + tb
                        act.wait_ge(a_turned, g + 1)
                        act.activation(B.aqT[:, 4 * half:4 * half + 4, tb * P:(tb + 1) * P],
                                       wk[:, (g + 2) % 4, :].rearrange("p (b t) -> p b t", b=4),
                                       ACT.Copy).then_inc(a_turn_read, 1)
                for n in range(TB * KVH + 2):
                    if n >= 2:
                        m = n - 2
                        act.wait_ge(p_turned, m + 1)
                        if m >= 2:
                            act.wait_ge(a_out, m - 1)
                        w = wk[:, 0:2, :].rearrange("p a (g r t) -> p (a g) r t", g=2, r=2)
                        if m >= KVH:
                            act.activation(B.probT[:, m % 2], w, ACT.Copy).then_inc(p_read, 1)
                        else:
                            act.activation(B.probT[:, m % 2, :, 1, :], w[:, :, 1, :],
                                           ACT.Copy).then_inc(p_read, 1)
                    if n < TB * KVH:
                        first = 0 if n >= KVH else P
                        act.wait_ge(shifted, n + 1)
                        for j in range(GRP):
                            act.activation(B.prob[:, n % 2, j, first:], B.logit[:, n % 2, j, first:],
                                           ACT.Exp, bias=B.nmax[:, n % 2, j:j + 1],
                                           accum_out=B.rsum[:, n % 3, j:j + 1])
                        act.activation(B.sexp[:, n % 3, :], B.sexp[:, n % 3, :], ACT.Exp).then_inc(probs, 1)
                turn_step(3)
                for u in range(U_O1, U_O1 + DC):
                    split_hi(act, u + AHEAD)
                norm_step(2)
                turn_step(4)

            hgrn()
            if stages > 1:
                peer(0)
            if stages > 2:
                turn_step(2)
                attention()
            if stages > 3:
                peer(1)

        @block.vector
        def _(dve):
            own = Chain(dve, dve_own)

            def turn_step(n):
                for g in range(4):
                    tb, half = divmod(g, 2)
                    t = slice(tb * P, (tb + 1) * P)
                    dve.wait_ge(turn_hi, 4 * n + g + 1)
                    dve.tensor_tensor(hT_lo[:, 4 * half:4 * half + 4, t],
                                      wk[:, g, :].rearrange("p (b t) -> p b t", b=4),
                                      hT_hi[:, 4 * half:4 * half + 4, t].bitcast(F32),
                                      ALU.subtract).then_inc(turn_lo, 1)

            def layer_norm(k, u_last, u_half=None):
                def half_stats(tb, half):
                    return dve.bn_stats(stats[:, tb, half, :], acc[:, tb, half * 512:(half + 1) * 512])

                if u_half is not None:
                    dve.wait_ge(unit_done, u_half + 1)
                    for tb in range(TB):
                        half_stats(tb, 0)
                for tb in range(TB):
                    if tb == 0:
                        dve.wait_ge(sum_block0, k + 1)
                    else:
                        dve.wait_ge(unit_done, u_last + 1)
                    if u_half is None:
                        half_stats(tb, 0)
                    last = half_stats(tb, 1)
                own(last)
                for tb in range(TB):
                    last = dve.bn_aggr(mean_var[:, tb, :], stats[:, tb].rearrange("p a b -> p (a b)"))
                own(last)
                own(dve.tensor_scalar(var_eps[:], mean_var[:, :, 1], LN_EPS / ALPHA ** 2, None, ALU.add))
                dve.reciprocal(rinv[:], var_eps[:]).then_inc(var_ready, 1)
                dve.wait_ge(par_in, 32 * (k + 1))
                for tb in range(TB):
                    dve.scalar_tensor_tensor(h_row[:, tb, :], acc[:, tb, :], mean_var[:, tb, 0:1],
                                             ln_par[:, 0, :], ALU.subtract, ALU.mult)
                dve.wait_ge(rstd_ready, k + 1)
                own(dve.scalar_tensor_tensor(rinv[:], rstd[:], -0.5, rstd[:], ALU.mult, ALU.mult))
                own(dve.tensor_tensor(rinv[:], rinv[:], var_eps[:], ALU.mult))
                own(dve.scalar_tensor_tensor(rstd[:], rinv[:], 1.5, rstd[:], ALU.add, ALU.mult))
                for tb in range(TB):
                    dve.scalar_tensor_tensor(h_row[:, tb, :], h_row[:, tb, :], rstd[:, tb:tb + 1],
                                             ln_par[:, 1, :], ALU.mult, ALU.add).then_inc(row_ready, 1)

            def hgrn():
                split_lo(dve, 0)
                xt_raw = B.o_row[:].rearrange("p a b -> p (a b)").rearrange("p (c t) -> p c t", c=DC)
                for k in range(4):
                    dve.wait_ge(xT_hi_ready, k + 1)
                    part = slice(2 * k, 2 * k + 2)
                    dve.tensor_tensor(hT_lo[:, part, :], xt_raw[:, part, :],
                                      hT_hi[:, part, :].bitcast(F32), ALU.subtract).then_inc(xT_ready, 1)
                split_lo(dve, 1)
                with dve.Fori(0, 2) as i:
                    for c in range(4):
                        split_lo(dve, U_F + c + AHEAD, i)
                dve.wait_ge(small_in, 48)
                own(dve.tensor_tensor(B.lb_m[:], B.lb_t[:, 0, :], B.lb_t[:, 1, :], ALU.max))
                dve.tensor_tensor(B.lb_t[:], B.lb_t[:], B.lb_m[:].unsqueeze(1).broadcast_to([P, 2, HEADS]),
                                  ALU.subtract).then_inc(lb_shift, 1)
                dve.wait_ge(consts, 1)
                dve.tensor_copy(iota_b[:], iota[:].unsqueeze(2).broadcast_to([P, NKEYS, OH]))
                own(dve.tensor_copy(B.pos_f[:], B.pos_i[:]))
                for tb in range(TB):
                    last = dve.tensor_scalar(B.ang[:, tb, :], B.freq[:], B.pos_f[:, tb:tb + 1], None,
                                             ALU.mult)
                own(last)
                for n, (quarter, dst) in enumerate(((0.0, B.red), (0.25, B.ang))):
                    own(dve.tensor_scalar(B.rnd[:], B.ang[:], 1.0 / TWO_PI, quarter, ALU.mult, ALU.add))
                    own(dve.tensor_scalar(B.rnd[:], B.rnd[:], ROUND, None, ALU.add))
                    own(dve.tensor_scalar(B.rnd[:], B.rnd[:], ROUND, None, ALU.subtract))
                    own(dve.scalar_tensor_tensor(dst[:], B.rnd[:], -C1, B.ang[:], ALU.mult, ALU.add))
                    own(dve.scalar_tensor_tensor(dst[:], B.rnd[:], -C2, dst[:], ALU.mult, ALU.add))
                    own(dve.scalar_tensor_tensor(dst[:], B.rnd[:], -C3, dst[:], ALU.mult, ALU.add))
                    own(dve.tensor_scalar(dst[:], dst[:], quarter * TWO_PI, PI_IN, ALU.add, ALU.min))
                    dve.tensor_scalar(dst[:], dst[:], -PI_IN, None, ALU.max).then_inc(angles, 1)
                dve.wait_ge(lb_exp, 1)
                own(dve.tensor_tensor(B.lb_m[:], B.lb_t[:, 0, :], B.lb_t[:, 1, :], ALU.add))
                own(dve.reciprocal(B.lb_m[:], B.lb_m[:]))
                dve.tensor_tensor(B.lb_1[:], B.lb_t[:, 1, :], B.lb_m[:], ALU.mult)
                own(dve.tensor_tensor(B.lb_f[:], B.lb_t[:, 0, :], B.lb_m[:], ALU.mult))
                with dve.Fori(0, 2) as i:
                    own.enter(i, 4)
                    for c in range(4):
                        dve.wait_ge(proj_read, U_F + c + 1 + 4 * i)
                        f = B.fT[:, bass.ds(4 * i + c, 1), :].rearrange("p o t -> p (o t)")
                        k = B.kT[:, bass.ds(4 * i + c, 1), :].rearrange("p o t -> p (o t)")
                        own(dve.tensor_scalar(f, f, B.lb_1[:, bass.ds(4 * i + c, 1)],
                                              B.lb_f[:, bass.ds(4 * i + c, 1)], ALU.mult, ALU.add))
                        dve.tensor_scalar(k, f, -1.0, 1.0, ALU.mult, ALU.add)
                    own.leave(2)
                for h in range(HEADS):
                    f, k, dec, q, kl = (t[:, h, :] for t in (B.fT, B.kT, B.decT, B.qT, B.klT))

                    def chunks(ap):
                        return ap.rearrange("p (n s) -> p n s", s=CHUNK)

                    own(dve.tensor_tensor(chunks(B.first[:]), chunks(f),
                                          B.mask_first[:].unsqueeze(1).broadcast_to([P, NCH, CHUNK]),
                                          ALU.mult))
                    own(dve.tensor_tensor_scan(dec, f, B.first[:], 0.0, ALU.mult, ALU.max))
                    own(dve.reciprocal(B.tmp[:], dec))
                    own(dve.tensor_tensor(k, k, B.tmp[:], ALU.mult))
                    dve.wait_ge(proj_read, DC + h + 1)
                    end = chunks(dec)[:, :, CHUNK - 1:CHUNK].broadcast_to([P, NCH, CHUNK])
                    dve.tensor_tensor(chunks(kl), chunks(k), end, ALU.mult)
                    dve.tensor_tensor(q, q, dec, ALU.mult).then_inc(decays, 1)
                for g in range(4):
                    tb, half = divmod(g, 2)
                    dve.wait_ge(att_raw, g + 1)
                    part = slice(half * 512, (half + 1) * 512)
                    dve.copy_predicated(
                        B.att[:, tb, part].rearrange("p (h t) -> p h t", h=4),
                        B.mask_att[:].unsqueeze(1).broadcast_to([P, 4, P]),
                        acc[:, tb, part].rearrange("p (h t) -> p h t", h=4)).then_inc(att_ready, 1)
                for c in range(NCH - 1):
                    dve.wait_ge(delta, c + 1)
                    new = wk[:, 2 * (c % 2):2 * (c % 2) + 2, :].rearrange("p a b -> p (a b)")
                    if c == 0:
                        dve.tensor_copy(B.state[:, 1, :], new).then_inc(state_ready, 1)
                        continue
                    dve.wait_ge(state_ready, c)
                    for h in range(HEADS):
                        f = slice(h * P, (h + 1) * P)
                        last = dve.scalar_tensor_tensor(
                            B.state[:, c + 1, f], B.state[:, c, f],
                            B.decT[:, h, (c + 1) * CHUNK - 1:(c + 1) * CHUNK], new[:, f], ALU.mult, ALU.add)
                    last.then_inc(state_ready, 1)
                sq = B.klT[:].rearrange("p h t -> p (h t)")[:, 0:D]
                def weigh_gate(half):
                    f = slice(half * 512, (half + 1) * 512)
                    dve.wait_ge(row_read, 3 + half)
                    return dve.scalar_tensor_tensor(
                        B.g_row[:, :, f], B.g_row[:, :, f], 1.0 / ALPHA,
                        B.norm_t[:, f].unsqueeze(1).broadcast_to([P, TB, 512]), ALU.mult, ALU.mult)

                dve.wait_ge(norm_in, 16)
                weigh_gate(0)
                for tb in range(TB):
                    dve.wait_ge(o_copied, tb + 1)
                    own(dve.tensor_tensor(sq, B.o_row[:, tb, :], B.o_row[:, tb, :], ALU.mult))
                    own(dve.tensor_reduce(B.ssq[:, tb, :], sq.rearrange("p (h e) -> p h e", h=HEADS), AX,
                                          ALU.add))
                    own(dve.tensor_scalar(B.ssq[:, tb, :], B.ssq[:, tb, :], 1.0 / P, RMS_EPS, ALU.mult,
                                          ALU.add))
                    dve.reciprocal(B.ssq[:, tb, :], B.ssq[:, tb, :]).then_inc(o_sq, 1)
                own(weigh_gate(1))
                for tb in range(TB):
                    dve.wait_ge(o_rms, tb + 1)
                    for h in range(HEADS):
                        f = slice(h * P, (h + 1) * P)
                        last = dve.scalar_tensor_tensor(B.o_row[:, tb, f], B.o_row[:, tb, f],
                                                        B.ssq[:, tb, h:h + 1], B.g_row[:, tb, f],
                                                        ALU.mult, ALU.mult)
                    last.then_inc(row_ready, 1)
                turn_step(0)
                dve.wait_ge(lo_ready, U_O0 + AHEAD)
                for u in range(U_O0, U_O0 + DC):
                    split_lo(dve, u + AHEAD)
                layer_norm(0, U_O0 + 7, U_O0 + 3)
                turn_step(1)

            def peer(l):
                def top_step(c):
                    dve.wait_ge(sc_copied, NHC * l + c + 1)
                    s = B.sc[:, c % 2]
                    v, ix = B.val[:, :, c, :], B.idx_u[:, :, c, :]
                    for tb in range(TB):
                        last = dve.max(v[:, tb, 0:8], s[:, tb, :])
                    own(last)
                    for tb in range(TB):
                        dve.max_index(ix[:, tb, 0:8], v[:, tb, 0:8], s[:, tb, :])
                        last = dve.match_replace(B.sc_cut[:, tb, :], v[:, tb, 0:8], s[:, tb, :], LOWEST)
                    last.then_inc(sc_done, 1)
                    dve.wait_ge(sc_done, NHC * l + c + 1)
                    for tb in range(TB):
                        last = dve.max(v[:, tb, 8:16], B.sc_cut[:, tb, :])
                    own(last)
                    for tb in range(TB):
                        last = dve.max_index(ix[:, tb, 8:16], v[:, tb, 8:16], B.sc_cut[:, tb, :])
                    own(last)

                for c in range(NHC):
                    top_step(c)
                own(dve.tensor_copy(B.idx[:], B.idx_u[:]))

                for tb in range(TB):
                    v4 = B.val[:, tb].rearrange("p (h c) k -> p h c k", c=2)
                    for h in range(HEADS):
                        last = dve.tensor_tensor(
                            B.cand[:, h, :].rearrange("p (a b) -> p a b", a=TOPK),
                            v4[:, h, 0, :].unsqueeze(2).broadcast_to([P, TOPK, TOPK]),
                            v4[:, h, 1, :].unsqueeze(1).broadcast_to([P, TOPK, TOPK]), ALU.add)
                    own(last)
                    for h in range(HEADS):
                        last = dve.max(B.top_s[:, tb, h, 0:8], B.cand[:, h, :])
                    own(last)
                    for h in range(HEADS):
                        dve.max_index(B.top_j[:, tb, h, 0:8], B.top_s[:, tb, h, 0:8], B.cand[:, h, :])
                        last = dve.match_replace(B.cand_cut[:, h, :], B.top_s[:, tb, h, 0:8],
                                                 B.cand[:, h, :], LOWEST)
                    own(last)
                    for h in range(HEADS):
                        last = dve.max(B.top_s[:, tb, h, 8:16], B.cand_cut[:, h, :])
                    own(last)
                    for h in range(HEADS):
                        last = dve.max_index(B.top_j[:, tb, h, 8:16], B.top_s[:, tb, h, 8:16],
                                             B.cand_cut[:, h, :])
                    own(last)
                    dve.tensor_tensor(B.gate[:, tb], B.top_s[:, tb],
                                      B.top_s[:, tb, :, 0:1].broadcast_to([P, HEADS, TOPK]),
                                      ALU.subtract).then_inc(gate_in, 1)
                    j = B.top_j[:, tb].rearrange("p h k -> p (h k)")
                    dve.tensor_scalar(B.j_int[:, 0, :], j, 4, None, ALU.logical_shift_right)
                    own(dve.tensor_scalar(B.j_int[:, 1, :], j, 15, None, ALU.bitwise_and))
                    own(dve.tensor_copy(B.j_f[:], B.j_int[:]))
                    i4 = B.idx[:, tb].rearrange("p (h c) k -> p h c k", c=2)
                    for c in range(2):
                        own(dve.tensor_tensor(
                            B.pick[:], iota[:, 0:TOPK].unsqueeze(1).broadcast_to([P, HEADS * TOPK, TOPK]),
                            B.j_f[:, c, :].unsqueeze(2).broadcast_to([P, HEADS * TOPK, TOPK]),
                            ALU.is_equal))
                        own(dve.tensor_tensor(
                            B.picked[:].rearrange("p (h k) a -> p h k a", h=HEADS),
                            B.pick[:].rearrange("p (h k) a -> p h k a", h=HEADS),
                            i4[:, :, c, :].unsqueeze(2).broadcast_to([P, HEADS, TOPK, TOPK]), ALU.mult))
                        own(dve.tensor_reduce(B.key_sel[:, tb, c, :], B.picked[:], AX, ALU.add))
                for tb in range(TB):
                    dve.wait_ge(gate_exp, TB * l + tb + 1)
                    own(dve.tensor_reduce(B.gsum[:, tb, :], B.gate[:, tb], AX, ALU.add))
                    own(dve.reciprocal(B.gsum[:, tb, :], B.gsum[:, tb, :]))
                    dve.scalar_tensor_tensor(B.gate[:, tb], B.gate[:, tb], 1.0 / ALPHA,
                                             B.gsum[:, tb, :].unsqueeze(2).broadcast_to([P, HEADS, TOPK]),
                                             ALU.mult, ALU.mult).then_inc(choice_ready, 1)

                dve.wait_ge(choice_read, TB * (l + 1))

                def weigh_early(c, i):
                    dve.wait_ge(gate_read, 4 * GATE_TRIPS * l + 2 * c + 2 + 4 * i)
                    t = bass.ds(4 * QT * i + 2 * QT * c, 2 * QT)
                    acts = B.gates[:, 0:EARLY, t]
                    dve.tensor_tensor(
                        acts, acts, wk[:, 2 * c:2 * c + 2, :].rearrange("p b (t k) -> p k (b t)", t=QT)[
                            :, 0:EARLY, :], ALU.mult).then_inc(early_weighed, 1)

                def onehot_step(c, i):
                    n = 4 * GATE_TRIPS * l + 2 * c
                    later = l > 0 or type(i) is not int
                    if later:
                        dve.wait_ge(weighted_pool, 3 * GATE_TRIPS * l - 1 + c + 3 * i)
                        if c == 1:
                            dve.wait_ge(weighted_act, GATE_TRIPS * l + i)
                    t = bass.ds(4 * QT * i + OH * c, OH)
                    dve.tensor_tensor(onehot1[:, c], iota_b[:],
                                      key1T[:, t].unsqueeze(1).broadcast_to([P, NKEYS, OH]),
                                      ALU.is_equal).then_inc(onehot1_ready, 1)
                    if later:
                        dve.wait_ge(gate_mm, n - 2 + 4 * i)
                    dve.tensor_tensor(onehot2[:, c], iota[:].unsqueeze(1).broadcast_to([P, OH, NKEYS]),
                                      key2T[:, t].unsqueeze(2).broadcast_to([P, OH, NKEYS]),
                                      ALU.is_equal).then_inc(onehot2_ready, 1)
                    if type(i) is not int:
                        weigh_early(c, i - 1)

                for c in range(2):
                    onehot_step(c, 0)
                with dve.Fori(1, GATE_TRIPS) as i:
                    for c in range(2):
                        onehot_step(c, i)
                for c in range(2):
                    weigh_early(c, GATE_TRIPS - 1)

                def weigh(n, i):
                    dve.wait_ge(act_ready, NKEYS * l + n + 1 + 4 * i)
                    dve.wait_ge(w_ready, NKEYS * l + n + 4 * i)
                    at = bass.ds(n + 4 * i, 1)
                    g = B.gates[:, at, :].rearrange("p o t -> p (o t)")
                    dve.tensor_tensor(w_full[:], gelu_a[:, n % 2, :], g, ALU.mult)
                    own(dve.tensor_tensor(w_hi[:, n % 2, :], gelu_a[:, n % 2, :], g, ALU.mult))
                    dve.tensor_tensor(w_lo[:, n % 2, :], w_full[:], w_hi[:, n % 2, :].bitcast(F32),
                                      ALU.subtract).then_inc(w_ready, 1)

                dve.wait_ge(lo_ready, U_DOWN[l] + AHEAD)
                with dve.Fori(0, EARLY // 4) as i:
                    for c in range(4):
                        dve.wait_ge(w_hi_ready, EARLY * l + c + 1 + 4 * i)
                        dve.tensor_tensor(w_lo[:, c % 2, :], B.gates[:, bass.ds(4 * i + c, 1), :].rearrange(
                            "p o t -> p (o t)"), w_hi[:, c % 2, :].bitcast(F32), ALU.subtract).then_inc(
                            w_ready, 1)
                        split_lo(dve, U_DOWN[l] + c + AHEAD, i)
                u = U_REST[l]
                split_lo(dve, u + 2)
                dve.wait_ge(unit_done, U_DOWN[l] + EARLY - 1)
                weigh(EARLY, 0)
                split_lo(dve, u + 3)
                split_lo(dve, u + 4)
                with dve.Fori(0, TRIPS) as i:
                    own.enter(i, TILES_LOOP)
                    for b in range(TILES_LOOP):
                        n, c = EARLY + 1 + b, u + 3 + 2 * b
                        dve.wait_ge(unit_done, c - 2 + 8 * i)
                        weigh(n, i)
                        split_lo(dve, c + 2, 2 * i)
                        split_lo(dve, c + 3, 2 * i)
                    own.leave(TRIPS)
                c = U_END[l] - 5
                for n in range(NKEYS - 3, NKEYS):
                    dve.wait_ge(unit_done, c - 2)
                    weigh(n, 0)
                    split_lo(dve, c + 2)
                    if n < NKEYS - 1:
                        split_lo(dve, c + 3)
                    c += 2
                layer_norm(2 * l + 1, U_END[l] - 1)

            def attention():
                for u in range(U_KV, U_KV + 4):
                    split_lo(dve, u + AHEAD)

                def rope(v, tb):
                    n = v.shape[1]
                    c = cos_t[:, tb].unsqueeze(1).broadcast_to([P, n, HALF])
                    s = sin_t[:, tb].unsqueeze(1).broadcast_to([P, n, HALF])
                    a, b = v[:, :, 0:HALF], v[:, :, HALF:ROPE]
                    dve.tensor_tensor(B.rt[:, 0, 0:n, :], a, c, ALU.mult)
                    dve.tensor_tensor(B.rt[:, 1, 0:n, :], b, s, ALU.mult)
                    dve.tensor_tensor(B.rt[:, 2, 0:n, :], b, c, ALU.mult)
                    own(dve.tensor_tensor(B.rt[:, 3, 0:n, :], a, s, ALU.mult))
                    dve.tensor_tensor(a, B.rt[:, 0, 0:n, :], B.rt[:, 1, 0:n, :], ALU.subtract)
                    return dve.tensor_tensor(b, B.rt[:, 2, 0:n, :], B.rt[:, 3, 0:n, :], ALU.add)

                dve.wait_ge(tables, 2)
                dve.wait_ge(akv_read, 1)
                for tb in range(TB):
                    k = B.kv_row[:, tb, 0, :].rearrange("p (h d) -> p h d", h=KVH)
                    own(rope(k, tb))
                    for r in range(2):
                        last = dve.tensor_copy(B.k2_row[:, tb, :, r, :], k)
                last.then_inc(roped, 1)
                for half in range(2):
                    for k in range(4):
                        split_lo(dve, U_WQ + 4 * half + k + AHEAD)
                    dve.wait_ge(aq_read, half + 1)
                    for tb in range(TB):
                        g = TB * (1 + half) + tb
                        rope(B.q_row[:, tb, half * 512:(half + 1) * 512].rearrange(
                            "p (h d) -> p h d", h=QH // 2), tb).then_inc(roped, 1)
                        dve.wait_ge(roped, g)

                def normalize(n):
                    tb, kv = divmod(n, KVH)
                    dve.wait_ge(a_out, n + 1)
                    dve.tensor_tensor(
                        B.ao_row[:, tb, kv * GRP * HD:(kv + 1) * GRP * HD].rearrange(
                            "p (a b d) -> p a b d", a=2, b=2),
                        wk[:, 2 + n % 2, 0:GRP * HD].rearrange(
                            "p (a b d) -> p a b d", a=2, b=2),
                        B.rnorm[:, n % 2, :].rearrange("p (b a) -> p a b", b=2).unsqueeze(3).broadcast_to(
                            [P, 2, 2, HD]), ALU.mult).then_inc(a_norm, 1)

                dve.wait_ge(consts, 2)
                for n in range(TB * KVH + 2):
                    if n < TB * KVH:
                        tb, kv = divmod(n, KVH)
                        s, first = n % 2, (0 if tb else P)
                        dve.wait_ge(logits, n + 1)
                        if n >= 2:
                            dve.wait_ge(probs, n - 1)
                        lg = B.logit[:, s, :, first:]
                        own(dve.scalar_tensor_tensor(
                            lg, acc[:, s, :].rearrange("p (g k) -> p g k", g=GRP)[:, :, first:], HD ** -0.5,
                            B.bias_att[:, first:].unsqueeze(1).broadcast_to([P, GRP, 2 * P - first]),
                            ALU.mult, ALU.add))
                        own(dve.tensor_reduce(B.rmax[:, s, :], lg, AX, ALU.max))
                        sink = sink_t[:, GRP * kv:GRP * (kv + 1)].rearrange("p (a b) -> p b a", a=2)
                        m22 = B.rmax[:, s, :].rearrange("p (b a) -> p b a", b=2)
                        own(dve.tensor_tensor(m22, m22, sink, ALU.max))
                        dve.tensor_tensor(B.sexp[:, n % 3, :].rearrange("p (b a) -> p b a", b=2), sink, m22,
                                          ALU.subtract)
                        dve.tensor_scalar(B.nmax[:, s, :], B.rmax[:, s, :], -1.0, None,
                                          ALU.mult).then_inc(shifted, 1)
                    if n >= 2:
                        m = n - 2
                        dve.wait_ge(probs, m + 1)
                        own(dve.tensor_tensor(B.rnorm[:, m % 2, :], B.rsum[:, m % 3, :],
                                              B.sexp[:, m % 3, :], ALU.add))
                        own(dve.reciprocal(B.rnorm[:, m % 2, :], B.rnorm[:, m % 2, :]))
                        normalize(m)
                turn_step(3)
                for u in range(U_O1, U_O1 + DC):
                    split_lo(dve, u + AHEAD)
                layer_norm(2, U_O1 + 7, U_O1 + 3)
                turn_step(4)

            hgrn()
            if stages > 1:
                peer(0)
            if stages > 2:
                turn_step(2)
                attention()
            if stages > 3:
                peer(1)


def col_blocks(w):
    return w.reshape(DC, P, -1, P).transpose(2, 1, 0, 3).reshape(-1, P, UNIT)


def row_blocks(w):
    return w.reshape(DC // 2, 2, P, -1, 512).transpose(3, 0, 2, 1, 4).reshape(-1, P, UNIT)


def peer_units(w_q, u_tab, v_tab):
    up = u_tab.reshape(NKEYS, P, DC, P).transpose(0, 3, 2, 1).reshape(NKEYS, P, UNIT)
    down = v_tab.reshape(NKEYS, P, D)
    rest = np.empty((2 * (NKEYS - EARLY), P, UNIT), up.dtype)
    rest[0] = up[EARLY]
    rest[1:-1:2] = up[EARLY + 1:]
    rest[2::2] = down[EARLY:-1]
    rest[-1] = down[-1]
    return [col_blocks(w_q), up[:EARLY], down[:EARLY], rest]


def kernel(x, positions, hg_w_in, hg_lb, hg_norm_w, hg_w_o, sw_w_q, sw_sinks, sw_w_o, w_kv, peer_w_q,
           peer_sub_keys, peer_u, peer_v, ln_mix_g, ln_mix_b, ln_ffn_g, ln_ffn_b):
    import concourse.bacc as bacc
    from concourse.bass_utils import run_bass_kernel_spmd

    w_in = hg_w_in[0]
    stream = np.concatenate(
        [col_blocks(w_in[:, D:2 * D]), col_blocks(w_in[:, 0:D]), row_blocks(w_in[:, 2 * D:]),
         row_blocks(hg_w_o[0])]
        + peer_units(peer_w_q[0], peer_u[0], peer_v[0])
        + [row_blocks(w_kv), row_blocks(sw_w_q[0]), row_blocks(sw_w_o[0])]
        + peer_units(peer_w_q[1], peer_u[1], peer_v[1]))
    assert stream.shape == (N_UNITS, P, UNIT)
    arrays = {
        "xT": x.reshape(SEQ, DC, P).transpose(2, 1, 0),
        "positions": positions.reshape(TB, P).transpose(1, 0),
        "stream": stream,
        "keys": peer_sub_keys.reshape(DEPTH, NHC, NKEYS, P).transpose(0, 3, 1, 2),
        "lb": hg_lb.reshape(2, HEADS, P).transpose(2, 0, 1),
        "norm_w": hg_norm_w.reshape(D),
        "sinks": sw_sinks.reshape(QH),
        "ln": np.stack([np.stack([g[l], b[l]]) for l in range(DEPTH)
                        for g, b in ((ln_mix_g, ln_mix_b), (ln_ffn_g, ln_ffn_b))]),
    }
    nc = bacc.Bacc("TRN2", target_bir_lowering=False, num_devices=1)
    arrays = {f"{k}_dram": np.ascontiguousarray(a) for k, a in arrays.items()}
    args = [nc.dram_tensor(k, a.shape, mybir.dt.from_np(a.dtype), kind="ExternalInput").ap()
            for k, a in arrays.items()]
    out = nc.dram_tensor("out_dram", (P, TB, D), F32, kind="ExternalOutput").ap()
    build(nc, *args, out)
    r = run_bass_kernel_spmd(nc, [arrays], core_ids=[0])
    return np.asarray(r.results[0]["out_dram"]).transpose(1, 0, 2).reshape(1, SEQ, D)
```
